# Optimizing a Trainium2 kernel written in Bass

```python
import math
import jax, jax.numpy as jnp
from jax import lax
import numpy as np

D_MODEL = 1024
BATCH = 1
SEQ = 512
DEPTH = 2

N_BRANCH = 4
BRANCH_WIDTH = 256
NORM_EPS = 1e-6
NEG_INF = -1e30

GLA_HEADS = 4
GLA_DK = 32
GLA_DV = 64
GLA_LOWRANK = 16
GLA_TAU = 16.0
GLA_CHUNK = 64

SWA_HEADS = 4
SWA_KV_HEADS = 2
SWA_HD = 64
SWA_WINDOW = 128

MOBA_HEADS = 4
MOBA_HD = 64
MOBA_BLOCK = 256
MOBA_TOPK = 3
MOBA_QCHUNK = 64

RET_HEADS = 4
RET_DK = 32
RET_DV = 64
RET_CHUNK = 128
RET_ROPE_BASE = 10000.0

N_GROUPS = 4
EXPERTS_PER_GROUP = 8
N_EXPERTS = N_GROUPS * EXPERTS_PER_GROUP
EXPERT_TOPK = 2
EXPERT_HIDDEN = 256
MOE_BLOCK = 256

IN_LAYOUT = (
    ('gla_q', GLA_HEADS * GLA_DK), ('gla_k', GLA_HEADS * GLA_DK), ('gla_v', GLA_HEADS * GLA_DV),
    ('gla_r', GLA_HEADS * GLA_DV), ('gla_a', GLA_LOWRANK),
    ('swa_q', SWA_HEADS * SWA_HD), ('swa_k', SWA_KV_HEADS * SWA_HD), ('swa_v', SWA_KV_HEADS * SWA_HD),
    ('moba_q', MOBA_HEADS * MOBA_HD), ('moba_k', MOBA_HEADS * MOBA_HD), ('moba_v', MOBA_HEADS * MOBA_HD),
    ('ret_q', RET_HEADS * RET_DK), ('ret_k', RET_HEADS * RET_DK), ('ret_v', RET_HEADS * RET_DV),
    ('ret_g', RET_HEADS * RET_DV),
    ('gates', N_BRANCH * D_MODEL),
)
IN_WIDTH = sum(w for _, w in IN_LAYOUT)

kernel_name = 'hybrid_gla_swa_moba_retention_hmoe'

def rms_norm(x, g):
    xf = x.astype(jnp.float32)
    y = xf * lax.rsqrt(jnp.mean(xf * xf, axis=-1, keepdims=True) + NORM_EPS)
    return (y * g.astype(jnp.float32)).astype(x.dtype)

def split_columns(z):
    parts, off = {}, 0
    for name, width in IN_LAYOUT:
        parts[name] = z[..., off:off + width]
        off += width
    return parts

def gla_mixer(q, k, v, r, a_lr, w_a2, b_a, norm_g):
    B, S, _ = q.shape
    H, DK, DV, C = GLA_HEADS, GLA_DK, GLA_DV, GLA_CHUNK
    N = S // C
    f32 = jnp.float32

    def chunked(t, d):
        return t.astype(f32).reshape(B, N, C, H, d).transpose(0, 3, 1, 2, 4)

    log_a = jax.nn.log_sigmoid((a_lr @ w_a2 + b_a).astype(f32)) / GLA_TAU
    b = jnp.cumsum(chunked(log_a, DK), axis=3)
    b_last = b[:, :, :, -1:, :]
    qc = chunked(q, DK) * (DK ** -0.5)
    kc = chunked(k, DK)
    vc = chunked(v, DV)
    q_dec = qc * jnp.exp(b)
    k_dec = kc * jnp.exp(-b)
    causal = jnp.tril(jnp.ones((C, C), dtype=bool))
    att = jnp.where(causal, jnp.einsum('bhnid,bhnjd->bhnij', q_dec, k_dec), 0.0)
    o = jnp.einsum('bhnij,bhnje->bhnie', att, vc)
    kv = jnp.einsum('bhnjd,bhnje->bhnde', kc * jnp.exp(b_last - b), vc)
    decay = jnp.exp(b_last[:, :, :, 0, :])

    def step(state, inp):
        dec, kv_n = inp
        return dec[..., None] * state + kv_n, state

    _, prev = lax.scan(step, jnp.zeros((B, H, DK, DV), f32),
                       (jnp.moveaxis(decay, 2, 0), jnp.moveaxis(kv, 2, 0)))
    o = o + jnp.einsum('bhnid,bhnde->bhnie', q_dec, jnp.moveaxis(prev, 0, 2))
    o = o.transpose(0, 2, 3, 1, 4).reshape(B, S, H, DV)
    o = rms_norm(o, norm_g) * jax.nn.silu(r.astype(f32).reshape(B, S, H, DV))
    return o.reshape(B, S, H * DV).astype(q.dtype)

def swa_mixer(q, k, v, sinks):
    B, S, _ = q.shape
    H, KV, HD, W = SWA_HEADS, SWA_KV_HEADS, SWA_HD, SWA_WINDOW
    G = H // KV
    NB = S // W
    f32 = jnp.float32
    qb = q.reshape(B, NB, W, KV, G, HD).transpose(0, 3, 4, 1, 2, 5)

    def band(t):
        t = t.reshape(B, NB, W, KV, HD).transpose(0, 3, 1, 2, 4)
        prev = jnp.pad(t, ((0, 0), (0, 0), (1, 0), (0, 0), (0, 0)))[:, :, :-1]
        return jnp.concatenate([prev, t], axis=3)

    kb, vb = band(k), band(v)
    s = jnp.einsum('bkgnqd,bknsd->bkgnqs', qb, kb).astype(f32) * (HD ** -0.5)
    qi = jnp.arange(W)[:, None]
    sj = jnp.arange(2 * W)[None, :]
    in_window = (sj > qi) & (sj <= qi + W)
    started = (jnp.arange(NB)[:, None, None] > 0) | (sj[None] >= W)
    s = jnp.where(in_window[None] & started, s, NEG_INF)
    sink = sinks.astype(f32).reshape(KV, G)[None, :, :, None, None]
    m = jnp.maximum(jnp.max(s, axis=-1), sink)
    p = jnp.exp(s - m[..., None])
    denom = jnp.sum(p, axis=-1) + jnp.exp(sink - m)
    o = jnp.einsum('bkgnqs,bknsd->bkgnqd', p, vb.astype(f32)) / denom[..., None]
    o = o.transpose(0, 3, 4, 1, 2, 5).reshape(B, S, H * HD)
    return o.astype(q.dtype)

def moba_mixer(q, k, v):
    B, S, _ = q.shape
    H, HD, BLK, QC = MOBA_HEADS, MOBA_HD, MOBA_BLOCK, MOBA_QCHUNK
    NBK = -(-S // BLK)
    SP = NBK * BLK
    NQ = SP // QC
    f32 = jnp.float32
    scale = HD ** -0.5

    def heads(t):
        t = t.reshape(B, S, H, HD).transpose(0, 2, 1, 3)
        return jnp.pad(t, ((0, 0), (0, 0), (0, SP - S), (0, 0)))

    qh, kh, vh = heads(q), heads(k), heads(v)
    kb = kh.reshape(B, H, NBK, BLK, HD)
    vb = vh.reshape(B, H, NBK, BLK, HD)
    k_mean = jnp.mean(kb.astype(f32), axis=3)
    gate = jnp.einsum('bhsd,bhnd->bhsn', qh.astype(f32), k_mean)
    q_blk = jnp.arange(SP) // BLK
    past = jnp.arange(NBK)[None, :] < q_blk[:, None]
    gate = jnp.where(past, gate, NEG_INF)
    n_sel = min(MOBA_TOPK, max(NBK - 1, 1))
    _, sel = lax.top_k(gate, n_sel)
    sel_valid = sel < q_blk[:, None]

    def chunks(t):
        return jnp.moveaxis(t.reshape((B, H, NQ, QC) + t.shape[3:]), 2, 0)

    b_ix = jnp.arange(B)[:, None, None, None]
    h_ix = jnp.arange(H)[None, :, None, None]

    def attend(args):
        qc, selc, validc, c = args
        blk = (c * QC) // BLK
        k_own = lax.dynamic_index_in_dim(kb, blk, axis=2, keepdims=False)
        v_own = lax.dynamic_index_in_dim(vb, blk, axis=2, keepdims=False)
        q_pos = c * QC + jnp.arange(QC)
        k_pos = blk * BLK + jnp.arange(BLK)
        s_own = jnp.einsum('bhqd,bhkd->bhqk', qc, k_own).astype(f32)
        s_own = jnp.where(k_pos[None, :] <= q_pos[:, None], s_own, NEG_INF)
        k_sel = kb[b_ix, h_ix, selc]
        v_sel = vb[b_ix, h_ix, selc]
        s_sel = jnp.einsum('bhqd,bhqnkd->bhqnk', qc, k_sel).astype(f32)
        s_sel = jnp.where(validc[..., None], s_sel, NEG_INF).reshape(B, H, QC, n_sel * BLK)
        p = jax.nn.softmax(jnp.concatenate([s_own, s_sel], axis=-1), axis=-1)
        o = jnp.einsum('bhqk,bhkd->bhqd', p[..., :BLK], v_own.astype(f32))
        o = o + jnp.einsum('bhqnk,bhqnkd->bhqd', p[..., BLK:].reshape(B, H, QC, n_sel, BLK),
                           v_sel.astype(f32))
        return o.astype(qc.dtype)

    out = lax.map(attend, (chunks(qh * scale), chunks(sel), chunks(sel_valid), jnp.arange(NQ)))
    out = jnp.moveaxis(out, 0, 2).reshape(B, H, SP, HD)[:, :, :S]
    return out.transpose(0, 2, 1, 3).reshape(B, S, H * HD)

def retention_mixer(q, k, v, g, norm_g):
    B, S, _ = q.shape
    H, DK, DV, C = RET_HEADS, RET_DK, RET_DV, RET_CHUNK
    N = S // C
    half = DK // 2
    f32 = jnp.float32
    pos = jnp.arange(S, dtype=f32)
    inv_freq = RET_ROPE_BASE ** (-jnp.arange(half, dtype=f32) * 2.0 / DK)
    ang = pos[:, None] * inv_freq[None, :]
    cos = jnp.cos(ang)[:, None, :]
    sin = jnp.sin(ang)[:, None, :]

    def rotate(t):
        t1, t2 = t[..., :half], t[..., half:]
        return jnp.concatenate([t1 * cos - t2 * sin, t1 * sin + t2 * cos], axis=-1)

    def chunked(t, d):
        return t.reshape(B, N, C, H, d).transpose(0, 3, 1, 2, 4)

    qc = chunked(rotate(q.astype(f32).reshape(B, S, H, DK)), DK)
    kc = chunked(rotate(k.astype(f32).reshape(B, S, H, DK)), DK) * (DK ** -0.5)
    vc = chunked(v.astype(f32).reshape(B, S, H, DV), DV)
    log_gamma = jnp.log1p(-jnp.exp2(-5.0 - jnp.arange(H, dtype=f32)))
    idx = jnp.arange(C, dtype=f32)
    rel = idx[:, None] - idx[None, :]
    decay_mat = jnp.where(rel >= 0, jnp.exp(jnp.maximum(rel, 0.0)[None] * log_gamma[:, None, None]), 0.0)
    att = jnp.einsum('bhnid,bhnjd->bhnij', qc, kc) * decay_mat[None, :, None]
    o = jnp.einsum('bhnij,bhnje->bhnie', att, vc)
    key_decay = jnp.exp((C - 1 - idx)[None, :] * log_gamma[:, None])
    query_decay = jnp.exp((idx + 1)[None, :] * log_gamma[:, None])
    chunk_decay = jnp.exp(C * log_gamma)
    kv = jnp.einsum('bhnjd,bhnje->bhnde', kc * key_decay[None, :, None, :, None], vc)

    def step(state, kv_n):
        return chunk_decay[None, :, None, None] * state + kv_n, state

    _, prev = lax.scan(step, jnp.zeros((B, H, DK, DV), f32), jnp.moveaxis(kv, 2, 0))
    o = o + jnp.einsum('bhnid,bhnde->bhnie', qc, jnp.moveaxis(prev, 0, 2)) * query_decay[None, :, None, :, None]
    o = o.transpose(0, 2, 3, 1, 4).reshape(B, S, H, DV)
    o = rms_norm(o, norm_g) * jax.nn.silu(g.astype(f32).reshape(B, S, H, DV))
    return o.reshape(B, S, H * DV).astype(q.dtype)

def token_mixer(u, w_in, gla_w_a2, gla_b_a, gla_norm_g, swa_sinks, ret_norm_g, w_branch, w_out):
    p = split_columns(u @ w_in)
    branches = (
        gla_mixer(p['gla_q'], p['gla_k'], p['gla_v'], p['gla_r'], p['gla_a'], gla_w_a2, gla_b_a, gla_norm_g),
        swa_mixer(p['swa_q'], p['swa_k'], p['swa_v'], swa_sinks),
        moba_mixer(p['moba_q'], p['moba_k'], p['moba_v']),
        retention_mixer(p['ret_q'], p['ret_k'], p['ret_v'], p['ret_g'], ret_norm_g),
    )
    gates = p['gates']
    merged = None
    for i, o in enumerate(branches):
        term = jax.nn.sigmoid(gates[..., i * D_MODEL:(i + 1) * D_MODEL]) * (o @ w_branch[i])
        merged = term if merged is None else merged + term
    return merged @ w_out

def hier_moe(u, w_group, b_group, w_expert, b_expert, w1, w3, w2):
    B, S, D = u.shape
    T = B * S
    TK = T * EXPERT_TOPK
    f32 = jnp.float32
    xt = u.reshape(T, D)
    p_group = jax.nn.softmax((xt @ w_group + b_group).astype(f32), axis=-1)
    g_sel = jnp.argmax(p_group, axis=-1)
    g_w = jnp.take_along_axis(p_group, g_sel[:, None], axis=1)[:, 0]
    e_logits = (xt @ w_expert + b_expert).astype(f32).reshape(T, N_GROUPS, EXPERTS_PER_GROUP)
    e_logits = jnp.take_along_axis(e_logits, g_sel[:, None, None], axis=1)[:, 0]
    top_logit, top_local = lax.top_k(e_logits, EXPERT_TOPK)
    top_w = jax.nn.softmax(top_logit, axis=-1) * g_w[:, None]
    expert_id = (g_sel[:, None] * EXPERTS_PER_GROUP + top_local).reshape(TK).astype(jnp.int32)
    weight = top_w.reshape(TK).astype(u.dtype)
    token_id = jnp.repeat(jnp.arange(T, dtype=jnp.int32), EXPERT_TOPK)

    n_blocks = -(-TK // MOE_BLOCK) + N_EXPERTS
    P = n_blocks * MOE_BLOCK
    order = jnp.argsort(expert_id)
    e_sorted = expert_id[order]
    counts = jnp.bincount(expert_id, length=N_EXPERTS)
    padded = ((counts + MOE_BLOCK - 1) // MOE_BLOCK) * MOE_BLOCK
    start = jnp.cumsum(counts) - counts
    pend = jnp.cumsum(padded)
    pstart = pend - padded
    dest = pstart[e_sorted] + jnp.arange(TK, dtype=jnp.int32) - start[e_sorted]
    slot_tok = jnp.full((P,), T, dtype=jnp.int32).at[dest].set(token_id[order])
    slot_w = jnp.zeros((P,), dtype=u.dtype).at[dest].set(weight[order])
    blk_e = jnp.clip(jnp.searchsorted(pend, jnp.arange(n_blocks, dtype=pend.dtype) * MOE_BLOCK, side='right'),
                     0, N_EXPERTS - 1)
    x_pad = jnp.concatenate([xt, jnp.zeros((1, D), xt.dtype)], axis=0)
    xs = x_pad[slot_tok].reshape(n_blocks, MOE_BLOCK, D)

    def expert_block(args):
        xb, e = args
        hdn = jax.nn.silu(xb @ w1[e]) * (xb @ w3[e])
        return hdn @ w2[e]

    ys = lax.map(expert_block, (xs, blk_e)).reshape(P, D)
    out = jnp.zeros((T + 1, D), ys.dtype).at[slot_tok].add(ys * slot_w[:, None])[:T]
    return out.reshape(B, S, D)

def setup_inputs(seed: int = 0) -> dict:
    key = jax.random.key(seed)
    ks = jax.random.split(key, 19)
    f32 = jnp.float32
    L, D = DEPTH, D_MODEL

    def nrm(k, shape, scale):
        return jax.random.normal(k, shape, f32) * scale

    return {
        'x': nrm(ks[0], (BATCH, SEQ, D), 1.0),
        'ln1_g': 1.0 + nrm(ks[1], (L, D), 0.02),
        'w_in': nrm(ks[2], (L, D, IN_WIDTH), D ** -0.5),
        'gla_w_a2': nrm(ks[3], (L, GLA_LOWRANK, GLA_HEADS * GLA_DK), GLA_LOWRANK ** -0.5),
        'gla_b_a': nrm(ks[4], (L, GLA_HEADS * GLA_DK), 0.1),
        'gla_norm_g': 1.0 + nrm(ks[5], (L, GLA_DV), 0.02),
        'swa_sinks': nrm(ks[6], (L, SWA_HEADS), 0.5),
        'ret_norm_g': 1.0 + nrm(ks[7], (L, RET_DV), 0.02),
        'w_branch': nrm(ks[8], (L, N_BRANCH, BRANCH_WIDTH, D), BRANCH_WIDTH ** -0.5),
        'w_out': nrm(ks[9], (L, D, D), D ** -0.5),
        'ln2_g': 1.0 + nrm(ks[10], (L, D), 0.02),
        'w_group': nrm(ks[11], (L, D, N_GROUPS), D ** -0.5),
        'b_group': nrm(ks[12], (L, N_GROUPS), 0.01),
        'w_expert': nrm(ks[13], (L, D, N_EXPERTS), D ** -0.5),
        'b_expert': nrm(ks[14], (L, N_EXPERTS), 0.01),
        'w1': nrm(ks[15], (L, N_EXPERTS, D, EXPERT_HIDDEN), D ** -0.5),
        'w3': nrm(ks[16], (L, N_EXPERTS, D, EXPERT_HIDDEN), D ** -0.5),
        'w2': nrm(ks[17], (L, N_EXPERTS, EXPERT_HIDDEN, D), EXPERT_HIDDEN ** -0.5),
        'final_g': 1.0 + nrm(ks[18], (D,), 0.02),
    }

def reference(x, ln1_g, w_in, gla_w_a2, gla_b_a, gla_norm_g, swa_sinks, ret_norm_g, w_branch, w_out,
              ln2_g, w_group, b_group, w_expert, b_expert, w1, w3, w2, final_g):
    h = x
    for l in range(DEPTH):
        h = h + token_mixer(rms_norm(h, ln1_g[l]), w_in[l], gla_w_a2[l], gla_b_a[l], gla_norm_g[l],
                            swa_sinks[l], ret_norm_g[l], w_branch[l], w_out[l])
        h = h + hier_moe(rms_norm(h, ln2_g[l]), w_group[l], b_group[l], w_expert[l], b_expert[l],
                         w1[l], w3[l], w2[l])
    return rms_norm(h, final_g)


_drawn_inputs = setup_inputs


def setup_inputs(seed=0):
    import zlib

    import numpy as np

    out = dict(_drawn_inputs(seed))
    spreads = {}
    factors = {'swa_sinks': 3.726, 'b_group': 3.134, 'final_g': 2.911}
    for name, (base, spread) in spreads.items():
        noise = np.random.default_rng([zlib.crc32(name.encode()), seed]).standard_normal(out[name].shape)
        drawn = base * np.exp(spread * noise) if base else spread * noise
        out[name] = __import__('jax').numpy.asarray(drawn.astype(out[name].dtype))
    for name, factor in factors.items():
        out[name] = (out[name] * factor).astype(out[name].dtype)
    return out
```

```python
import concourse.bass as bass
from concourse import mybir
from contextlib import ExitStack
import numpy as np

L, D, S, P = 2, 1024, 512, 128
NT, KD = S // P, D // P
HEADS, DK, DV, HD, CG = 4, 32, 64, 64, 64
NE, NG, EG, FH = 32, 4, 8, 256
NP = NE // 2
CAP, NW = 64, 8
WIN = 6928
EPS = 1e-6
NEG = -1.0e30
COL = {"gq": 0, "gk": 128, "gv": 256, "gr": 512, "ga": 768, "sq": 784, "sk": 1040, "sv": 1168,
       "mq": 1296, "mk": 1552, "mv": 1808, "rq": 2064, "rk": 2192, "rv": 2320, "rg": 2576, "gate": 2832}
UNITS = [("ga", 128), ("gv", 256), ("gr", 256), ("gq", 256), ("sq", 256), ("sk", 256), ("rq", 256),
         ("rv", 256), ("rg", 256), ("mq", 256), ("mk", 256), ("mv", 256)]
U_GATE, U_OUT, U_ALL = 12, 28, 32
RING = 4
PLACE = (0, 2, 1, 3)
HALVES = [("T", 0, 0, "ga"), ("R", 1, 0, "gv"), ("R", 1, 1, "gv"), ("R", 2, 0, "gr"), ("R", 2, 1, "gr"),
          ("T", 3, 0, "gq"), ("T", 3, 128, "gk"), ("T", 4, 0, "sq"), ("T", 4, 128, "sq"), ("T", 5, 0, "sk"),
          ("V", 5, 128, "sv"), ("T", 6, 0, "rq"), ("T", 6, 128, "rk"), ("R", 7, 0, "rv"), ("R", 7, 1, "rv"),
          ("R", 8, 0, "rg"), ("R", 8, 1, "rg"), ("T", 9, 0, "mq"), ("T", 9, 128, "mq"), ("T", 10, 0, "mk"),
          ("T", 10, 128, "mk"), ("R", 11, 0, "mv"), ("R", 11, 1, "mv")]
NH = len(HALVES)
N_CST = NT + 8
NITEMS = 2 * HEADS * NT
STEP0 = 20
ROWS = S * 2
SENT = 1 << 20


class Sig:

    def __init__(self, handle, per_layer, credit=0):
        self.h, self.k, self.credit = handle, per_layer, credit

    def at(self, lay, n):
        return lay * self.k + (n + self.credit)


def used_at(u):
    if u < U_GATE:
        return 2 * u + 1
    return NH + 2 * (u - U_GATE + 1) if u < U_OUT else NH + 32 + (4 if u < U_OUT + 2 else 8)


def item(n):
    win, h, t = n < NITEMS // 2, (n // NT) % HEADS, n % NT
    k0 = max(t - 1, 0) if win else 0
    return win, h, t, k0, t + 1 - k0


def trunk(nc, a, out):
    f32, f32r, i32, u32 = mybir.dt.float32, mybir.dt.float32r, mybir.dt.int32, mybir.dt.uint32
    ALU, ACT, AX = mybir.AluOpType, mybir.ActivationFunctionType, mybir.AxisListType
    ds = bass.ds
    ctx = ExitStack()
    KB = 1024
    BASE = -(-nc.sbuf_base // 64) * 64

    def sb(name, shape, dt, off):
        return nc.alloc_sbuf_tensor_at(name, shape, dt, offset=BASE + int(off))

    h_dram = nc.dram_tensor("h_dram", (S, D), f32, kind="Internal").ap()
    x_dram = nc.dram_tensor("x_dram", (S, D), f32, kind="Internal").ap()
    y_dram = nc.dram_tensor("y_dram", (ROWS, D), f32, kind="Internal").ap()
    list_dram = nc.dram_tensor("list_dram", (S * NE, 1), i32, kind="Internal").ap()

    spare_dram = nc.dram_tensor("spare_dram", (3 * P, 1), i32, kind="Internal").ap()

    R_U, R_RAW, R_RH, R_B, R_O, R_T1, R_T2, R_C = (x * KB for x in (0, 32, 64, 96, 112, 144, 176, 198))
    uH = sb("uH", [P, KD, S], f32r, R_U)
    uL = sb("uL", [P, KD, S], f32r, R_U + 16 * KB)
    raw = sb("raw", [P, RING, 2048], f32, R_RAW)
    ringL = sb("ringL", [P, RING, 2048], f32r, R_RAW)
    ringH = sb("ringH", [P, RING, 2048], f32r, R_RH)
    swq = sb("swq", [P, 2, S], f32, R_B)
    swk = sb("swk", [P, S], f32, R_B + 4 * KB)
    swv = sb("swv", [P, NT, P], f32, R_B + 6 * KB)
    tabs = sb("tabs", [P, 1920], f32, R_B + 8 * KB)
    cos, sin = tabs[:, 0:512], tabs[:, 512:1024]
    decay = tabs[:, 1024:1536].rearrange("p (h i) -> p h i", h=HEADS)
    qdec, kdec, rot = tabs[:, 1536:1664], tabs[:, 1664:1792], tabs[:, 1792:1920]
    w13 = sb("w13", [P, 4, 2, 2048], f32, R_RAW)
    w2 = [sb(f"w2_{x}", [P, 2, D], f32, off) for x, off in
          enumerate((R_B, R_B + 8 * KB, R_T1, R_T1 + 8 * KB))]
    oH = sb("oH", [P, 8, S], f32r, R_O)
    oL = sb("oL", [P, 8, S], f32r, R_O + 16 * KB)
    u2T = sb("u2T", [P, KD, S], f32, R_O)
    ut = sb("ut", [P, 2, D], f32, R_O + 16 * KB)
    junk = sb("junk", [P, D], f32, R_O + 24 * KB)
    qT = sb("qT", [P, S], f32, R_T1)
    kT = sb("kT", [P, S], f32, R_T1 + 2 * KB)
    k2T = sb("k2T", [P, S], f32, R_T1 + 4 * KB)
    bT = sb("bT", [P, S], f32, R_T1 + 6 * KB)
    k2 = sb("k2", [P, NT, P], f32, R_T1 + 8 * KB)
    vv = sb("vv", [P, NT, 256], f32, R_T1 + 10 * KB)
    zaT = sb("zaT", [16, S], f32, R_T1 + 6 * KB)
    sr = sb("sr", [P, NT, 256], f32, R_T1 + 14 * KB)
    attT = sb("attT", [P, HEADS, NT, P], f32, R_T1 + 18 * KB)
    prev = sb("prev", [P, 8, DV], f32, R_T1 + 26 * KB)
    on = sb("on", [P, NT, HEADS, DV], f32, R_T1 + 28 * KB)
    lga = sb("lga", [P, 2, S], f32, R_T1 + 28 * KB)
    g1 = sb("g1", [P, D], f32, R_T1 + 28 * KB)
    g2 = sb("g2", [P, D], f32, R_T1 + 24 * KB)
    merged = sb("merged", [P, KD, S], f32, R_T1)
    sig = sb("sig", [P, 2, S], f32, R_T1 + 16 * KB)
    term = sb("term", [P, 2, S], f32, R_T1 + 20 * KB)
    braw = [sb(f"braw{x}", [P, 512], f32, R_T1 + (24 + 4 * x) * KB) for x in range(2)]
    bL = [sb(f"bL{x}", [P, 512], f32r, R_T1 + (24 + 4 * x) * KB) for x in range(2)]
    bH = [sb(f"bH{x}", [P, 512], f32r, R_T1 + (26 + 4 * x) * KB) for x in range(2)]
    yl = sb("yl", [P, 2, 2, D], f32, R_O)
    mq = sb("mq", [P, 2, S], f32, R_T2)
    mk = sb("mk", [P, 2, S], f32, R_T2 + 4 * KB)
    mv = sb("mv", [P, NT, 256], f32, R_T2 + 8 * KB)
    pr = sb("pr", [P, 2, S], f32, R_T2 + 12 * KB)
    prT = sb("prT", [P, 2, S], f32, R_T2 + 16 * KB)
    hs = sb("hs", [P, NT, D], f32, R_T2)
    rc = sb("rc", [P, 320], f32, R_T2 + 16 * KB)
    upper, ones, iota32 = rc[:, 0:128], rc[:, 128:256], rc[:, 256:288]
    wr = sb("wr", [P, KD, NG + NE], f32, R_T2 + 17.5 * KB)
    xg = [sb(f"xg{x}", [P, D], f32, R_U + 4 * x * KB) for x in range(2)]
    xT = [sb(f"xT{x}", [P, D], f32, R_U + (8 + 4 * x) * KB) for x in range(2)]
    ysb = [sb(f"ysb{x}", [P, D], f32, R_U + (16 + 4 * x) * KB) for x in range(2)]
    silu = sb("silu", [P, FH], f32, R_U + 24 * KB)
    hid = sb("hid", [P, FH], f32, R_U + 25 * KB)
    hT = sb("hT", [P, 2, P], f32, R_U + 26 * KB)
    at = [R_C]

    def small(name, shape, dt=f32):
        n = int(np.prod(shape[1:])) * 4
        t = sb(name, shape, dt, at[0])
        at[0] += -(-n // 32) * 32
        return t

    cst = small("cst", [P, 544])
    ident, wmask, gmask = cst[:, 0:128], cst[:, 128:384], cst[:, 384:512]
    cdec, prio, nhalf = cst[:, 512:513], cst[:, 516:520], cst[:, 520:536]
    wa2 = small("wa2", [16, L, P])
    wa2s = small("wa2s", [16, P])
    ba = small("ba", [P, L])
    ng = small("ng", [P, L, 2, DV])
    sink = small("sink", [P, L, HEADS])
    nsink = small("nsink", [P, L, HEADS])
    rb = small("rb", [P, L, NG + NE])
    sent = small("sent", [P, NW, NP], i32)
    val = small("val", [P, 8], i32)
    ss = small("ss", [P, 8]); ms = small("ms", [P, 8]); rstd = small("rstd", [P, 8])
    hss = small("hss", [P, HEADS, NT]); hms = small("hms", [P, 16]); hrs = small("hrs", [P, HEADS, NT])
    dec = small("dec", [P, 8])
    nm = small("nm", [P, 2]); nb = small("nb", [P, 2]); es = small("es", [P, 2]); den = small("den", [P, 2])
    den2 = small("den2", [P, 2]); rden = small("rden", [P, 2])
    lists = small("lists", [P, NW, NP], i32)
    toks = small("toks", [P, NW, NP], i32)
    gi = [small(f"gi{x}", [P, 1], i32) for x in range(2)]
    di = [small(f"di{x}", [P, 1], i32) for x in range(2)]
    wts = small("wts", [P, 2, NT])
    extra = small("extra", [P, L + 1])
    windows = small("windows", [P, 2, L + 1], i32)
    most = small("most", [P, 1]); over_n = small("over_n", [P, NW])
    rt = [R_T1 + 16 * KB]

    def rtmp(name, shape, dt=f32):
        n = int(np.prod(shape[1:])) * 4
        t = sb(name, shape, dt, rt[0])
        rt[0] += -(-n // 32) * 32
        return t

    lg = rtmp("lg", [P, NT, NG + NE])
    gm = rtmp("gm", [P, NT]); gd = rtmp("gd", [P, NT, NG]); ge = rtmp("ge", [P, NT, NG])
    gs = rtmp("gs", [P, NT]); gw = rtmp("gw", [P, NT]); geq = rtmp("geq", [P, NT, NG])
    gp = rtmp("gp", [P, NT, NG]); pm = rtmp("pm", [P, NT]); oh = rtmp("oh", [P, NT, NG])
    gidx = rtmp("gidx", [P, NT]); esel = rtmp("esel", [P, NT, NG, EG]); el = rtmp("el", [P, NT, EG])
    v8 = rtmp("v8", [P, NT, 8]); i8 = rtmp("i8", [P, NT, 8], u32); dx = rtmp("dx", [P, NT])
    ex = rtmp("ex", [P, NT]); ex1 = rtmp("ex1", [P, NT]); rex = rtmp("rex", [P, NT])
    idf = rtmp("idf", [P, NT, 2]); eid = rtmp("eid", [P, NT, 2])
    second = rtmp("second", [P, NT, 2]); slot0 = rtmp("slot0", [P, NT, 2])
    sel = rtmp("sel", [P, NT, 2, NE]); selM = rtmp("selM", [P, NT, NE])
    rk = rtmp("rk", [P, NT, 2, NE]); rank = rtmp("rank", [P, NT, 2]); row = rtmp("row", [P, 8], i32)
    assert rt[0] <= R_T1 + 24 * KB and BASE + at[0] <= nc.sbuf_usable_end, (at[0], rt[0])

    ps = ctx.enter_context(nc.psum_tensor("ps", [P, 8 * 512], f32))

    def bank(b, n=512):
        return ps[:, b * 512:b * 512 + n]

    A = [2, 3, 4, 5, 6, 7]

    def signal(name, per_layer, credit=0):
        return Sig(ctx.enter_context(nc.semaphore(name)), per_layer, credit)

    s_cst = signal("s_cst", 0)
    s_init = signal("s_init", 0)
    w_in_slot = [signal(f"w_in_slot{s}", 16 * 8) for s in range(RING)]
    w_h = signal("w_h", U_ALL)
    w_l = signal("w_l", U_ALL)
    b_in = [signal(f"b_in{x}", 16 * 8) for x in range(2)]
    b_h = signal("b_h", 16)
    b_l = signal("b_l", 16)
    w13_in = [signal(f"w13_in{x}", 32 * 8) for x in range(4)]
    w2_in = [signal(f"w2_in{x}", 16 * 8) for x in range(4)]
    tabs_in = signal("tabs_in", 16)
    g1_in = signal("g1_in", 16)
    g2_in = signal("g2_in", 16)
    rc_in = signal("rc_in", 16 * 3)
    h_out = signal("h_out", 16)
    h_in = signal("h_in", 16)
    list0 = signal("list0", 16)
    h_ready = signal("h_ready", NT)
    n_ss = signal("n_ss", 8, 1); n_ms = signal("n_ms", 8); n_rs = signal("n_rs", 8); n_u = signal("n_u", 8)
    n_t = signal("n_t", 8); n_h = signal("n_h", 8); n_l = signal("n_l", 4)
    pj = signal("pj", NH + 40)
    NB0, NB1 = (NH + 1) // 2, NH // 2
    pj_free = [signal("pj_free0", NB0 + 20), signal("pj_free1", NB1 + 20)]
    wa = signal("wa", 1)
    lgm = signal("lgm", 1)
    lg_a = signal("lg_a", 1); lg_b = signal("lg_b", 1); lg_d = signal("lg_d", 1); lg_e = signal("lg_e", 4)
    rotd = signal("rotd", 2); rqk = signal("rqk", 1)
    att0 = signal("att0", 1)
    att = signal("att", 8); att_e = signal("att_e", 8)
    ktr = signal("ktr", 2); kk2 = signal("kk2", 2); kv = signal("kv", 2); st = signal("st", 2)
    srg = signal("srg", 2)
    o_m = signal("o_m", 8); o_sq = signal("o_sq", 8); o_ms = signal("o_ms", 2); o_rs = signal("o_rs", 2)
    o_e = signal("o_e", 8); o_n = signal("o_n", 2); o_t = signal("o_t", 4); o_h = signal("o_h", 4)
    o_l = signal("o_l", 4)
    sc = signal("sc", NITEMS); sc_b = signal("sc_b", NITEMS); sc_p = signal("sc_p", NITEMS)
    sc_n = signal("sc_n", NITEMS); sc_t = signal("sc_t", NITEMS)
    sc_ea = signal("sc_ea", NITEMS // 2); sc_ed = signal("sc_ed", NITEMS // 2)
    a_o = signal("a_o", 4); a_h = signal("a_h", 4); a_l = signal("a_l", 4)
    yb = signal("yb", 32, 4); tm = signal("tm", 32)
    mg = signal("mg", 24)
    m_h = signal("m_h", 8); m_l = signal("m_l", 8)
    u2o = [signal(f"u2o{x}", 16 * 2) for x in range(2)]
    rl = signal("rl", NT)
    r_e = signal("r_e", 2); r_x = signal("r_x", 2); r_m = signal("r_m", 1); r_r = signal("r_r", 1)
    r_row = signal("r_row", 1)
    l_sc = signal("l_sc", 16 * 8); l_in = signal("l_in", 16 * 4); l_g = signal("l_g", 1)
    xg_in = [signal(f"xg_in{x}", 16 * 8) for x in range(2)]
    x_t = signal("x_t", NP); x_ca = signal("x_ca", NP); x_cd = signal("x_cd", NP)
    up = signal("up", NP, 2); sl = signal("sl", NP); hd = signal("hd", NP); h_t = signal("h_t", NP)
    h_c = signal("h_c", NP); yd = signal("yd", NP)
    y_ea = signal("y_ea", NP, 1); y_ed = signal("y_ed", NP, 1)
    y_out = [signal(f"y_out{x}", 16 * 8, 16) for x in range(2)]
    yl_in = [signal(f"yl_in{x}", 16 * 2) for x in range(2)]
    win_n = signal("win_n", 1)
    ov_w, ov_x, ov_t, ov_c, ov_u, ov_s, ov_h, ov_ht, ov_hc, ov_y, ov_e, ov_o, ov_p = (
        ctx.enter_context(nc.semaphore(f"ov_{x}")) for x in
        ("weights", "rows", "transposed", "columns", "up", "silu", "hidden", "hidden_t", "hidden_c", "down", "out", "stored", "index"))
    s_out = [signal(f"s_out{x}", 0) for x in range(2)]
    fin = signal("fin", 0)
    tmc = lambda t: slice(t * P, (t + 1) * P)

    block = ctx.enter_context(nc.Block())
    DVE_LINKS, ACT_LINKS = 159, 2
    dve_c = signal("dve_c", DVE_LINKS)
    act_c = signal("act_c", ACT_LINKS)
    pc = signal("pc", 2 * NP)

    def w_in_cols(l, c0, n):
        return a["w_in"][ds(l, 1), :, c0:c0 + n].rearrange("o (k p) n -> p (o k) n", p=P)

    held = ctx.enter_context(nc.semaphore("held"))

    def wait(eng, s, value):
        eng.wait_ge(s, value)

    def hold(eng, s, value):
        eng.wait_ge(s, value).then_inc(held, 1)

    def window_range(eng, lay):
        hold(eng, win_n.h, win_n.at(lay, 1))
        return (eng.value_load(windows[0:1, 0, ds(lay, 1)], min_val=0, max_val=(NW - 1) * L),
                eng.value_load(windows[0:1, 1, ds(lay, 1)], min_val=0, max_val=NW - 1))

    def later_windows(eng, before, own, item_):
        with eng.If(own):
            with eng.Fori(0, own) as w:
                with eng.Fori(0, NP) as p:
                    item_((before + w) * NP + p, p, (w + 1) * NP + p)

    @block.sync
    def _(sp):
        for t in range(NT):
            sp.dma_start(hs[:, t, :], a["x"][0, t * P:(t + 1) * P, :]).then_inc(s_cst.h, 16)
        for dst, src in ((cst[:], a["c_small"]), (wa2[:], a["gla_w_a2"].rearrange("l r n -> r l n")),
                         (ba[:], a["gla_b_a"].rearrange("l n -> n l")),
                         (ng[:, :, 0, :], a["gla_norm_g"].partition_broadcast(P)),
                         (ng[:, :, 1, :], a["ret_norm_g"].partition_broadcast(P)),
                         (sink[:], a["swa_sinks"].partition_broadcast(P)),
                         (rb[:, :, 0:NG], a["b_group"].partition_broadcast(P)),
                         (rb[:, :, NG:], a["b_expert"].partition_broadcast(P))):
            sp.dma_start(dst, src, allow_slow_non_contiguous=True).then_inc(s_cst.h, 16)
        sp.dma_start(g1[:], a["ln1_g"][0:1, :].partition_broadcast(P)).then_inc(g1_in.h, 16)
        with sp.Fori(0, L) as lay:

            def fill(u, src, dst=None):
                if u < RING:
                    hold(sp, up.h, up.at(lay, u // 2 - 1))
                else:
                    hold(sp, pj.h, pj.at(lay, used_at(u - RING)))
                sp.dma_start(dst, src).then_inc(w_in_slot[u % RING].h, 16)

            for u, (name, n) in enumerate(UNITS):
                slot = raw[:, u % RING, 0:KD * n].rearrange("p (k n) -> p k n", k=KD)
                fill(u, w_in_cols(lay, COL[name], n), slot)
                if u == 3:
                    hold(sp, h_ready.h, h_ready.at(lay, NT))
                    sp.dma_start(h_dram.rearrange("(t p) n -> p t n", p=P), hs[:]).then_inc(h_out.h, 16)
                if u == 4:
                    sp.dma_start(tabs[:], a["c_tabs"]).then_inc(tabs_in.h, 16)
                    sp.dma_start(list_dram.rearrange("(p n) o -> p (n o)", p=P), sent[:].rearrange("p r e -> p (r e)"))\
                      .then_inc(list0.h, 16)

            def gate_fill(g, u):
                slot = raw[:, u % RING, :].rearrange("p (k n) -> p k n", k=KD)
                hold(sp, pj.h, pj.at(lay, used_at(u - RING)) if isinstance(g, int) else pj.at(lay, NH - 2 * (RING - 1)) + g * 2)
                src = a["w_in"][ds(lay, 1), :, ds(g * 256 + COL["gate"], 256)].rearrange("o (k p) n -> p (o k) n", p=P)
                sp.dma_start(slot, src).then_inc(w_in_slot[u % RING].h, 16)

            def bfill(i, c):
                hold(sp, yb.h, yb.at(lay, 2 * c - 2) + i * 8)
                src = a["w_branch"][ds(lay, 1), ds(i, 1), :, c * 256:(c + 1) * 256].rearrange("o q (k p) n -> p (o q k) n", p=P)
                sp.dma_start(braw[c % 2][:].rearrange("p (k n) -> p k n", k=2), src).then_inc(b_in[c % 2].h, 16)

            def out_fill(u):
                slot = raw[:, u % RING, :].rearrange("p (k n) -> p k n", k=KD)
                c0 = (u - U_OUT) * 256
                fill(u, a["w_out"][ds(lay, 1), :, c0:c0 + 256].rearrange("o (k p) n -> p (o k) n", p=P), slot)

            gate_fill(0, U_GATE)
            gate_fill(1, U_GATE + 1)
            for c in range(4):
                gate_fill(c + 2, U_GATE + c + 2)
                bfill(0, c)
            with sp.Fori(1, 3) as i:
                for c in range(4):
                    gate_fill(i * 4 + (c + 2), U_GATE + c + 2)
                    bfill(i, c)
            hold(sp, a_l.h, a_l.at(lay, 2))

            def w2_fill(i, r):
                src = a["w2"][ds(lay, 1), ds(i * 2 + (r // 2 + NP * (r % 2)), 1)].rearrange("o q (k p) n -> p (o q k) n", p=P)
                sp.dma_start(w2[r][:], src).then_inc(w2_in[r].h, 16)

            def w13_fill(i, r):
                for m, name in enumerate(("w1", "w3")):
                    src = a[name][ds(lay, 1), ds(i * 2 + (r // 2 + NP * (r % 2)), 1)].rearrange("o q (p k) n -> p (o q k n)", k=KD)
                    sp.dma_start(w13[:, PLACE[r], m, :], src).then_inc(w13_in[r].h, 16)

            w2_fill(0, 0)
            w2_fill(0, 1)
            for c in range(4):
                if c < 2:
                    gate_fill(14 + c, U_GATE + 14 + c)
                else:
                    out_fill(U_OUT + c - 2)
                bfill(3, c)
            out_fill(U_OUT + 2)
            sp.dma_start(hs[:], h_dram.rearrange("(t p) n -> p t n", p=P)).then_inc(h_in.h, 16)
            sp.dma_start(rc[:, 0:288], a["c_router"]).then_inc(rc_in.h, 16)
            sp.dma_start(wr[:, :, 0:NG], a["w_group"][ds(lay, 1)].rearrange("o (p k) n -> p (o k) n", k=KD)).then_inc(rc_in.h, 16)
            sp.dma_start(wr[:, :, NG:], a["w_expert"][ds(lay, 1)].rearrange("o (p k) n -> p (o k) n", k=KD)).then_inc(rc_in.h, 16)
            out_fill(U_OUT + 3)
            hold(sp, yb.h, yb.at(lay, 32))
            sp.dma_start(g2[:], a["ln2_g"][ds(lay, 1), :].partition_broadcast(P)).then_inc(g2_in.h, 16)

            hold(sp, pj.h, pj.at(lay, used_at(U_OUT + 1)))
            w13_fill(0, 0)
            w13_fill(0, 1)
            hold(sp, m_l.h, m_l.at(lay, KD))
            w2_fill(0, 2)
            w2_fill(0, 3)
            hold(sp, pj.h, pj.at(lay, used_at(U_OUT + 3)))
            w13_fill(0, 2)
            w13_fill(0, 3)
            with sp.Fori(1, NP // 2) as i:
                for y in range(2):
                    hold(sp, up.h, up.at(lay, y - 1) + i * 2)
                    w13_fill(i, 2 * y)
                    w13_fill(i, 2 * y + 1)
                    hold(sp, yd.h, yd.at(lay, y - 1) + i * 2)
                    w2_fill(i, 2 * y)
                    w2_fill(i, 2 * y + 1)

            def window_weights(n, p, col):
                hold(sp, yd.h, yd.at(lay, NP))
                hold(sp, ov_y, n + 1)
                for x in range(2):
                    for m, name in enumerate(("w1", "w3")):
                        src = a[name][ds(lay, 1), ds(p + NP * x, 1)].rearrange("o q (p k) n -> p (o q k n)", k=KD)
                        sp.dma_start(w13[:, PLACE[x], m, :], src).then_inc(ov_w, 16)
                    src = a["w2"][ds(lay, 1), ds(p + NP * x, 1)].rearrange("o q (k p) n -> p (o q k) n", p=P)
                    sp.dma_start(w2[x][:], src).then_inc(ov_w, 16)

            before, own = window_range(sp, lay)
            later_windows(sp, before, own, window_weights)
            hold(sp, ov_y, (before + own) * NP + 1)
            hold(sp, n_u.h, n_u.at(lay, 8))
            sp.dma_start(g1[:], a["c_next_gain"][ds(lay, 1), :].partition_broadcast(P)).then_inc(g1_in.h, 16)
        hold(sp, h_out.h, 16 * L)
        for t in range(NT):
            hold(sp, fin.h, t + 1)
            sp.dma_start(out[0, t * P:(t + 1) * P, :], ut[:, t % 2, :]).then_inc(s_out[t % 2].h, 16)
        for x in range(2):
            hold(sp, s_out[x].h, 16 * NT // 2)


    @block.tensor
    def _(pe):
        mm = nc.tensor.matmul

        def mm3(o, h, l, rh, rl_, first, last):
            mm(o, h, rh, start=first, stop=False)
            mm(o, h, rl_, start=False, stop=False)
            return mm(o, l, rh, start=False, stop=last)

        pe.wait_ge(s_cst.h, 16 * N_CST)
        with pe.Fori(0, L) as lay:

            def norm_transposes(n, dst_free):
                t = n % NT
                b = A[0] if t % 2 == 0 else A[2]
                pe.wait_ge(n_u.h, n_u.at(lay, n + 1))
                if t >= 2:
                    pe.wait_ge(dst_free.h, dst_free.at(lay, n - 1))
                for k in range(KD):
                    last = nc.tensor.transpose(ps[:, b * 512 + k * P:b * 512 + (k + 1) * P],
                                               ut[:, t % 2, k * P:(k + 1) * P], ident)
                last.then_inc(n_t.h, 1)

            for t in range(NT):
                norm_transposes(t, n_l)
            pe.wait_ge(n_l.h, n_l.at(lay, NT))

            def half(q):
                kind, u, off, name = HALVES[q]
                s, b = u % RING, q % 2
                n = UNITS[u][1]
                wH = ringH[:, s, 0:KD * n].rearrange("p (k n) -> p k n", k=KD)
                wL = ringL[:, s, 0:KD * n].rearrange("p (k n) -> p k n", k=KD)
                pe.wait_ge(w_l.h, w_l.at(lay, u + 1))
                if q >= 2:
                    pe.wait_ge(pj_free[b].h, pj_free[b].at(lay, q // 2))
                if kind == "T":
                    for k in range(KD):
                        last = mm3(bank(b), wH[:, k, off:off + P], wL[:, k, off:off + P], uH[:, k, :], uL[:, k, :],
                                   k == 0, k == KD - 1)
                else:
                    tiles, n0, nn = (range(2 * off, 2 * off + 2), 0, 256) if kind == "R" else (range(NT), off, P)
                    for i, t in enumerate(tiles):
                        for k in range(KD):
                            last = mm3(ps[:, b * 512 + i * nn:b * 512 + (i + 1) * nn], uH[:, k, tmc(t)], uL[:, k, tmc(t)],
                                       wH[:, k, n0:n0 + nn], wL[:, k, n0:n0 + nn], k == 0, k == KD - 1)
                last.then_inc(pj.h, 1)

            def log_decay():
                pe.wait_ge(pj_free[0].h, pj_free[0].at(lay, 1))
                pe.wait_ge(wa.h, wa.at(lay, 1))
                mm(bank(A[0]), wa2s[:], zaT[:], start=True, stop=True).then_inc(lgm.h, 1)

            def scores(br):
                if br == 0:
                    pe.wait_ge(pj_free[0].h, pj_free[0].at(lay, 4))
                else:
                    pe.wait_ge(rqk.h, rqk.at(lay, 1))
                for h in range(HEADS):
                    r = slice(DK * h, DK * (h + 1))
                    for t in range(NT):
                        last = mm(ps[:, A[h] * 512 + t * P:A[h] * 512 + (t + 1) * P], kT[r, tmc(t)], qT[r, tmc(t)],
                                  start=True, stop=True)
                    last.then_inc(att.h, 1)
                if br:
                    pe.wait_ge(o_l.h, o_l.at(lay, 2))
                for t in range(NT):
                    last = nc.tensor.transpose(ps[:, A[4] * 512 + t * P:A[4] * 512 + (t + 1) * P], k2T[:, tmc(t)], ident)
                last.then_inc(ktr.h, 1)

            def chunk_kv(br):
                hold(pe, kk2.h, kk2.at(lay, br + 1))
                if br:
                    pe.wait_ge(pj_free[0].h, pj_free[0].at(lay, 8))
                for n in range(8 if br == 0 else NT):
                    b = A[4] if br == 0 and n % 2 else A[5]
                    r = slice(CG * (n % 2), CG * (n % 2 + 1)) if br == 0 else slice(0, P)
                    t = n // 2 if br == 0 else n
                    for h in range(HEADS):
                        last = mm(ps[DK * h:DK * (h + 1), b * 512 + n * DV:b * 512 + (n + 1) * DV],
                                  k2[r, t, DK * h:DK * (h + 1)], vv[r, t, DV * h:DV * (h + 1)], start=True, stop=True)
                last.then_inc(kv.h, 1)

            def mix_out(br):
                pe.wait_ge(st.h, st.at(lay, br + 1))
                pe.wait_ge(att_e.h, att_e.at(lay, 4 * br + 4))
                r4 = [slice(DK * h, DK * (h + 1)) for h in range(HEADS)]
                qi = qT if br == 0 else bT
                for h in range(HEADS):
                    for t in range(NT):
                        o = ps[:, A[h] * 512 + t * DV:A[h] * 512 + (t + 1) * DV]
                        if br == 0:
                            for c in (2 * t, 2 * t + 1):
                                half_rows = slice(CG * (c % 2), CG * (c % 2 + 1))
                                mm(o[half_rows], qi[r4[h], CG * c:CG * (c + 1)], prev[r4[h], c, :], start=True, stop=False,
                                   skip_group_check=True)
                        else:
                            mm(o, qi[r4[h], tmc(t)], prev[r4[h], t, :], start=True, stop=False, skip_group_check=True)
                        last = mm(o, attT[:, h, t, :], vv[:, t, DV * h:DV * (h + 1)], start=False, stop=True,
                                  skip_group_check=True)
                    last.then_inc(o_m.h, 1)

            def out_transposes(br):
                pe.wait_ge(o_n.h, o_n.at(lay, br + 1))
                for hh in range(2):
                    for t in range(NT):
                        last = nc.tensor.transpose(ps[:, A[4 + hh] * 512 + t * P:A[4 + hh] * 512 + (t + 1) * P],
                                                   on[:, t, 2 * hh:2 * hh + 2, :].rearrange("p h e -> p (h e)"), ident)
                    last.then_inc(o_t.h, 1)

            def rotate():
                pe.wait_ge(pj_free[0].h, pj_free[0].at(lay, 7))
                pe.wait_ge(o_e.h, o_e.at(lay, 4))
                for x, src in enumerate((qT, kT)):
                    mm(bank(A[x]), rot, src[:], start=True, stop=True).then_inc(rotd.h, 1)

            def step(s):
                if 2 <= s:
                    for n in (2 * s - 4, 2 * s - 3):
                        win, h, t, k0, nk = item(n)
                        x = n % 2
                        e = (sc_ea, sc_ed)[x]
                        pe.wait_ge(e.h, e.at(lay, n // 2 + 1))
                        if n % 8 == 0 and n:
                            pe.wait_ge(a_l.h, a_l.at(lay, n // 8))
                        if n == 0:
                            pe.wait_ge(o_l.h, o_l.at(lay, 4))
                        o = ps[HD * (h % 2):HD * (h % 2 + 1), A[4] * 512 + t * P:A[4] * 512 + (t + 1) * P]
                        for i in range(nk):
                            v = swv[:, k0 + i, HD * (h // 2):HD * (h // 2 + 1)] if win else mv[:, k0 + i, HD * h:HD * (h + 1)]
                            last = mm(o, v, prT[:, x, i * P:(i + 1) * P], start=i == 0, stop=i == nk - 1, skip_group_check=True)
                    if n % 8 == 7:
                        last.then_inc(a_o.h, 1)
                if 1 <= s <= NITEMS // 2:
                    for n in (2 * s - 2, 2 * s - 1):
                        nk = item(n)[4]
                        pe.wait_ge(sc_n.h, sc_n.at(lay, n + 1))
                        for i in range(nk):
                            last = nc.tensor.transpose(ps[:, A[2 + n % 2] * 512 + i * P:A[2 + n % 2] * 512 + (i + 1) * P],
                                                       pr[:, n % 2, i * P:(i + 1) * P], ident)
                        last.then_inc(sc_t.h, 1)
                if s < NITEMS // 2:
                    if s == 0:
                        pe.wait_ge(o_e.h, o_e.at(lay, 8))
                    for n in (2 * s, 2 * s + 1):
                        win, h, t, k0, nk = item(n)
                        g = h // 2 if win else h % 2
                        r = slice(HD * g, HD * (g + 1))
                        keys = slice(k0 * P, (k0 + nk) * P)
                        q, k = (swq[r, h % 2, tmc(t)], swk[r, keys]) if win else (mq[r, h // 2, tmc(t)], mk[r, h // 2, keys])
                        mm(bank(A[n % 2], nk * P), q, k, start=True, stop=True).then_inc(sc.h, 1)

            PIECES = {1: log_decay, 7: lambda: scores(0), 8: lambda: chunk_kv(0), 10: lambda: mix_out(0),
                      12: lambda: out_transposes(0), 13: rotate, 15: lambda: scores(1), 16: lambda: chunk_kv(1),
                      18: lambda: mix_out(1), 20: lambda: out_transposes(1)}
            for q in range(NH):
                half(q)
                if q in PIECES:
                    PIECES[q]()
                if q >= STEP0:
                    step(q - STEP0)

            def branch(i, steps):
                for j in range(KD):
                    c, b = j // 2, (NH + j) % 2
                    wH, wL = (w[:, c, :].rearrange("p (k n) -> p k n", k=KD) for w in (ringH, ringL))
                    if j % 2 == 0:
                        pe.wait_ge(w_l.h, w_l.at(lay, U_GATE + c + 1) + i * 4)
                    pe.wait_ge(pj_free[b].h, pj_free[b].at(lay, (NH + j) // 2) + i * 4)
                    for k in range(KD):
                        last = mm3(bank(b), wH[:, k, ds((j % 2) * P, P)], wL[:, k, ds((j % 2) * P, P)],
                                   uH[:, k, :], uL[:, k, :], k == 0, k == KD - 1)
                    last.then_inc(pj.h, 1)
                    if steps is not None and j + steps < NITEMS // 2 + 2:
                        step(j + steps)
                    if j == 0 and steps == NH - STEP0:
                        pe.wait_ge(o_l.h, o_l.at(lay, 4))
                    if j == 0 and steps == NH - STEP0 + KD:
                        pe.wait_ge(a_l.h, a_l.at(lay, 2))
                    if j == 0 and steps is None:
                        pe.wait_ge(a_l.h, a_l.at(lay, 4))
                    if j % 2 == 0:
                        pe.wait_ge(b_l.h, b_l.at(lay, c + 1) + i * 4)
                    if not (steps == NH - STEP0 and j == 0):
                        pe.wait_ge(tm.h, tm.at(lay, j) + i * 8)
                    cc = ds((j % 2) * P, P)
                    for k in range(2):
                        h, l = (w[c % 2][:].rearrange("p (k n) -> p k n", k=2)[:, k, cc] for w in (bH, bL))
                        rh, rl_ = ((w[:, ds(i * 2 + k, 1), :] if steps is None else w[:, i * 2 + k:i * 2 + k + 1, :]).rearrange("p a n -> p (a n)")
                                   for w in (oH, oL))
                        last = mm3(bank(A[5]), h, l, rh, rl_, k == 0, k == 1)
                    last.then_inc(yb.h, 1)

            branch(0, NH - STEP0)
            branch(1, NH - STEP0 + KD)
            with pe.Fori(2, 4) as i:
                branch(i, None)

            def out_half(c, t):
                b = (NH + 32 + 4 * c + t) % 2
                pe.wait_ge(pj_free[b].h, pj_free[b].at(lay, (NH + 32 + 4 * c + t) // 2))
                if t == 0:
                    pe.wait_ge(w_l.h, w_l.at(lay, U_OUT + 2 * c + 2))
                for k in range(KD):
                    if c == 0 and t == 0:
                        pe.wait_ge(m_l.h, m_l.at(lay, k + 1))
                    rh, rl_ = (w[:, 2 * c:2 * c + 2, k * 256:(k + 1) * 256] for w in (ringH, ringL))
                    last = mm3(bank(b).rearrange("p (a n) -> p a n", a=2), uH[:, k, tmc(t)], uL[:, k, tmc(t)], rh, rl_,
                               k == 0, k == KD - 1)
                last.then_inc(pj.h, 1)

            def route(t):
                norm_transposes(NT + t, n_h)
                if t == 0:
                    pe.wait_ge(rc_in.h, rc_in.at(lay, 48))
                pe.wait_ge(n_h.h, n_h.at(lay, NT + t + 1))
                for k in range(KD):
                    last = mm(ps[:, A[5] * 512 + t * 36:A[5] * 512 + (t + 1) * 36], u2T[:, k, tmc(t)], wr[:, k, :],
                              start=k == 0, stop=k == KD - 1, skip_group_check=True)
                last.then_inc(rl.h, 1)

            for t in range(NT):
                out_half(0, t)
            for t in range(NT):
                out_half(1, t)
                if t:
                    route(t - 1)
            route(NT - 1)

            pe.wait_ge(r_m.h, r_m.at(lay, 1))
            for t in range(NT):
                o = ps[:, A[4] * 512 + t * NE:A[4] * 512 + (t + 1) * NE]
                for s in range(t):
                    mm(o, ones, selM[:, s, :], start=s == 0, stop=False, skip_group_check=True)
                mm(o, upper, selM[:, t, :], start=t == 0, stop=True, skip_group_check=True)
            for t in range(NT):
                last = mm(ps[:, A[4] * 512 + NT * NE:A[4] * 512 + (NT + 1) * NE], ones, selM[:, t, :], start=t == 0,
                          stop=t == NT - 1, skip_group_check=True)
            last.then_inc(r_r.h, 1)

            def transpose_rows(src):
                for k in range(KD):
                    last = nc.tensor.transpose(ps[:, A[2] * 512 + k * P:A[2] * 512 + (k + 1) * P],
                                               src[:, k * P:(k + 1) * P], ident)
                return last

            def two_experts(o, lhs, rhs, first, last):
                for x in range(2):
                    r = slice(CAP * x, CAP * (x + 1))
                    ins = mm(o[r], lhs[:, r], rhs[x], start=first, stop=last, skip_group_check=True)
                return ins

            def up_product(b, x_t_, r0):
                for k in range(KD):
                    w = [w13[:, PLACE[r0 + x]].rearrange("p m (k n) -> p m k n", k=KD)[:, :, k, :] for x in range(2)]
                    last = two_experts(bank(b).rearrange("p (m n) -> p m n", m=2), x_t_[:, k * P:(k + 1) * P], w, k == 0, k == KD - 1)
                return last

            def transpose_hidden():
                for k in range(2):
                    last = nc.tensor.transpose(ps[:, A[4] * 512 + k * P:A[4] * 512 + (k + 1) * P], hid[:, k * P:(k + 1) * P], ident)
                return last

            def down_product(r0):
                for c in range(2):
                    for k in range(2):
                        w = [w2[r0 + x][:, k, c * 512:(c + 1) * 512] for x in range(2)]
                        last = two_experts(bank(A[c]), hT[:, k, :], w, k == 0, k == 1)
                return last

            def pair_rows(i, y):
                pe.wait_ge(xg_in[y].h, xg_in[y].at(lay, 16) + i * 16)
                transpose_rows(xg[y]).then_inc(x_t.h, 1)

            def pair(i, y, more):
                pe.wait_ge(x_ca.h, x_ca.at(lay, y + 1) + i * 2)
                pe.wait_ge(x_cd.h, x_cd.at(lay, y + 1) + i * 2)
                for x in range(2):
                    pe.wait_ge(w13_in[2 * y + x].h, w13_in[2 * y + x].at(lay, 32) + i * 32)
                up_product(y, xT[y], 2 * y).then_inc(up.h, 1)
                if more:
                    pair_rows(i + y, 1 - y)
                pe.wait_ge(hd.h, hd.at(lay, y + 1) + i * 2)
                transpose_hidden().then_inc(h_t.h, 1)
                pe.wait_ge(h_c.h, h_c.at(lay, y + 1) + i * 2)
                pe.wait_ge(y_ea.h, y_ea.at(lay, y) + i * 2)
                pe.wait_ge(y_ed.h, y_ed.at(lay, y) + i * 2)
                for x in range(2):
                    pe.wait_ge(w2_in[2 * y + x].h, w2_in[2 * y + x].at(lay, 16) + i * 16)
                down_product(2 * y).then_inc(yd.h, 1)

            pair_rows(0, 0)
            with pe.Fori(0, NP // 2 - 1) as i:
                pair(i, 0, True)
                pair(i, 1, True)
            pair(NP // 2 - 1, 0, True)
            pair(NP // 2 - 1, 1, False)

            def window_item(n, p, col):
                for e in (y_ea, y_ed):
                    hold(pe, e.h, e.at(lay, NP))
                hold(pe, ov_x, n * 16 + 16)
                hold(pe, ov_c, n + 1)
                transpose_rows(xg[0]).then_inc(ov_t, 1)
                hold(pe, ov_w, n * 96 + 96)
                hold(pe, ov_c, n + 2)
                up_product(0, xT[0], 0).then_inc(ov_u, 1)
                hold(pe, ov_h, n + 1)
                transpose_hidden().then_inc(ov_ht, 1)
                hold(pe, ov_hc, n + 1)
                hold(pe, ov_e, n + 1)
                down_product(0).then_inc(ov_y, 1)

            before, own = window_range(pe, lay)
            later_windows(pe, before, own, window_item)

    @block.scalar
    def _(act):
        fn = nc.scalar.activation
        act.wait_ge(s_cst.h, 16 * N_CST)

        with act.Fori(0, L) as lay:
            links = [0]

            def act_link(ins):
                links[0] += 1
                ins.then_inc(act_c.h, 1)
                act.wait_ge(act_c.h, act_c.at(lay, links[0]))

            def split_h(u):
                act.wait_ge(w_in_slot[u % RING].h, w_in_slot[u % RING].at(lay, 16 * (u // RING + 1)))
                n = 1024 if u == 0 else 2048
                fn(ringH[:, u % RING, 0:n], raw[:, u % RING, 0:n], ACT.Copy).then_inc(w_h.h, 1)

            def bank_full(q):
                act.wait_ge(pj.h, pj.at(lay, q + 1))

            def copy_out(q, dst, func=ACT.Copy):
                bank_full(q)
                n = bank(q % 2) if dst.shape[0] == P else ps[0:16, (q % 2) * 512:(q % 2) * 512 + 512]
                fn(dst, n, func).then_inc(pj_free[q % 2].h, 1)

            def squares(n, t, ready, value):
                act.wait_ge(ready.h, value)
                act.wait_ge(n_ss.h, n_ss.at(lay, n))
                fn(junk[:], hs[:, t, :], ACT.Square, accum_out=ss[:, n:n + 1]).then_inc(n_ss.h, 1)

            def norm_h(t):
                act.wait_ge(n_t.h, n_t.at(lay, t + 1))
                b = A[0] if t % 2 == 0 else A[2]
                fn(uH[:, :, tmc(t)], ps[:, b * 512:b * 512 + 1024].rearrange("p (k n) -> p k n", k=KD), ACT.Copy)\
                    .then_inc(n_h.h, 1)

            split_h(0)
            split_h(1)
            for t in range(NT):
                squares(t, t, h_ready, h_ready.at(lay, t + 1))
                if t:
                    norm_h(t - 1)
            norm_h(NT - 1)

            def k2_rows(br):
                act.wait_ge(ktr.h, ktr.at(lay, br + 1))
                fn(k2[:].rearrange("p t n -> p (t n)"), bank(A[4]), ACT.Copy).then_inc(kk2.h, 1)

            def head_squares(br):
                for h in range(HEADS):
                    act.wait_ge(o_m.h, o_m.at(lay, 4 * br + h + 1))
                    fn(on[:, :, h, :], bank(A[h], 256).rearrange("p (t e) -> p t e", t=NT), ACT.Square).then_inc(o_sq.h, 1)

            def out_h(br):
                for hh in range(2):
                    act.wait_ge(o_t.h, o_t.at(lay, 2 * br + hh + 1))
                    fn(oH[:, (0, 6)[br] + hh, :], bank(A[4 + hh]), ACT.Copy).then_inc(o_h.h, 1)

            def step(s):
                if 1 <= s <= NITEMS // 2:
                    n = 2 * s - 2
                    act.wait_ge(sc_t.h, sc_t.at(lay, n + 1))
                    nk = item(n)[4]
                    fn(prT[:, 0, 0:nk * P], bank(A[2], nk * P), ACT.Copy).then_inc(sc_ea.h, 1)
                if s - 2 in (3, 7, 11, 15):
                    m = (s - 2) // 4
                    act.wait_ge(a_o.h, a_o.at(lay, m + 1))
                    fn(oH[:, 2 + m, :], bank(A[4]), ACT.Copy).then_inc(a_h.h, 1)
                if s < NITEMS // 2:
                    for n in (2 * s, 2 * s + 1):
                        win, h, t, k0, nk = item(n)
                        x = n % 2
                        hold(act, sc_b.h, sc_b.at(lay, n + 1))
                        if win:
                            fn(es[:, x:x + 1], sink[:, ds(lay, 1), h:h + 1].rearrange("p a b -> p (a b)"), ACT.Exp,
                               bias=nb[:, x:x + 1])
                        fn(pr[:, x, 0:nk * P], bank(A[x], nk * P), ACT.Exp, bias=nb[:, x:x + 1], scale=HD ** -0.5,
                           accum_out=den[:, x:x + 1]).then_inc(sc_p.h, 1)

            for q in range(NH):
                kind, u, off, name = HALVES[q]
                if q == 0 or HALVES[q - 1][1] != u:
                    split_h(u + 2)
                if q == 0:
                    fn(wa2s[:], wa2[:, ds(lay, 1), :].rearrange("p a n -> p (a n)"), ACT.Copy).then_inc(wa.h, 1)
                    copy_out(q, zaT[:])
                elif name in ("gv", "rv"):
                    copy_out(q, vv[:, 2 * off:2 * off + 2, :].rearrange("p t n -> p (t n)"))
                elif name in ("gr", "rg"):
                    copy_out(q, sr[:, 2 * off:2 * off + 2, :].rearrange("p t n -> p (t n)"), ACT.Silu)
                elif q == 7:
                    bank_full(q)
                    fn(swq[0:HD, 0, :], bank(1)[0:HD], ACT.Copy)
                    fn(swq[0:HD, 1, :], bank(1)[HD:P], ACT.Copy).then_inc(pj_free[1].h, 1)
                elif q == 9:
                    copy_out(q, swk[:])
                elif q == 11:
                    copy_out(q, qT[:])
                elif q == 12:
                    copy_out(q, kT[:])
                elif q == 17:
                    act.wait_ge(h_out.h, h_out.at(lay, 16))
                    copy_out(q, mq[:, 0, :])
                elif q == 19:
                    copy_out(q, mk[:, 0, :])
                elif q == 21:
                    copy_out(q, mv[:, 0:2, :].rearrange("p t n -> p (t n)"))
                if q == 1:
                    hold(act, lgm.h, lgm.at(lay, 1))
                    act_link(fn(lga[:, 0, :], bank(A[0]), ACT.Abs, bias=ba[:, ds(lay, 1)]))
                    act_link(fn(lga[:, 0, :], lga[:, 0, :], ACT.Exp, scale=-1.0))
                    fn(lga[:, 0, :], lga[:, 0, :], ACT.Ln, bias=1.0).then_inc(lg_a.h, 1)
                if q == 2:
                    act.wait_ge(lg_b.h, lg_b.at(lay, 1))
                    fn(qT[:], bT[:], ACT.Exp, scale=1.0 / 16).then_inc(lg_e.h, 1)
                    fn(kT[:], bT[:], ACT.Exp, scale=-1.0 / 16).then_inc(lg_e.h, 1)
                    fn(dec[:], bT[:].rearrange("p (n c) -> p n c", c=CG)[:, :, CG - 1], ACT.Exp, scale=1.0 / 16).then_inc(lg_e.h, 1)
                    act.wait_ge(lg_d.h, lg_d.at(lay, 1))
                    fn(k2T[:], k2T[:], ACT.Exp, scale=1.0 / 16).then_inc(lg_e.h, 1)
                if q in (7, 15):
                    k2_rows(q // 15)
                if q in (10, 18):
                    head_squares(q // 18)
                if q in (12, 20):
                    out_h(q // 20)
                if q >= STEP0:
                    step(q - STEP0)

            def branch(i, steps):
                for j in range(KD):
                    c, b = j // 2, (NH + j) % 2
                    if j % 2 == 0:
                        x = c % 2
                        act.wait_ge(b_in[x].h, b_in[x].at(lay, 16 * (c // 2 + 1)) + i * 32)
                        fn(bH[x][:], braw[x][:], ACT.Copy).then_inc(b_h.h, 1)
                        s = (c + 2) % RING
                        act.wait_ge(w_in_slot[s].h, w_in_slot[s].at(lay, 16 * ((U_GATE + c + 2) // RING + 1)) + i * 16)
                        fn(ringH[:, s, :], raw[:, s, :], ACT.Copy).then_inc(w_h.h, 1)
                    act.wait_ge(pj.h, pj.at(lay, NH + j + 1) + i * 8)
                    if not (isinstance(i, int) and i == 0 and j < 2):
                        act.wait_ge(tm.h, tm.at(lay, j - 1) + i * 8)
                    fn(sig[:, j % 2, :], bank(b), ACT.Sigmoid).then_inc(pj_free[b].h, 1)
                    if steps is not None and j + steps < NITEMS // 2 + 2:
                        step(j + steps)

            branch(0, NH - STEP0)
            branch(1, NH - STEP0 + KD)
            with act.Fori(2, 4) as i:
                branch(i, None)
            act.wait_ge(pj.h, pj.at(lay, NH + 32))
            for k in range(KD):
                act.wait_ge(mg.h, mg.at(lay, 16 + k + 1))
                fn(uH[:, k, :], merged[:, k, :], ACT.Copy).then_inc(m_h.h, 1)
            split_h(U_OUT + 2)
            split_h(U_OUT + 3)

            def norm_2(t):
                act.wait_ge(n_t.h, n_t.at(lay, NT + t + 1))
                b = A[0] if t % 2 == 0 else A[2]
                fn(u2T[:, :, tmc(t)], ps[:, b * 512:b * 512 + 1024].rearrange("p (k n) -> p k n", k=KD), ACT.Copy)\
                    .then_inc(n_h.h, 1)

            for t in range(NT):
                q = NH + 36 + t
                squares(NT + t, t, pj_free[q % 2], pj_free[q % 2].at(lay, q // 2 + 1))
                if t:
                    norm_2(t - 1)
            norm_2(NT - 1)
            act.wait_ge(r_x.h, r_x.at(lay, 1))
            fn(ge[:].rearrange("p t g -> p (t g)"), gd[:].rearrange("p t g -> p (t g)"), ACT.Exp).then_inc(r_e.h, 1)
            act.wait_ge(r_x.h, r_x.at(lay, 2))
            fn(ex[:], dx[:], ACT.Exp).then_inc(r_e.h, 1)

            def rows_copy(i, y):
                act.wait_ge(x_t.h, x_t.at(lay, y + 1) + i * 2)
                fn(xT[y][:, 0:512], bank(A[2]), ACT.Copy).then_inc(x_ca.h, 1)

            def hidden_copy():
                return fn(hT[:].rearrange("p k n -> p (k n)"), bank(A[4], 256), ACT.Copy)

            def pair(i, y, more):
                act.wait_ge(up.h, up.at(lay, y + 1) + i * 2)
                fn(silu[:], bank(y, FH), ACT.Silu).then_inc(sl.h, 1)
                if more:
                    rows_copy(i + y, 1 - y)
                act.wait_ge(h_t.h, h_t.at(lay, y + 1) + i * 2)
                hidden_copy().then_inc(h_c.h, 1)
                act.wait_ge(yd.h, yd.at(lay, y + 1) + i * 2)
                act.wait_ge(y_out[y].h, y_out[y].at(lay, 0) + i * 16)
                fn(ysb[y][:, 512:1024], bank(A[1]), ACT.Copy).then_inc(y_ea.h, 1)

            rows_copy(0, 0)
            with act.Fori(0, NP // 2 - 1) as i:
                pair(i, 0, True)
                pair(i, 1, True)
            pair(NP // 2 - 1, 0, True)
            pair(NP // 2 - 1, 1, False)

            def window_item(n, p, col):
                hold(act, ov_t, n + 1)
                fn(xT[0][:], ps[:, A[2] * 512:A[2] * 512 + 1024], ACT.Copy).then_inc(ov_c, 1)
                hold(act, ov_u, n + 1)
                fn(silu[:], bank(0, FH), ACT.Silu).then_inc(ov_s, 1)
                hold(act, ov_ht, n + 1)
                hidden_copy().then_inc(ov_hc, 1)

            before, own = window_range(act, lay)
            later_windows(act, before, own, window_item)
        for t in range(NT):
            act.wait_ge(h_ready.h, h_ready.at(L, t + 1))
            act.wait_ge(n_ss.h, n_ss.at(L, t))
            fn(junk[:], hs[:, t, :], ACT.Square, accum_out=ss[:, t:t + 1]).then_inc(n_ss.h, 1)

    @block.gpsimd
    def _(pool):
        gp_ = nc.gpsimd
        for s in (up, yb, y_ea, y_ed, n_ss):
            pool.sem_inc(s.h, s.credit)
        for s in (ov_c, ov_y, ov_e):
            pool.sem_inc(s, 1)
        gp_.memset(sent[:], SENT).then_inc(s_init.h, 1)
        gp_.iota(val[:], pattern=[[2 * P, NT], [1, 2]], base=0, channel_multiplier=2).then_inc(s_init.h, 1)
        hold(pool, s_init.h, 3)
        for x, s in enumerate((y_out[0].h, y_out[1].h, ov_o)):
            pool.dma_start(spare_dram[x * P:(x + 1) * P, :], sent[:, 0, 0:1]).then_inc(s, 16)
        hold(pool, s_cst.h, 16 * N_CST)

        with pool.Fori(0, L) as lay:

            def split_l(u):
                n = 1024 if u == 0 else 2048
                s = u % RING
                hold(pool, w_h.h, w_h.at(lay, u + 1))
                gp_.tensor_tensor(ringL[:, s, 0:n], raw[:, s, 0:n], ringH[:, s, 0:n].bitcast(f32), ALU.subtract).then_inc(w_l.h, 1)

            def norm_scale(n):
                hold(pool, n_ms.h, n_ms.at(lay, n + 1))
                gp_.tensor_tensor(rstd[:, n:n + 1], ms[:, n:n + 1], nhalf[:, 0:1], ALU.pow).then_inc(n_rs.h, 1)

            split_l(0)
            split_l(1)
            for t in range(NT):
                norm_scale(t)
            gp_.memset(attT[:].rearrange("p h t i -> p (h t i)"), 0.0).then_inc(att0.h, 1)

            def gain(br):
                q = (4, 16)[br]
                hold(pool, pj_free[0].h, pj_free[0].at(lay, q // 2 + 1))
                hold(pool, pj_free[1].h, pj_free[1].at(lay, q // 2))
                g = ng[:, ds(lay, 1), br, :].rearrange("p a e -> p (a e)").rearrange("p (o e) -> p o e", o=1)
                v = sr[:].rearrange("p t (h e) -> p (t h) e", e=DV)
                gp_.tensor_tensor(v, v, g.broadcast_to([P, 16, DV]), ALU.mult).then_inc(srg.h, 1)

            def head_scale(br):
                hold(pool, o_ms.h, o_ms.at(lay, br + 1))
                gp_.tensor_tensor(hrs[:].rearrange("p h t -> p (h t)"), hms[:], nhalf, ALU.pow).then_inc(o_rs.h, 1)

            for q in range(NH):
                u = HALVES[q][1]
                if q == 0 or HALVES[q - 1][1] != u:
                    split_l(u + 2)
                if q in (4, 16):
                    gain(q // 16)
                if q in (10, 18):
                    head_scale(q // 18)

            def branch(i):
                for j in range(KD):
                    c = j // 2
                    if j % 2 == 0:
                        x, s = c % 2, (c + 2) % RING
                        hold(pool, b_h.h, b_h.at(lay, c + 1) + i * 4)
                        gp_.tensor_tensor(bL[x][:], braw[x][:], bH[x][:].bitcast(f32), ALU.subtract).then_inc(b_l.h, 1)
                        hold(pool, w_h.h, w_h.at(lay, U_GATE + c + 3) + i * 4)
                        gp_.tensor_tensor(ringL[:, s, :], raw[:, s, :], ringH[:, s, :].bitcast(f32), ALU.subtract).then_inc(w_l.h, 1)
                    if not (isinstance(i, int) and i == 0):
                        hold(pool, tm.h, tm.at(lay, j + 1) + i * 8)
                        gp_.tensor_tensor(merged[:, j, :], merged[:, j, :], term[:, j % 2, :], ALU.add).then_inc(mg.h, 1)

            branch(0)
            with pool.Fori(1, 4) as i:
                branch(i)
            split_l(U_OUT + 2)
            split_l(U_OUT + 3)

            for t in range(NT):
                norm_scale(NT + t)
                hold(pool, n_u.h, n_u.at(lay, NT + t + 1))
                pool.dma_start(x_dram[t * P:(t + 1) * P, :], ut[:, t % 2, :]).then_inc(u2o[t % 2].h, 16)

            hold(pool, list0.h, list0.at(lay, 16))
            hold(pool, r_row.h, r_row.at(lay, 1))
            for n in range(8):
                gp_.indirect_dma_start(list_dram, bass.IndirectOffsetOnAxis(row[:, n:n + 1], axis=0), val[:, n:n + 1], None)\
                   .then_inc(l_sc.h, 16)
            hold(pool, l_sc.h, l_sc.at(lay, 16 * 8))
            by_slot = list_dram.rearrange("(x r s e) o -> x s r (e o)", x=2, r=NW, s=CAP)
            for r in (slice(0, 1), slice(1, NW)):
                for x in range(2):
                    pool.dma_start(lists[CAP * x:CAP * (x + 1), r, :], by_slot[x][:, r, :]).then_inc(l_in.h, 16)
            for x in range(2):
                hold(pool, u2o[x].h, u2o[x].at(lay, 32))

            def column(dst, src, i, y):
                p = i * 2 + y
                v = src[:, 0, p:p + 1] if isinstance(p, int) else src[:, 0, ds(p, 1)]
                gp_.tensor_copy(dst[:], v).then_inc(pc.h, 1)

            def gather(i, y):
                if not isinstance(i, int) or i:
                    hold(pool, x_t.h, x_t.at(lay, y - 1) + i * 2)
                    hold(pool, xg_in[y].h, xg_in[y].at(lay, 0) + i * 16)
                column(gi[y], toks, i, y)
                hold(pool, pc.h, pc.at(lay, y + 1) if isinstance(i, int) else pc.at(lay, 2 * y - 1) + i * 4)
                gp_.indirect_dma_start(xg[y][:], None, x_dram, bass.IndirectOffsetOnAxis(gi[y][:, 0:1], axis=0),
                                       bounds_check=S - 1, oob_is_err=False).then_inc(xg_in[y].h, 16)

            def scatter(i, y, copies):
                hold(pool, y_ea.h, y_ea.at(lay, y + 1) + i * 2)
                hold(pool, y_ed.h, y_ed.at(lay, y + 1) + i * 2)
                hold(pool, y_out[y].h, y_out[y].at(lay, 0) + i * 16)
                column(di[y], lists, i, y)
                hold(pool, pc.h, pc.at(lay, copies) + i * 4)
                gp_.indirect_dma_start(y_dram, bass.IndirectOffsetOnAxis(di[y][:, 0:1], axis=0), ysb[y][:], None,
                                       bounds_check=ROWS - 1, oob_is_err=False).then_inc(y_out[y].h, 16)

            hold(pool, l_g.h, l_g.at(lay, 1))
            gather(0, 0)
            gather(0, 1)
            with pool.Fori(0, NP // 2 - 1) as i:
                for y in range(2):
                    gather(i + 1, y)
                    scatter(i, y, 4 + 2 * y)
            scatter(NP // 2 - 1, 0, 3)
            scatter(NP // 2 - 1, 1, 4)

            def window_rows(n, p, col):
                hold(pool, x_t.h, x_t.at(lay, NP))
                hold(pool, xg_in[0].h, xg_in[0].at(lay, 16 * 8))
                hold(pool, y_out[0].h, y_out[0].at(lay, 16 * 8))
                for dst, src in ((gi[0], toks), (di[0], lists)):
                    gp_.tensor_copy(dst[:], src[:].rearrange("p r e -> p (r e)")[:, ds(col, 1)]).then_inc(ov_p, 1)
                hold(pool, ov_p, n * 2 + 2)
                gp_.indirect_dma_start(xg[0][:], None, x_dram, bass.IndirectOffsetOnAxis(gi[0][:, 0:1], axis=0),
                                       bounds_check=S - 1, oob_is_err=False).then_inc(ov_x, 16)
                hold(pool, ov_e, n + 2)
                gp_.indirect_dma_start(y_dram, bass.IndirectOffsetOnAxis(di[0][:, 0:1], axis=0), ysb[0][:], None,
                                       bounds_check=ROWS - 1, oob_is_err=False).then_inc(ov_o, 16)
                hold(pool, ov_o, n * 16 + 32)

            before, own = window_range(pool, lay)
            later_windows(pool, before, own, window_rows)

            for x in range(2):
                hold(pool, y_out[x].h, y_out[x].at(lay, 16 * 8))
            for t in range(NT):
                if t >= 2:
                    hold(pool, h_ready.h, h_ready.at(lay, NT + t - 1))
                pool.dma_start(yl[:, t % 2].rearrange("p k n -> p (k n)"),
                               y_dram[2 * t * P:2 * (t + 1) * P, :].rearrange("(p k) n -> p (k n)", k=2)).then_inc(yl_in[t % 2].h, 16)
        for t in range(NT):
            hold(pool, n_ms.h, n_ms.at(L, t + 1))
            gp_.tensor_tensor(rstd[:, t:t + 1], ms[:, t:t + 1], nhalf[:, 0:1], ALU.pow).then_inc(n_rs.h, 1)

    @block.vector
    def _(dve):
        v = nc.vector
        dve.wait_ge(s_cst.h, 16 * N_CST)
        v.memset(extra[:], 0.0)
        v.memset(windows[:].rearrange("p a b -> p (a b)"), 0)
        v.tensor_scalar(nsink[:], sink[:], -1.0, None, ALU.mult).then_inc(s_init.h, 1)
        dve.wait_ge(s_init.h, 3)
        dve.sem_inc(h_ready.h, NT)

        def norm_rows(lay, n, gain, permute, slot_free=None):
            t = n % NT
            dve.wait_ge(n_rs.h, n_rs.at(lay, n + 1))
            if slot_free is not None:
                slot_free(t)
            o = ut[:, t % 2, :]
            i = hs[:, t, :]
            g = gain[:]
            if permute:
                o = o.rearrange("p (k q) -> p q k", k=KD)
                i = i.rearrange("p (q k) -> p q k", k=KD)
                g = g.rearrange("p (q k) -> p q k", k=KD)
            v.scalar_tensor_tensor(o, i, rstd[:, n:n + 1], g, ALU.mult, ALU.mult).then_inc(n_u.h, 1)

        def mean_square(lay, n):
            dve.wait_ge(n_ss.h, n_ss.at(lay, n + 1))
            v.tensor_scalar(ms[:, n:n + 1], ss[:, n:n + 1], 1.0 / D, EPS, ALU.mult, ALU.add).then_inc(n_ms.h, 1)

        with dve.Fori(0, L) as lay:
            links = [0]

            def link(ins, alone=False):
                links[0] += 1
                ins.then_inc(dve_c.h, 1)
                (hold if alone else wait)(dve, dve_c.h, dve_c.at(lay, links[0]))

            def norm_low(t):
                dve.wait_ge(n_h.h, n_h.at(lay, t + 1))
                b = A[0] if t % 2 == 0 else A[2]
                v.tensor_tensor(uL[:, :, tmc(t)], ps[:, b * 512:b * 512 + 1024].rearrange("p (k n) -> p k n", k=KD),
                                uH[:, :, tmc(t)].bitcast(f32), ALU.subtract).then_inc(n_l.h, 1)

            def ut_transposed(t):
                if t >= 2:
                    dve.wait_ge(n_t.h, n_t.at(lay, t - 1))

            dve.wait_ge(g1_in.h, g1_in.at(lay, 16))
            mean_square(lay, 0)
            for t in range(NT):
                norm_rows(lay, t, g1, False, ut_transposed)
                if t < NT - 1:
                    mean_square(lay, t + 1)
                if t:
                    norm_low(t - 1)
            norm_low(NT - 1)

            def bank_full(q):
                dve.wait_ge(pj.h, pj.at(lay, q + 1))

            def copy_out(q, dst):
                bank_full(q)
                v.tensor_copy(dst, bank(q % 2)).then_inc(pj_free[q % 2].h, 1)

            def log_decay():
                dve.wait_ge(lg_a.h, lg_a.at(lay, 1))
                link(v.tensor_scalar(lga[:, 1, :], bank(A[0]), ba[:, ds(lay, 1)], 0.0, ALU.add, ALU.min))
                link(v.tensor_tensor(lga[:, 1, :], lga[:, 1, :], lga[:, 0, :], ALU.subtract))
                for n in range(S // CG):
                    c = slice(n * CG, (n + 1) * CG)
                    last = v.tensor_tensor_scan(bT[:, c], lga[:, 1, c], lga[:, 1, c], 0.0, ALU.add, ALU.bypass)
                last.then_inc(lg_b.h, 1)
                dve.wait_ge(lg_b.h, lg_b.at(lay, 1))
                b = bT[:].rearrange("p (n c) -> p n c", c=CG)
                v.tensor_tensor(k2T[:].rearrange("p (n c) -> p n c", c=CG), b[:, :, CG - 1:CG].broadcast_to([P, S // CG, CG]), b,
                                ALU.subtract).then_inc(lg_d.h, 1)

            def mask_scores(br):
                if br == 0:
                    dve.wait_ge(att0.h, att0.at(lay, 1))
                for h in range(HEADS):
                    hold(dve, att.h, att.at(lay, 4 * br + h + 1))
                    src = bank(A[h]).rearrange("p (t i) -> p t i", t=NT)
                    if br == 0:
                        m = gmask.bitcast(u32).rearrange("p (o i) -> p o i", o=1).broadcast_to([P, NT, P])
                        v.copy_predicated(attT[:, h, :, :], m, src).then_inc(att_e.h, 1)
                    else:
                        v.tensor_tensor(attT[:, h, :, :], src, decay[:, h:h + 1, :].broadcast_to([P, NT, P]), ALU.mult)\
                            .then_inc(att_e.h, 1)

            def states(br):
                if br == 0:
                    link(v.memset(prev[:, 0, :], 0.0))
                    dve.wait_ge(lg_e.h, lg_e.at(lay, 4))
                dve.wait_ge(kv.h, kv.at(lay, br + 1))
                count = 8 if br == 0 else NT
                for n in range(count - 1):
                    b = A[4] if br == 0 and n % 2 else A[5]
                    ins = v.scalar_tensor_tensor(prev[:, n + 1, :], prev[:, n, :], dec[:, n:n + 1] if br == 0 else cdec,
                                                 ps[:, b * 512 + n * DV:b * 512 + (n + 1) * DV], ALU.mult, ALU.add)
                    if n < count - 2:
                        link(ins)
                    else:
                        ins.then_inc(st.h, 1)

            def head_norm(br):
                for h in range(HEADS):
                    dve.wait_ge(o_sq.h, o_sq.at(lay, 4 * br + h + 1))
                    ins = v.tensor_reduce(hss[:, h, :], on[:, :, h, :], AX.X, ALU.add)
                link(ins)
                v.tensor_scalar(hms[:], hss[:].rearrange("p h t -> p (h t)"), 1.0 / DV, EPS, ALU.mult, ALU.add).then_inc(o_ms.h, 1)
                dve.wait_ge(o_rs.h, o_rs.at(lay, br + 1))
                for h in range(HEADS):
                    r = hrs[:, h, :].rearrange("p (t o) -> p t o", o=1).broadcast_to([P, NT, DV])
                    v.tensor_tensor(on[:, :, h, :], bank(A[h], 256).rearrange("p (t e) -> p t e", t=NT), r, ALU.mult)\
                        .then_inc(o_e.h, 1)
                dve.wait_ge(o_e.h, o_e.at(lay, 4 * br + 4))
                dve.wait_ge(srg.h, srg.at(lay, br + 1))
                o = on[:].rearrange("p t h e -> p (t h e)")
                v.tensor_tensor(o, o, sr[:].rearrange("p t n -> p (t n)"), ALU.mult).then_inc(o_n.h, 1)

            def out_low(br):
                for hh in range(2):
                    dve.wait_ge(o_h.h, o_h.at(lay, 2 * br + hh + 1))
                    k = (0, 6)[br] + hh
                    v.tensor_tensor(oL[:, k, :], bank(A[4 + hh]), oH[:, k, :].bitcast(f32), ALU.subtract).then_inc(o_l.h, 1)

            def rotate():
                dve.wait_ge(tabs_in.h, tabs_in.at(lay, 16))
                dve.wait_ge(rotd.h, rotd.at(lay, 2))
                v.tensor_tensor(bT[:], bank(A[0]), sin, ALU.mult)
                v.tensor_tensor(k2T[:], bank(A[1]), sin, ALU.mult)
                v.tensor_tensor(qT[:], qT[:], cos, ALU.mult)
                link(v.tensor_tensor(kT[:], kT[:], cos, ALU.mult))
                v.tensor_tensor(qT[:], qT[:], bT[:], ALU.add)
                link(v.tensor_tensor(kT[:], kT[:], k2T[:], ALU.add))
                for dst, src, d in ((bT, qT, qdec), (k2T, kT, kdec)):
                    last = v.tensor_tensor(dst[:].rearrange("p (t i) -> p t i", t=NT), src[:].rearrange("p (t i) -> p t i", t=NT),
                                           d.rearrange("p (o i) -> p o i", o=1).broadcast_to([P, NT, P]), ALU.mult)
                last.then_inc(rqk.h, 1)

            def step(s):
                if 1 <= s <= NITEMS // 2:
                    n = 2 * s - 1
                    dve.wait_ge(sc_t.h, sc_t.at(lay, n + 1))
                    nk = item(n)[4]
                    v.tensor_copy(prT[:, 1, 0:nk * P], bank(A[3], nk * P)).then_inc(sc_ed.h, 1)
                if s - 2 in (3, 7, 11, 15):
                    m = (s - 2) // 4
                    dve.wait_ge(a_h.h, a_h.at(lay, m + 1))
                    v.tensor_tensor(oL[:, 2 + m, :], bank(A[4]), oH[:, 2 + m, :].bitcast(f32), ALU.subtract).then_inc(a_l.h, 1)
                if s < NITEMS // 2:
                    pair = (2 * s, 2 * s + 1)
                    for n in pair:
                        win, h, t, k0, nk = item(n)
                        x = n % 2
                        dve.wait_ge(sc.h, sc.at(lay, n + 1))
                        m0 = 0 if win and nk == 2 else nk - 1
                        o = ps[:, A[x] * 512 + m0 * P:A[x] * 512 + nk * P]
                        link(v.tensor_tensor(o, o, wmask[:, 0:256] if m0 < nk - 1 else wmask[:, 128:256], ALU.add))
                        link(v.tensor_reduce(nm[:, x:x + 1], bank(A[x], nk * P), AX.X, ALU.max, negate=True))
                        if win:
                            lim = nsink[:, ds(lay, 1), h:h + 1].rearrange("p a b -> p (a b)")
                            v.tensor_scalar(nb[:, x:x + 1], nm[:, x:x + 1], HD ** -0.5, lim, ALU.mult, ALU.min).then_inc(sc_b.h, 1)
                        else:
                            v.tensor_scalar(nb[:, x:x + 1], nm[:, x:x + 1], HD ** -0.5, None, ALU.mult).then_inc(sc_b.h, 1)
                    for n in pair:
                        win, h, t, k0, nk = item(n)
                        x = n % 2
                        dve.wait_ge(sc_p.h, sc_p.at(lay, n + 1))
                        d = den
                        if win:
                            link(v.tensor_tensor(den2[:, x:x + 1], den[:, x:x + 1], es[:, x:x + 1], ALU.add))
                            d = den2
                        link(v.reciprocal(rden[:, x:x + 1], d[:, x:x + 1]))
                        v.tensor_scalar(pr[:, x, 0:nk * P], pr[:, x, 0:nk * P], rden[:, x:x + 1], None, ALU.mult).then_inc(sc_n.h, 1)

            for q in range(NH):
                name = HALVES[q][3]
                if name == "gq":
                    dve.wait_ge(lg_e.h, lg_e.at(lay, 4))
                    bank_full(q)
                    v.scalar_tensor_tensor(qT[:], bank(q % 2), DK ** -0.5, qT[:], ALU.mult, ALU.mult).then_inc(pj_free[q % 2].h, 1)
                elif name == "gk":
                    bank_full(q)
                    v.tensor_tensor(kT[:], bank(q % 2), kT[:], ALU.mult)
                    v.tensor_tensor(k2T[:], bank(q % 2), k2T[:], ALU.mult).then_inc(pj_free[q % 2].h, 1)
                elif q == 8:
                    bank_full(q)
                    v.tensor_copy(swq[HD:P, 0, :], bank(0)[0:HD])
                    v.tensor_copy(swq[HD:P, 1, :], bank(0)[HD:P]).then_inc(pj_free[0].h, 1)
                elif q == 10:
                    copy_out(q, swv[:].rearrange("p t n -> p (t n)"))
                elif q == 18:
                    dve.wait_ge(h_out.h, h_out.at(lay, 16))
                    copy_out(q, mq[:, 1, :])
                elif q == 20:
                    copy_out(q, mk[:, 1, :])
                elif q == 22:
                    copy_out(q, mv[:, 2:4, :].rearrange("p t n -> p (t n)"))
                if q == 1:
                    log_decay()
                if q in (7, 15):
                    mask_scores(q // 15)
                if q in (8, 16):
                    states(q // 16)
                if q in (10, 18):
                    head_norm(q // 18)
                if q in (12, 20):
                    out_low(q // 20)
                if q == 13:
                    rotate()
                if q >= STEP0:
                    step(q - STEP0)

            def branch(i, steps):
                for j in range(KD):
                    b = (NH + j) % 2
                    if steps is not None and j + steps < NITEMS // 2 + 2:
                        step(j + steps)
                    dve.wait_ge(pj_free[b].h, pj_free[b].at(lay, (NH + j) // 2 + 1) + i * 4)
                    dve.wait_ge(yb.h, yb.at(lay, j + 1) + i * 8)
                    if not (isinstance(i, int) and i == 0):
                        if not (isinstance(i, int) and i == 1 and j < 2):
                            dve.wait_ge(mg.h, mg.at(lay, j - 1 - 8) + i * 8)
                        v.tensor_tensor(term[:, j % 2, :], sig[:, j % 2, :], bank(A[5]), ALU.mult).then_inc(tm.h, 1)
                    else:
                        v.tensor_tensor(merged[:, j, :], sig[:, j % 2, :], bank(A[5]), ALU.mult).then_inc(tm.h, 1)

            branch(0, NH - STEP0)
            branch(1, NH - STEP0 + KD)
            with dve.Fori(2, 4) as i:
                branch(i, None)
            for k in range(KD):
                dve.wait_ge(m_h.h, m_h.at(lay, k + 1))
                v.tensor_tensor(uL[:, k, :], merged[:, k, :], uH[:, k, :].bitcast(f32), ALU.subtract).then_inc(m_l.h, 1)

            dve.wait_ge(h_in.h, h_in.at(lay, 16))
            def residual(c, t):
                q = NH + 32 + 4 * c + t
                bank_full(q)
                o = hs[:, t, c * 512:(c + 1) * 512]
                v.tensor_tensor(o, o, bank(q % 2), ALU.add).then_inc(pj_free[q % 2].h, 1)

            def ut_stored(t):
                if t >= 2:
                    dve.wait_ge(n_t.h, n_t.at(lay, NT + t - 1))
                    dve.wait_ge(u2o[t % 2].h, u2o[t % 2].at(lay, 16))

            for t in range(NT):
                residual(0, t)
            dve.wait_ge(g2_in.h, g2_in.at(lay, 16))
            for t in range(NT):
                residual(1, t)
                mean_square(lay, NT + t)
                norm_rows(lay, NT + t, g2, True, ut_stored)

            dve.wait_ge(rc_in.h, rc_in.at(lay, 48))
            dve.wait_ge(rl.h, rl.at(lay, NT))
            b2 = rb[:, ds(lay, 1), :].broadcast_to([P, NT, NG + NE])
            link(v.tensor_tensor(lg[:], bank(A[5], NT * 36).rearrange("p (t n) -> p t n", t=NT), b2, ALU.add))

            def over(x, n):
                return x.rearrange("p (t o) -> p t o", o=1).broadcast_to([P, NT, n])

            link(v.tensor_reduce(gm[:], lg[:, :, 0:NG], AX.X, ALU.max))
            v.tensor_tensor(gd[:], lg[:, :, 0:NG], over(gm[:], NG), ALU.subtract).then_inc(r_x.h, 1)
            dve.wait_ge(r_x.h, r_x.at(lay, 1))
            link(v.tensor_scalar(geq[:], gd[:], 0.0, None, ALU.is_equal))
            link(v.tensor_tensor(gp[:], geq[:], prio.rearrange("p (o g) -> p o g", o=1).broadcast_to([P, NT, NG]), ALU.mult))
            link(v.tensor_reduce(pm[:], gp[:], AX.X, ALU.max))
            link(v.tensor_tensor(oh[:], gp[:], over(pm[:], NG), ALU.is_equal))
            link(v.tensor_scalar(gidx[:], pm[:], -1.0, float(NG), ALU.mult, ALU.add))
            link(v.tensor_tensor(esel[:], lg[:, :, NG:].rearrange("p t (g e) -> p t g e", g=NG),
                                 oh[:].rearrange("p t (g o) -> p t g o", o=1).broadcast_to([P, NT, NG, EG]), ALU.mult))
            link(v.tensor_reduce(el[:], esel[:].rearrange("p t g e -> p t e g"), AX.X, ALU.add), alone=True)
            for t in range(NT):
                last = v.max(v8[:, t, :], el[:, t, :])
            link(last)
            v.tensor_tensor(dx[:], v8[:, :, 1], v8[:, :, 0], ALU.subtract).then_inc(r_x.h, 1)
            for t in range(NT):
                last = v.max_index(i8[:, t, :], v8[:, t, :], el[:, t, :])
            link(last)
            link(v.tensor_copy(idf[:], i8[:, :, 0:2]))
            link(v.scalar_tensor_tensor(eid[:], over(gidx[:], 2), float(EG), idf[:], ALU.mult, ALU.add))
            link(v.tensor_tensor(sel[:].rearrange("p t c e -> p (t c) e"),
                                 iota32.rearrange("p (o e) -> p o e", o=1).broadcast_to([P, 2 * NT, NE]),
                                 eid[:].rearrange("p t (c o) -> p (t c) o", o=1).broadcast_to([P, 2 * NT, NE]), ALU.is_equal))
            v.tensor_tensor(selM[:], sel[:, :, 0, :], sel[:, :, 1, :], ALU.add).then_inc(r_m.h, 1)
            dve.wait_ge(r_e.h, r_e.at(lay, 1))
            link(v.tensor_reduce(gs[:], ge[:], AX.X, ALU.add))
            link(v.reciprocal(gw[:], gs[:]))
            dve.wait_ge(r_e.h, r_e.at(lay, 2))
            link(v.tensor_scalar(ex1[:], ex[:], 1.0, None, ALU.add))
            link(v.reciprocal(rex[:], ex1[:]))
            link(v.tensor_tensor(wts[:, 0, :], rex[:], gw[:], ALU.mult))
            link(v.tensor_tensor(wts[:, 1, :], wts[:, 0, :], ex[:], ALU.mult))
            link(v.tensor_scalar(second[:], eid[:], float(NP), float(S * NP - NP), ALU.is_ge, ALU.mult))
            link(v.tensor_tensor(slot0[:], second[:], eid[:], ALU.add))
            dve.wait_ge(r_r.h, r_r.at(lay, 1))
            link(v.tensor_tensor(rk[:], sel[:], bank(A[4], P).rearrange("p (t o e) -> p t o e", t=NT, o=1).broadcast_to([P, NT, 2, NE]),
                                 ALU.mult))
            link(v.tensor_reduce(rank[:], rk[:], AX.X, ALU.add))
            v.scalar_tensor_tensor(row[:], rank[:].rearrange("p t c -> p (t c)"), float(NP), slot0[:].rearrange("p t c -> p (t c)"),
                                   ALU.mult, ALU.add).then_inc(r_row.h, 1)
            link(v.tensor_reduce(most[:], bank(A[4], P + NE)[:, P:P + NE], AX.X, ALU.max))
            for x in range(1, NW):
                last = v.tensor_scalar(over_n[:, x - 1:x], most[:], float(x * CAP), None, ALU.is_gt)
            link(last)
            link(v.tensor_reduce(over_n[:, NW - 1:NW], over_n[:, 0:NW - 1], AX.X, ALU.add))
            link(v.tensor_tensor(extra[:, ds(lay + 1, 1)], over_n[:, NW - 1:NW], extra[:, ds(lay, 1)], ALU.add))
            v.tensor_copy(windows[:, 0, ds(lay + 1, 1)], extra[:, ds(lay + 1, 1)])
            v.tensor_copy(windows[:, 1, ds(lay, 1)], over_n[:, NW - 1:NW]).then_inc(win_n.h, 1)
            dve.wait_ge(l_in.h, l_in.at(lay, 16 * 4))
            v.tensor_scalar(toks[:], lists[:], 1, None, ALU.arith_shift_right).then_inc(l_g.h, 1)

            def rows_copy(i, y):
                dve.wait_ge(x_t.h, x_t.at(lay, y + 1) + i * 2)
                v.tensor_copy(xT[y][:, 512:1024], bank(A[3])).then_inc(x_cd.h, 1)

            def pair(i, y, more):
                dve.wait_ge(sl.h, sl.at(lay, y + 1) + i * 2)
                v.tensor_tensor(hid[:], silu[:], bank(y)[:, FH:2 * FH], ALU.mult).then_inc(hd.h, 1)
                if more:
                    rows_copy(i + y, 1 - y)
                dve.wait_ge(yd.h, yd.at(lay, y + 1) + i * 2)
                dve.wait_ge(y_out[y].h, y_out[y].at(lay, 0) + i * 16)
                v.tensor_copy(ysb[y][:, 0:512], bank(A[0])).then_inc(y_ed.h, 1)

            rows_copy(0, 0)
            with dve.Fori(0, NP // 2 - 1) as i:
                pair(i, 0, True)
                pair(i, 1, True)
            pair(NP // 2 - 1, 0, True)
            pair(NP // 2 - 1, 1, False)

            def window_item(n, p, col):
                hold(dve, ov_s, n + 1)
                v.tensor_tensor(hid[:], silu[:], bank(0)[:, FH:2 * FH], ALU.mult).then_inc(ov_h, 1)
                hold(dve, ov_y, n + 2)
                hold(dve, y_out[0].h, y_out[0].at(lay, 16 * 8))
                hold(dve, ov_o, n * 16 + 16)
                v.tensor_copy(ysb[0][:], ps[:, A[0] * 512:A[0] * 512 + 1024]).then_inc(ov_e, 1)

            before, own = window_range(dve, lay)
            later_windows(dve, before, own, window_item)

            for t in range(NT):
                dve.wait_ge(yl_in[t % 2].h, yl_in[t % 2].at(lay, 16 * (t // 2 + 1)))
                link(v.scalar_tensor_tensor(hs[:, t, :], yl[:, t % 2, 0, :], wts[:, 0, t:t + 1], hs[:, t, :], ALU.mult, ALU.add))
                v.scalar_tensor_tensor(hs[:, t, :], yl[:, t % 2, 1, :], wts[:, 1, t:t + 1], hs[:, t, :], ALU.mult, ALU.add)\
                    .then_inc(h_ready.h, 1)
            assert links[0] == DVE_LINKS, links

        dve.wait_ge(g1_in.h, g1_in.at(L, 16))
        for t in range(NT):
            mean_square(L, t)
            dve.wait_ge(n_rs.h, n_rs.at(L, t + 1))
            if t >= 2:
                dve.wait_ge(s_out[t % 2].h, 16)
            v.scalar_tensor_tensor(ut[:, t % 2, :], hs[:, t, :], rstd[:, t:t + 1], g1[:], ALU.mult, ALU.mult).then_inc(fin.h, 1)

    return ctx


def tables():
    f = np.float32
    p = np.arange(P)
    ident = np.eye(P, dtype=f)
    wmask = np.where(np.concatenate([p[None, :] > p[:, None], p[None, :] <= p[:, None]], 1), 0.0, NEG).astype(f)
    gmask = ((p[:, None] <= p[None, :]) & (p[:, None] // CG == p[None, :] // CG)).astype(f)
    log_gamma = np.log1p(-np.exp2(-5.0 - np.arange(HEADS, dtype=np.float64)))
    head = p // DK
    cdec = np.exp(P * log_gamma)[head][:, None]
    small = np.zeros((P, 544), f)
    small[:, 0:128], small[:, 128:384], small[:, 384:512] = ident, wmask, gmask
    small[:, 512:513] = cdec
    small[:, 516:520] = np.arange(NG, 0, -1)
    small[:, 520:536] = -0.5
    half = DK // 2
    d = p % DK
    inv = (f(10000.0) ** (-np.arange(half, dtype=f) * f(2.0) / f(DK))).astype(f)
    ang = (np.arange(S, dtype=f)[None, :] * inv[d % half][:, None]).astype(f)
    rot = np.zeros((P, P), f)
    for m in range(P):
        if d[m] < half:
            rot[m + half, m] = -1.0
        else:
            rot[m - half, m] = 1.0
    idx = np.arange(P, dtype=np.float64)
    rel = idx[None, :] - idx[:, None]
    sc = DK ** -0.5
    dm = np.where(rel[:, None, :] >= 0, np.exp(np.maximum(rel, 0)[:, None, :] * log_gamma[None, :, None]), 0.0) * sc
    qd = np.exp((idx + 1)[None, :] * log_gamma[head][:, None])
    kd = np.exp((P - 1 - idx)[None, :] * log_gamma[head][:, None]) * sc
    tabs = np.concatenate([np.cos(ang.astype(np.float64)), np.sin(ang.astype(np.float64)), dm.reshape(P, -1), qd, kd, rot], 1).astype(f)
    router = np.concatenate([(p[:, None] < p[None, :]), np.ones((P, P)), np.tile(np.arange(NE), (P, 1))], 1).astype(f)
    return {"c_small": small, "c_tabs": tabs, "c_router": router}


def kernel(**inputs):
    import concourse.bacc as bacc
    from concourse.bass_utils import run_bass_kernel_spmd

    nc = bacc.Bacc("TRN2", target_bir_lowering=False, num_devices=1)
    host = {k: np.ascontiguousarray(x) for k, x in inputs.items()}
    host["c_next_gain"] = np.concatenate([host["ln1_g"][1:], host.pop("final_g")[None]], 0)
    host.update(tables())
    arrays, a = {}, {}
    for k, x in host.items():
        arrays[f"in_{k}"] = x
        a[k] = nc.dram_tensor(f"in_{k}", x.shape, mybir.dt.from_np(x.dtype), kind="ExternalInput").ap()
    out = nc.dram_tensor("out", (1, S, D), mybir.dt.float32, kind="ExternalOutput").ap()
    trunk(nc, a, out).close()
    r = run_bass_kernel_spmd(nc, [arrays], core_ids=[0])
    return r.results[0]["out"]
```

```python
import concourse.bass as bass
from concourse import mybir
from contextlib import ExitStack
import numpy as np

L, D, S, P = 2, 1024, 512, 128
NT, KD = S // P, D // P
HEADS, DK, DV, HD, CG = 4, 32, 64, 64, 64
NE, NG, EG, FH = 32, 4, 8, 256
NP = NE // 2
CAP, NW = 64, 8
SUMS = 8 * (NP // 2)
WIN = 6928
EPS = 1e-6
NEG = -1.0e30
COL = {"gq": 0, "gk": 128, "gv": 256, "gr": 512, "ga": 768, "sq": 784, "sk": 1040, "sv": 1168,
       "mq": 1296, "mk": 1552, "mv": 1808, "rq": 2064, "rk": 2192, "rv": 2320, "rg": 2576, "gate": 2832}
UNITS = [("gv", 256), ("ga", 128), ("gr", 256), ("gq", 256), ("sq", 256), ("sk", 256), ("rq", 256),
         ("rv", 256), ("rg", 256), ("mq", 256), ("mk", 256), ("mv", 256)]
U_GATE, U_OUT, U_ALL = 12, 28, 32
RING = 4
PLACE = (0, 2, 1, 3)
HALVES = [("R", 0, 0, "gv"), ("R", 0, 1, "gv"), ("T", 1, 0, "ga"), ("R", 2, 0, "gr"), ("R", 2, 1, "gr"),
          ("T", 3, 0, "gq"), ("T", 3, 128, "gk"), ("T", 4, 0, "sq"), ("T", 4, 128, "sq"), ("T", 5, 0, "sk"),
          ("T", 5, 128, "sv"), ("T", 6, 0, "rq"), ("T", 6, 128, "rk"), ("R", 7, 0, "rv"), ("R", 7, 1, "rv"),
          ("R", 8, 0, "rg"), ("R", 8, 1, "rg"), ("T", 9, 0, "mq"), ("T", 9, 128, "mq"), ("T", 10, 0, "mk"),
          ("T", 10, 128, "mk"), ("R", 11, 0, "mv"), ("R", 11, 1, "mv")]
NH = len(HALVES)
N_CST = NT + 8
NITEMS = 2 * HEADS * NT
STEP0 = 20
SENT = 1 << 20


class Sig:

    def __init__(self, handle, per_layer, credit=0):
        self.h, self.k, self.credit = handle, per_layer, credit

    def at(self, lay, n):
        return lay * self.k + (n + self.credit)


def used_at(u):
    if u < U_GATE:
        return max(2 * u + 1, 2)
    return NH + 2 * (u - U_GATE + 1) if u < U_OUT else NH + 32 + (4 if u < U_OUT + 2 else 8)


def item(n):
    win, h, t = n < NITEMS // 2, n % 16 // 8 * 2 + n % 2, n % 8 // 2
    k0 = max(t - 1, 0) if win else 0
    return win, h, t, k0, t + 1 - k0


def trunk(nc, a, out):
    f32, f32r, i32, u32 = mybir.dt.float32, mybir.dt.float32r, mybir.dt.int32, mybir.dt.uint32
    ALU, ACT, AX = mybir.AluOpType, mybir.ActivationFunctionType, mybir.AxisListType
    ds = bass.ds
    ctx = ExitStack()
    KB = 1024
    BASE = -(-nc.sbuf_base // 64) * 64

    def sb(name, shape, dt, off):
        return nc.alloc_sbuf_tensor_at(name, shape, dt, offset=BASE + int(off))

    h_dram = nc.dram_tensor("h_dram", (S, D), f32, kind="Internal").ap()
    x_dram = nc.dram_tensor("x_dram", (S, D), f32, kind="Internal").ap()

    R_U, R_RAW, R_RH, R_B, R_O, R_T1, R_T2, R_C = (x * KB for x in (0, 32, 64, 96, 112, 144, 176, 198))
    uH = sb("uH", [P, KD, S], f32r, R_U)
    uL = sb("uL", [P, KD, S], f32r, R_U + 16 * KB)
    raw = sb("raw", [P, RING, 2048], f32, R_RAW)
    ringL = sb("ringL", [P, RING, 2048], f32r, R_RAW)
    ringH = sb("ringH", [P, RING, 2048], f32r, R_RH)
    swq = sb("swq", [P, 2, S], f32, R_B)
    swk = sb("swk", [P, S], f32, R_B + 4 * KB)
    swv = sb("swv", [P, NT, P], f32, R_B + 6 * KB)
    tabs = sb("tabs", [P, 1920], f32, R_B + 8 * KB)
    cos, sin = tabs[:, 0:512], tabs[:, 512:1024]
    decay = tabs[:, 1024:1536].rearrange("p (h i) -> p h i", h=HEADS)
    qdec, kdec, rot = tabs[:, 1536:1664], tabs[:, 1664:1792], tabs[:, 1792:1920]
    w13 = sb("w13", [P, 4, 2, 2048], f32, R_RAW)
    w2 = [sb(f"w2_{x}", [P, 2, D], f32, off) for x, off in
          enumerate((R_B, R_B + 8 * KB, R_T1, R_T1 + 8 * KB))]
    oH = sb("oH", [P, 8, S], f32r, R_O)
    oL = sb("oL", [P, 8, S], f32r, R_O + 16 * KB)
    u2T = sb("u2T", [P, KD, S], f32, R_O)
    ut = sb("ut", [P, 2, D], f32, R_O + 16 * KB)
    junk = sb("junk", [P, D], f32, R_O + 24 * KB)
    qT = sb("qT", [P, S], f32, R_T1)
    kT = sb("kT", [P, S], f32, R_T1 + 2 * KB)
    k2T = sb("k2T", [P, S], f32, R_T1 + 4 * KB)
    bT = sb("bT", [P, S], f32, R_T1 + 6 * KB)
    k2 = sb("k2", [P, NT, P], f32, R_T1 + 8 * KB)
    vv = sb("vv", [P, NT, 256], f32, R_T1 + 10 * KB)
    zaT = sb("zaT", [16, S], f32, R_T1 + 6 * KB)
    sr = sb("sr", [P, NT, 256], f32, R_T1 + 14 * KB)
    attT = sb("attT", [P, HEADS, NT, P], f32, R_T1 + 18 * KB)
    prev = sb("prev", [P, 8, DV], f32, R_T1 + 26 * KB)
    on = sb("on", [P, NT, HEADS, DV], f32, R_T1 + 28 * KB)
    lga = sb("lga", [P, 2, S], f32, R_T1 + 28 * KB)
    g1 = sb("g1", [P, D], f32, R_T1 + 28 * KB)
    g2 = sb("g2", [P, D], f32, R_T1 + 24 * KB)
    merged = sb("merged", [P, KD, S], f32, R_T1)
    sig = sb("sig", [P, 2, S], f32, R_T1 + 16 * KB)
    term = sb("term", [P, 2, S], f32, R_T1 + 20 * KB)
    braw = [sb(f"braw{x}", [P, 512], f32, R_T1 + (24 + 4 * x) * KB) for x in range(2)]
    bL = [sb(f"bL{x}", [P, 512], f32r, R_T1 + (24 + 4 * x) * KB) for x in range(2)]
    bH = [sb(f"bH{x}", [P, 512], f32r, R_T1 + (26 + 4 * x) * KB) for x in range(2)]
    mq = sb("mq", [P, 2, S], f32, R_T2)
    mk = sb("mk", [P, 2, S], f32, R_T2 + 4 * KB)
    mv = sb("mv", [P, NT, 256], f32, R_T2 + 8 * KB)
    pr = sb("pr", [P, 2, S], f32, R_T2 + 12 * KB)
    prT = sb("prT", [P, 2, S], f32, R_T2 + 16 * KB)
    svT = prT[:, 0, :]
    hs = sb("hs", [P, NT, D], f32, R_T2)
    rc = sb("rc", [P, 776], f32, R_T2 + 16 * KB)
    upper, ones, iota, val = rc[:, 0:128], rc[:, 128:256], rc[:, 256:768], rc[:, 768:776]
    wr = sb("wr", [P, KD, NG + NE], f32, R_T2 + 19.5 * KB)
    xg = [sb(f"xg{x}", [P, D], f32, R_U + 4 * x * KB) for x in range(2)]
    xT = [sb(f"xT{x}", [P, D], f32, R_U + (8 + 4 * x) * KB) for x in range(2)]
    yH = [sb(f"yH{x}", [P, D], f32r, off) for x, off in enumerate((R_U + 16 * KB, R_O + 12 * KB))]
    yL = [sb(f"yL{x}", [P, D], f32r, off) for x, off in enumerate((R_U + 20 * KB, R_U + 28 * KB))]
    silu = sb("silu", [P, FH], f32, R_U + 24 * KB)
    hid = sb("hid", [P, FH], f32, R_U + 25 * KB)
    hT = sb("hT", [P, 2, P], f32, R_U + 26 * KB)
    tok_of = [sb(f"tok_of{x}", [P, S], f32r, R_O + 2 * x * KB) for x in range(2)]
    tok_w = sb("tok_w", [P, S], f32r, R_T2 + 19.5 * KB)
    yHw = sb("yHw", [P, D], f32r, R_O + 4 * KB)
    yLw = sb("yLw", [P, D], f32r, R_O + 8 * KB)
    slot_of = sb("slot_of", [P, 8, P], f32, R_O + 28 * KB)
    at = [R_C]

    def small(name, shape, dt=f32):
        n = int(np.prod(shape[1:])) * 4
        t = sb(name, shape, dt, at[0])
        at[0] += -(-n // 32) * 32
        return t

    cst = small("cst", [P, 544])
    ident, wmask, gmask = cst[:, 0:128], cst[:, 128:384], cst[:, 384:512]
    cdec, prio, nhalf = cst[:, 512:513], cst[:, 516:520], cst[:, 520:536]
    wa2 = small("wa2", [16, L, P])
    wa2s = small("wa2s", [16, P])
    ba = small("ba", [P, L])
    ng = small("ng", [P, L, 2, DV])
    sink = small("sink", [P, L, HEADS])
    nsink = small("nsink", [P, L, HEADS])
    rb = small("rb", [P, L, NG + NE])
    ss = small("ss", [P, 8]); ms = small("ms", [P, 8]); rstd = small("rstd", [P, 8])
    hss = small("hss", [P, HEADS, NT]); hms = small("hms", [P, 16]); hrs = small("hrs", [P, HEADS, NT])
    dec = small("dec", [P, 8])
    nm = small("nm", [P, 2]); nb = small("nb", [P, 2]); es = small("es", [P, 2]); den = small("den", [P, 2])
    den2 = small("den2", [P, 2]); rden = small("rden", [P, 2])
    lists = small("lists", [P, NP]); toks = small("toks", [P, NP], i32); tokf = small("tokf", [P, NP])
    slot_w = small("slot_w", [P, NP]); empty = small("empty", [P, NP])
    gi = [small(f"gi{x}", [P, 1], i32) for x in range(2)]
    wts = small("wts", [P, NT, 2])
    extra = small("extra", [P, L + 1])
    windows = small("windows", [P, 2, L + 1], i32)
    most = small("most", [P, 1]); over_n = small("over_n", [P, NW])
    rt = [R_T1 + 16 * KB]

    def rtmp(name, shape, dt=f32):
        n = int(np.prod(shape[1:])) * 4
        t = sb(name, shape, dt, rt[0])
        rt[0] += -(-n // 32) * 32
        return t

    lg = rtmp("lg", [P, NT, NG + NE])
    gm = rtmp("gm", [P, NT]); gd = rtmp("gd", [P, NT, NG]); ge = rtmp("ge", [P, NT, NG])
    gs = rtmp("gs", [P, NT]); gw = rtmp("gw", [P, NT]); geq = rtmp("geq", [P, NT, NG])
    gp = rtmp("gp", [P, NT, NG]); pm = rtmp("pm", [P, NT]); oh = rtmp("oh", [P, NT, NG])
    gidx = rtmp("gidx", [P, NT]); esel = rtmp("esel", [P, NT, NG, EG]); el = rtmp("el", [P, NT, EG])
    v8 = rtmp("v8", [P, NT, 8]); i8 = rtmp("i8", [P, NT, 8], u32); dx = rtmp("dx", [P, NT])
    ex = rtmp("ex", [P, NT]); ex1 = rtmp("ex1", [P, NT]); rex = rtmp("rex", [P, NT])
    idf = rtmp("idf", [P, NT, 2]); eid = rtmp("eid", [P, NT, 2])
    x64 = rtmp("x64", [P, 8]); out_of = rtmp("out_of", [P, 8]); below = rtmp("below", [P, 8]); slot = rtmp("slot", [P, 8])
    pair_of = rtmp("pair_of", [P, 8, NP]); tok_rhs = rtmp("tok_rhs", [P, 8, 2, NP]); w_rhs = rtmp("w_rhs", [P, 8, NP])
    count = rtmp("count", [P, NT + 1, NE])
    sel = rtmp("sel", [P, NT, 2, NE]); selM = rtmp("selM", [P, NT, NE])
    rk = rtmp("rk", [P, NT, 2, NE]); rank = rtmp("rank", [P, 8])
    assert rt[0] <= R_T1 + 28 * KB and BASE + at[0] <= nc.sbuf_usable_end, (at[0], rt[0])

    ps = ctx.enter_context(nc.psum_tensor("ps", [P, 8 * 512], f32))

    def bank(b, n=512):
        return ps[:, b * 512:b * 512 + n]

    A = [2, 3, 4, 5, 6, 7]

    def signal(name, per_layer, credit=0):
        return Sig(ctx.enter_context(nc.semaphore(name)), per_layer, credit)

    s_cst = signal("s_cst", 0)
    s_init = signal("s_init", 0)
    w_in_slot = [signal(f"w_in_slot{s}", 16 * 8) for s in range(RING)]
    w_h = signal("w_h", U_ALL)
    w_l = signal("w_l", U_ALL)
    b_in = [signal(f"b_in{x}", 16 * 8) for x in range(2)]
    b_h = signal("b_h", 16)
    b_l = signal("b_l", 16)
    w13_in = [signal(f"w13_in{x}", 32 * 8) for x in range(4)]
    w2_in = [signal(f"w2_in{x}", 16 * 8) for x in range(4)]
    tabs_in = signal("tabs_in", 16)
    g1_in = signal("g1_in", 16)
    g2_in = signal("g2_in", 16)
    rc_in = signal("rc_in", 16 * 3)
    h_out = signal("h_out", 16)
    h_in = signal("h_in", 16)
    n_ss = signal("n_ss", 8, 1); n_ms = signal("n_ms", 8); n_rs = signal("n_rs", 8); n_u = signal("n_u", 8)
    n_t = signal("n_t", 8); n_h = signal("n_h", 8); n_l = signal("n_l", 4)
    pj = signal("pj", NH + 40)
    NB0, NB1 = (NH + 1) // 2, NH // 2
    pj_free = [signal("pj_free0", NB0 + 20), signal("pj_free1", NB1 + 20)]
    sv_t = signal("sv_t", 1); sv_c = signal("sv_c", 1)
    wa = signal("wa", 1)
    lgm = signal("lgm", 1)
    lg_a = signal("lg_a", 1); lg_b = signal("lg_b", 1); lg_d = signal("lg_d", 1); lg_e = signal("lg_e", 4)
    rotd = signal("rotd", 2); rqk = signal("rqk", 1)
    att0 = signal("att0", 1)
    att = signal("att", 8); att_e = signal("att_e", 8)
    ktr = signal("ktr", 2); kk2 = signal("kk2", 2); kv = signal("kv", 2); st = signal("st", 2)
    srg = signal("srg", 2)
    o_m = signal("o_m", 8); o_sq = signal("o_sq", 8); o_ms = signal("o_ms", 2); o_rs = signal("o_rs", 2)
    o_e = signal("o_e", 8); o_n = signal("o_n", 2); o_t = signal("o_t", 4); o_h = signal("o_h", 4)
    o_l = signal("o_l", 4)
    sc = signal("sc", NITEMS); sc_b = signal("sc_b", NITEMS); sc_p = signal("sc_p", NITEMS)
    sc_n = signal("sc_n", NITEMS); sc_t = signal("sc_t", NITEMS)
    sc_ea = signal("sc_ea", NITEMS // 2); sc_ed = signal("sc_ed", NITEMS // 2)
    a_o = signal("a_o", 4); a_h = signal("a_h", 4); a_l = signal("a_l", 4)
    yb = signal("yb", 32, 4); tm = signal("tm", 32)
    mg = signal("mg", 24)
    m_h = signal("m_h", 8); m_l = signal("m_l", 8)
    u2o = [signal(f"u2o{x}", 16 * 2) for x in range(2)]
    rl = signal("rl", NT)
    r_e = signal("r_e", 2); r_x = signal("r_x", 2); r_m = signal("r_m", 1); r_r = signal("r_r", 1)
    l_a = signal("l_a", 1); l_p = signal("l_p", 1); l_b = signal("l_b", 1); l_q = signal("l_q", 1)
    xz = signal("xz", 2); l_g = signal("l_g", 1)
    xg_in = [signal(f"xg_in{x}", 16 * 8) for x in range(2)]
    x_t = signal("x_t", NP); x_ca = signal("x_ca", NP); x_cd = signal("x_cd", NP)
    up = signal("up", NP, 2); sl = signal("sl", NP); hd = signal("hd", NP); h_t = signal("h_t", NP)
    h_c = signal("h_c", NP); yd = signal("yd", NP)
    y_h = signal("y_h", NP); y_l = signal("y_l", NP); t_of = signal("t_of", NP)
    cm = signal("cm", SUMS); ca = signal("ca", SUMS, 10)
    win_n = signal("win_n", 1)
    ov_w, ov_x, ov_t, ov_c, ov_u, ov_s, ov_h, ov_ht, ov_hc, ov_y, ov_p = (
        ctx.enter_context(nc.semaphore(f"ov_{x}")) for x in
        ("weights", "rows", "transposed", "columns", "up", "silu", "hidden", "hidden_t", "hidden_c", "down", "index"))
    ov_yh, ov_yl, ov_of, ov_cm, ov_ca = (ctx.enter_context(nc.semaphore(f"ov_{x}")) for x in
                                         ("out_h", "out_l", "tokens", "product", "added"))
    ov_la, ov_lp, ov_lg, ov_link = (ctx.enter_context(nc.semaphore(f"ov_{x}")) for x in
                                    ("slots", "lists_product", "lists", "link"))
    s_out = [signal(f"s_out{x}", 0) for x in range(2)]
    fin = signal("fin", 0)
    tmc = lambda t: slice(t * P, (t + 1) * P)

    block = ctx.enter_context(nc.Block())
    DVE_LINKS, ACT_LINKS, WIN_LINKS = 165, 2, 9
    dve_c = signal("dve_c", DVE_LINKS)
    act_c = signal("act_c", ACT_LINKS)
    pc = signal("pc", NP)

    def w_in_cols(l, c0, n):
        return a["w_in"][ds(l, 1), :, c0:c0 + n].rearrange("o (k p) n -> p (o k) n", p=P)

    held = ctx.enter_context(nc.semaphore("held"))

    def wait(eng, s, value):
        eng.wait_ge(s, value)

    def hold(eng, s, value):
        eng.wait_ge(s, value).then_inc(held, 1)

    def window_range(eng, lay):
        hold(eng, win_n.h, win_n.at(lay, 1))
        return (eng.value_load(windows[0:1, 0, ds(lay, 1)], min_val=0, max_val=(NW - 1) * L),
                eng.value_load(windows[0:1, 1, ds(lay, 1)], min_val=0, max_val=NW - 1))

    def later_windows(eng, before, own, lists_, item_):
        with eng.If(own):
            with eng.Fori(0, own) as w:
                if lists_ is not None:
                    lists_(before + w)
                with eng.Fori(0, NP) as p:
                    item_((before + w) * NP + p, p)

    @block.sync
    def _(sp):
        for t in range(NT):
            sp.dma_start(hs[:, t, :], a["x"][0, t * P:(t + 1) * P, :]).then_inc(s_cst.h, 16)
        for dst, src in ((cst[:], a["c_small"]), (wa2[:], a["gla_w_a2"].rearrange("l r n -> r l n")),
                         (ba[:], a["gla_b_a"].rearrange("l n -> n l")),
                         (ng[:, :, 0, :], a["gla_norm_g"].partition_broadcast(P)),
                         (ng[:, :, 1, :], a["ret_norm_g"].partition_broadcast(P)),
                         (sink[:], a["swa_sinks"].partition_broadcast(P)),
                         (rb[:, :, 0:NG], a["b_group"].partition_broadcast(P)),
                         (rb[:, :, NG:], a["b_expert"].partition_broadcast(P))):
            sp.dma_start(dst, src, allow_slow_non_contiguous=True).then_inc(s_cst.h, 16)
        sp.dma_start(g1[:], a["ln1_g"][0:1, :].partition_broadcast(P)).then_inc(g1_in.h, 16)
        with sp.Fori(0, L) as lay:

            def fill(u, src, dst=None):
                if u < RING:
                    hold(sp, up.h, up.at(lay, u // 2 - 1))
                else:
                    hold(sp, pj.h, pj.at(lay, used_at(u - RING)))
                sp.dma_start(dst, src).then_inc(w_in_slot[u % RING].h, 16)

            for u, (name, n) in enumerate(UNITS):
                slot = raw[:, u % RING, 0:KD * n].rearrange("p (k n) -> p k n", k=KD)
                fill(u, w_in_cols(lay, COL[name], n), slot)
                if u == 3:
                    hold(sp, s_cst.h, 16 * N_CST)
                    hold(sp, ca.h, ca.at(lay, 0))
                    sp.dma_start(h_dram.rearrange("(t p) n -> p t n", p=P), hs[:]).then_inc(h_out.h, 16)
                if u == 4:
                    sp.dma_start(tabs[:], a["c_tabs"]).then_inc(tabs_in.h, 16)

            def gate_fill(g, u):
                slot = raw[:, u % RING, :].rearrange("p (k n) -> p k n", k=KD)
                hold(sp, pj.h, pj.at(lay, used_at(u - RING)) if isinstance(g, int) else pj.at(lay, NH - 2 * (RING - 1)) + g * 2)
                src = a["w_in"][ds(lay, 1), :, ds(g * 256 + COL["gate"], 256)].rearrange("o (k p) n -> p (o k) n", p=P)
                sp.dma_start(slot, src).then_inc(w_in_slot[u % RING].h, 16)

            def bfill(i, c):
                hold(sp, yb.h, yb.at(lay, 2 * c - 2) + i * 8)
                src = a["w_branch"][ds(lay, 1), ds(i, 1), :, c * 256:(c + 1) * 256].rearrange("o q (k p) n -> p (o q k) n", p=P)
                sp.dma_start(braw[c % 2][:].rearrange("p (k n) -> p k n", k=2), src).then_inc(b_in[c % 2].h, 16)

            def out_fill(u):
                slot = raw[:, u % RING, :].rearrange("p (k n) -> p k n", k=KD)
                c0 = (u - U_OUT) * 256
                fill(u, a["w_out"][ds(lay, 1), :, c0:c0 + 256].rearrange("o (k p) n -> p (o k) n", p=P), slot)

            gate_fill(0, U_GATE)
            gate_fill(1, U_GATE + 1)
            for c in range(4):
                gate_fill(c + 2, U_GATE + c + 2)
                bfill(0, c)
            with sp.Fori(1, 3) as i:
                for c in range(4):
                    gate_fill(i * 4 + (c + 2), U_GATE + c + 2)
                    bfill(i, c)
            hold(sp, a_l.h, a_l.at(lay, 2))

            def w2_fill(i, r):
                src = a["w2"][ds(lay, 1), ds(i * 2 + (r // 2 + NP * (r % 2)), 1)].rearrange("o q (k p) n -> p (o q k) n", p=P)
                sp.dma_start(w2[r][:], src).then_inc(w2_in[r].h, 16)

            def w13_fill(i, r):
                for m, name in enumerate(("w1", "w3")):
                    src = a[name][ds(lay, 1), ds(i * 2 + (r // 2 + NP * (r % 2)), 1)].rearrange("o q (p k) n -> p (o q k n)", k=KD)
                    sp.dma_start(w13[:, PLACE[r], m, :], src).then_inc(w13_in[r].h, 16)

            w2_fill(0, 0)
            w2_fill(0, 1)
            for c in range(4):
                if c < 2:
                    gate_fill(14 + c, U_GATE + 14 + c)
                else:
                    out_fill(U_OUT + c - 2)
                bfill(3, c)
            out_fill(U_OUT + 2)
            sp.dma_start(hs[:], h_dram.rearrange("(t p) n -> p t n", p=P)).then_inc(h_in.h, 16)
            sp.dma_start(rc[:], a["c_router"]).then_inc(rc_in.h, 16)
            sp.dma_start(wr[:, :, 0:NG], a["w_group"][ds(lay, 1)].rearrange("o (p k) n -> p (o k) n", k=KD)).then_inc(rc_in.h, 16)
            sp.dma_start(wr[:, :, NG:], a["w_expert"][ds(lay, 1)].rearrange("o (p k) n -> p (o k) n", k=KD)).then_inc(rc_in.h, 16)
            out_fill(U_OUT + 3)
            hold(sp, yb.h, yb.at(lay, 32))
            sp.dma_start(g2[:], a["ln2_g"][ds(lay, 1), :].partition_broadcast(P)).then_inc(g2_in.h, 16)

            hold(sp, pj.h, pj.at(lay, used_at(U_OUT + 1)))
            w13_fill(0, 0)
            w13_fill(0, 1)
            hold(sp, m_l.h, m_l.at(lay, KD))
            w2_fill(0, 2)
            w2_fill(0, 3)
            hold(sp, pj.h, pj.at(lay, used_at(U_OUT + 3)))
            w13_fill(0, 2)
            w13_fill(0, 3)
            with sp.Fori(1, NP // 2) as i:
                for y in range(2):
                    hold(sp, up.h, up.at(lay, y - 1) + i * 2)
                    w13_fill(i, 2 * y)
                    w13_fill(i, 2 * y + 1)
                    hold(sp, yd.h, yd.at(lay, y - 1) + i * 2)
                    w2_fill(i, 2 * y)
                    w2_fill(i, 2 * y + 1)

            def window_weights(n, p):
                hold(sp, yd.h, yd.at(lay, NP))
                hold(sp, ov_y, n + 1)
                for x in range(2):
                    for m, name in enumerate(("w1", "w3")):
                        src = a[name][ds(lay, 1), ds(p + NP * x, 1)].rearrange("o q (p k) n -> p (o q k n)", k=KD)
                        sp.dma_start(w13[:, PLACE[x], m, :], src).then_inc(ov_w, 16)
                    src = a["w2"][ds(lay, 1), ds(p + NP * x, 1)].rearrange("o q (k p) n -> p (o q k) n", p=P)
                    sp.dma_start(w2[x][:], src).then_inc(ov_w, 16)

            before, own = window_range(sp, lay)
            later_windows(sp, before, own, None, window_weights)
            hold(sp, ov_y, (before + own) * NP + 1)
            hold(sp, n_u.h, n_u.at(lay, 8))
            sp.dma_start(g1[:], a["c_next_gain"][ds(lay, 1), :].partition_broadcast(P)).then_inc(g1_in.h, 16)
        hold(sp, h_out.h, 16 * L)
        for t in range(NT):
            hold(sp, fin.h, t + 1)
            sp.dma_start(out[0, t * P:(t + 1) * P, :], ut[:, t % 2, :]).then_inc(s_out[t % 2].h, 16)
        for x in range(2):
            hold(sp, s_out[x].h, 16 * NT // 2)


    @block.tensor
    def _(pe):
        mm = nc.tensor.matmul

        def mm3(o, h, l, rh, rl_, first, last):
            mm(o, h, rh, start=first, stop=False)
            mm(o, h, rl_, start=False, stop=False)
            return mm(o, l, rh, start=False, stop=last)

        pe.wait_ge(s_cst.h, 16 * N_CST)
        with pe.Fori(0, L) as lay:

            def norm_transposes(n, dst_free):
                t = n % NT
                b = A[0] if t % 2 == 0 else A[2]
                pe.wait_ge(n_u.h, n_u.at(lay, n + 1))
                if t >= 2:
                    pe.wait_ge(dst_free.h, dst_free.at(lay, n - 1))
                for k in range(KD):
                    last = nc.tensor.transpose(ps[:, b * 512 + k * P:b * 512 + (k + 1) * P],
                                               ut[:, t % 2, k * P:(k + 1) * P], ident)
                last.then_inc(n_t.h, 1)

            norm_transposes(0, n_l)
            norm_transposes(1, n_l)

            def half(q):
                kind, u, off, name = HALVES[q]
                s, b = u % RING, q % 2
                n = UNITS[u][1]
                wH = ringH[:, s, 0:KD * n].rearrange("p (k n) -> p k n", k=KD)
                wL = ringL[:, s, 0:KD * n].rearrange("p (k n) -> p k n", k=KD)
                pe.wait_ge(w_l.h, w_l.at(lay, u + 1))
                if q >= 2:
                    pe.wait_ge(pj_free[b].h, pj_free[b].at(lay, q // 2))
                if kind == "T":
                    for k in range(KD):
                        last = mm3(bank(b), wH[:, k, off:off + P], wL[:, k, off:off + P], uH[:, k, :], uL[:, k, :],
                                   k == 0, k == KD - 1)
                else:
                    for i in range(2):
                        if q < 2:
                            if 1 <= 2 * q + i < NT - 1:
                                norm_transposes(2 * q + i + 1, n_l)
                            hold(pe, n_l.h, n_l.at(lay, 2 * q + i + 1))
                        for k in range(KD):
                            last = mm3(ps[:, b * 512 + i * n:b * 512 + (i + 1) * n], uH[:, k, tmc(2 * off + i)],
                                       uL[:, k, tmc(2 * off + i)], wH[:, k, :], wL[:, k, :], k == 0, k == KD - 1)
                last.then_inc(pj.h, 1)

            def log_decay():
                pe.wait_ge(pj_free[0].h, pj_free[0].at(lay, 2))
                pe.wait_ge(wa.h, wa.at(lay, 1))
                mm(bank(A[0]), wa2s[:], zaT[:], start=True, stop=True).then_inc(lgm.h, 1)

            def scores(br):
                if br == 0:
                    pe.wait_ge(pj_free[0].h, pj_free[0].at(lay, 4))
                else:
                    pe.wait_ge(rqk.h, rqk.at(lay, 1))
                for t in range(NT):
                    for h in range(HEADS):
                        r = slice(DK * h, DK * (h + 1))
                        last = mm(ps[:, A[h] * 512 + t * P:A[h] * 512 + (t + 1) * P], kT[r, tmc(t)], qT[r, tmc(t)],
                                  start=True, stop=True)
                        if t == NT - 1:
                            last.then_inc(att.h, 1)
                if br:
                    pe.wait_ge(o_l.h, o_l.at(lay, 2))
                for t in range(NT):
                    last = nc.tensor.transpose(ps[:, A[4] * 512 + t * P:A[4] * 512 + (t + 1) * P], k2T[:, tmc(t)], ident)
                last.then_inc(ktr.h, 1)

            def chunk_kv(br):
                hold(pe, kk2.h, kk2.at(lay, br + 1))
                if br:
                    pe.wait_ge(pj_free[0].h, pj_free[0].at(lay, 8))
                for n in range(8 if br == 0 else NT):
                    b = A[4] if br == 0 and n % 2 else A[5]
                    r = slice(CG * (n % 2), CG * (n % 2 + 1)) if br == 0 else slice(0, P)
                    t = n // 2 if br == 0 else n
                    for h in range(HEADS):
                        last = mm(ps[DK * h:DK * (h + 1), b * 512 + n * DV:b * 512 + (n + 1) * DV],
                                  k2[r, t, DK * h:DK * (h + 1)], vv[r, t, DV * h:DV * (h + 1)], start=True, stop=True)
                last.then_inc(kv.h, 1)

            def mix_out(br):
                pe.wait_ge(st.h, st.at(lay, br + 1))
                pe.wait_ge(att_e.h, att_e.at(lay, 4 * br + 4))
                r4 = [slice(DK * h, DK * (h + 1)) for h in range(HEADS)]
                qi = qT if br == 0 else bT
                for t in range(NT):
                    o = [ps[:, A[h] * 512 + t * DV:A[h] * 512 + (t + 1) * DV] for h in range(HEADS)]
                    for c in ((2 * t, 2 * t + 1) if br == 0 else (t,)):
                        for h in range(HEADS):
                            if br == 0:
                                half_rows = slice(CG * (c % 2), CG * (c % 2 + 1))
                                mm(o[h][half_rows], qi[r4[h], CG * c:CG * (c + 1)], prev[r4[h], c, :], start=True, stop=False,
                                   skip_group_check=True)
                            else:
                                mm(o[h], qi[r4[h], tmc(t)], prev[r4[h], t, :], start=True, stop=False, skip_group_check=True)
                    for h in range(HEADS):
                        last = mm(o[h], attT[:, h, t, :], vv[:, t, DV * h:DV * (h + 1)], start=False, stop=True,
                                  skip_group_check=True)
                        if t == NT - 1:
                            last.then_inc(o_m.h, 1)

            def window_values():
                pe.wait_ge(pj_free[0].h, pj_free[0].at(lay, 6))
                for t in range(NT):
                    last = nc.tensor.transpose(ps[:, A[5] * 512 + t * P:A[5] * 512 + (t + 1) * P], svT[:, tmc(t)], ident)
                last.then_inc(sv_t.h, 1)

            def out_transposes(br):
                if br == 0:
                    pe.wait_ge(sv_c.h, sv_c.at(lay, 1))
                pe.wait_ge(o_n.h, o_n.at(lay, br + 1))
                for hh in range(2):
                    for t in range(NT):
                        last = nc.tensor.transpose(ps[:, A[4 + hh] * 512 + t * P:A[4 + hh] * 512 + (t + 1) * P],
                                                   on[:, t, 2 * hh:2 * hh + 2, :].rearrange("p h e -> p (h e)"), ident)
                    last.then_inc(o_t.h, 1)

            def rotate():
                pe.wait_ge(pj_free[0].h, pj_free[0].at(lay, 7))
                pe.wait_ge(o_e.h, o_e.at(lay, 4))
                for x, src in enumerate((qT, kT)):
                    mm(bank(A[x]), rot, src[:], start=True, stop=True).then_inc(rotd.h, 1)

            def step(s):
                if 2 <= s:
                    pair_ = (2 * s - 4, 2 * s - 3)
                    for n in pair_:
                        e = (sc_ea, sc_ed)[n % 2]
                        hold(pe, e.h, e.at(lay, n // 2 + 1))
                    if n % 8 == 1 and n > 1:
                        hold(pe, a_l.h, a_l.at(lay, n // 8))
                    if n == 1:
                        hold(pe, o_l.h, o_l.at(lay, 4))
                    for i in range(item(n)[4]):
                        for n in pair_:
                            win, h, t, k0, nk = item(n)
                            o = ps[HD * (h % 2):HD * (h % 2 + 1), A[4] * 512 + t * P:A[4] * 512 + (t + 1) * P]
                            v = swv[:, k0 + i, HD * (h // 2):HD * (h // 2 + 1)] if win else mv[:, k0 + i, HD * h:HD * (h + 1)]
                            last = mm(o, v, prT[:, n % 2, i * P:(i + 1) * P], start=i == 0, stop=i == nk - 1, skip_group_check=True)
                    if n % 8 == 7:
                        last.then_inc(a_o.h, 1)
                if 1 <= s <= NITEMS // 2:
                    for n in (2 * s - 2, 2 * s - 1):
                        nk = item(n)[4]
                        pe.wait_ge(sc_n.h, sc_n.at(lay, n + 1))
                        for i in range(nk):
                            last = nc.tensor.transpose(ps[:, A[2 + n % 2] * 512 + i * P:A[2 + n % 2] * 512 + (i + 1) * P],
                                                       pr[:, n % 2, i * P:(i + 1) * P], ident)
                        last.then_inc(sc_t.h, 1)
                if s < NITEMS // 2:
                    if s == 0:
                        pe.wait_ge(o_e.h, o_e.at(lay, 8))
                    for n in (2 * s, 2 * s + 1):
                        win, h, t, k0, nk = item(n)
                        g = h // 2 if win else h % 2
                        r = slice(HD * g, HD * (g + 1))
                        keys = slice(k0 * P, (k0 + nk) * P)
                        q, k = (swq[r, h % 2, tmc(t)], swk[r, keys]) if win else (mq[r, h // 2, tmc(t)], mk[r, h // 2, keys])
                        mm(bank(A[n % 2], nk * P), q, k, start=True, stop=True).then_inc(sc.h, 1)

            PIECES = {3: log_decay, 7: lambda: scores(0), 8: lambda: chunk_kv(0), 10: lambda: mix_out(0),
                      11: window_values, 12: lambda: out_transposes(0), 13: rotate, 15: lambda: scores(1), 16: lambda: chunk_kv(1),
                      18: lambda: mix_out(1), 20: lambda: out_transposes(1)}
            for q in range(NH):
                half(q)
                if q in PIECES:
                    PIECES[q]()
                if q >= STEP0:
                    step(q - STEP0)

            def branch(i, steps):
                for j in range(KD):
                    c, b = j // 2, (NH + j) % 2
                    wH, wL = (w[:, c, :].rearrange("p (k n) -> p k n", k=KD) for w in (ringH, ringL))
                    if j % 2 == 0:
                        pe.wait_ge(w_l.h, w_l.at(lay, U_GATE + c + 1) + i * 4)
                    pe.wait_ge(pj_free[b].h, pj_free[b].at(lay, (NH + j) // 2) + i * 4)
                    for k in range(KD):
                        last = mm3(bank(b), wH[:, k, ds((j % 2) * P, P)], wL[:, k, ds((j % 2) * P, P)],
                                   uH[:, k, :], uL[:, k, :], k == 0, k == KD - 1)
                    last.then_inc(pj.h, 1)
                    if steps is not None and j + steps < NITEMS // 2 + 2:
                        step(j + steps)
                    if j == 0 and steps == NH - STEP0:
                        pe.wait_ge(o_l.h, o_l.at(lay, 4))
                    if j == 0 and steps == NH - STEP0 + KD:
                        pe.wait_ge(a_l.h, a_l.at(lay, 2))
                    if j == 0 and steps is None:
                        pe.wait_ge(a_l.h, a_l.at(lay, 4))
                    if j % 2 == 0:
                        pe.wait_ge(b_l.h, b_l.at(lay, c + 1) + i * 4)
                    if not (steps == NH - STEP0 and j == 0):
                        pe.wait_ge(tm.h, tm.at(lay, j) + i * 8)
                    cc = ds((j % 2) * P, P)
                    for k in range(2):
                        h, l = (w[c % 2][:].rearrange("p (k n) -> p k n", k=2)[:, k, cc] for w in (bH, bL))
                        rh, rl_ = ((w[:, ds(i * 2 + k, 1), :] if steps is None else w[:, i * 2 + k:i * 2 + k + 1, :]).rearrange("p a n -> p (a n)")
                                   for w in (oH, oL))
                        last = mm3(bank(A[5]), h, l, rh, rl_, k == 0, k == 1)
                    last.then_inc(yb.h, 1)

            branch(0, NH - STEP0)
            branch(1, NH - STEP0 + KD)
            with pe.Fori(2, 4) as i:
                branch(i, None)

            def out_half(c, t):
                b = (NH + 32 + 4 * c + t) % 2
                pe.wait_ge(pj_free[b].h, pj_free[b].at(lay, (NH + 32 + 4 * c + t) // 2))
                if t == 0:
                    pe.wait_ge(w_l.h, w_l.at(lay, U_OUT + 2 * c + 2))
                for k in range(KD):
                    if c == 0 and t == 0:
                        pe.wait_ge(m_l.h, m_l.at(lay, k + 1))
                    rh, rl_ = (w[:, 2 * c:2 * c + 2, k * 256:(k + 1) * 256] for w in (ringH, ringL))
                    last = mm3(bank(b).rearrange("p (a n) -> p a n", a=2), uH[:, k, tmc(t)], uL[:, k, tmc(t)], rh, rl_,
                               k == 0, k == KD - 1)
                last.then_inc(pj.h, 1)

            def transpose_2(t):
                norm_transposes(NT + t, n_h)

            def route(t):
                if t == 0:
                    pe.wait_ge(rc_in.h, rc_in.at(lay, 48))
                pe.wait_ge(n_h.h, n_h.at(lay, NT + t + 1))
                for k in range(KD):
                    last = mm(ps[:, A[5] * 512 + t * 36:A[5] * 512 + (t + 1) * 36], u2T[:, k, tmc(t)], wr[:, k, :],
                              start=k == 0, stop=k == KD - 1, skip_group_check=True)
                last.then_inc(rl.h, 1)

            for t in range(NT):
                out_half(0, t)
            for t in range(NT):
                out_half(1, t)
                if t >= 1:
                    transpose_2(t - 1)
                if t >= 2:
                    route(t - 2)
            transpose_2(NT - 1)
            route(NT - 2)
            route(NT - 1)

            pe.wait_ge(r_m.h, r_m.at(lay, 1))
            mm(bank(A[4], (NT + 1) * NE), ones, count[:].rearrange("p t e -> p (t e)"), start=True, stop=False,
               skip_group_check=True)
            mm(bank(A[4], P), upper, selM[:].rearrange("p t e -> p (t e)"), start=False, stop=True,
               skip_group_check=True).then_inc(r_r.h, 1)

            def list_product(rhs, c0, n):
                for x in range(8):
                    last = mm(ps[:, A[4] * 512 + c0:A[4] * 512 + c0 + n], slot_of[:, x, :], rhs(x), start=x == 0, stop=x == 7,
                              skip_group_check=True)
                return last

            def list_tokens():
                return list_product(lambda x: tok_rhs[:, x].rearrange("p a e -> p (a e)"), 256, 2 * NP)

            def list_weights():
                return list_product(lambda x: w_rhs[:, x, :], 384, NP)

            pe.wait_ge(l_a.h, l_a.at(lay, 1))
            list_tokens().then_inc(l_p.h, 1)
            pe.wait_ge(l_b.h, l_b.at(lay, 1))
            list_weights().then_inc(l_q.h, 1)

            def transpose_rows(src):
                for k in range(KD):
                    last = nc.tensor.transpose(ps[:, A[2] * 512 + k * P:A[2] * 512 + (k + 1) * P],
                                               src[:, k * P:(k + 1) * P], ident)
                return last

            def two_experts(o, lhs, rhs, first, last):
                for x in range(2):
                    r = slice(CAP * x, CAP * (x + 1))
                    ins = mm(o[r], lhs[:, r], rhs[x], start=first, stop=last, skip_group_check=True)
                return ins

            def up_product(b, x_t_, r0):
                for k in range(KD):
                    w = [w13[:, PLACE[r0 + x]].rearrange("p m (k n) -> p m k n", k=KD)[:, :, k, :] for x in range(2)]
                    last = two_experts(bank(b).rearrange("p (m n) -> p m n", m=2), x_t_[:, k * P:(k + 1) * P], w, k == 0, k == KD - 1)
                return last

            def transpose_hidden():
                for k in range(2):
                    last = nc.tensor.transpose(ps[:, A[4] * 512 + k * P:A[4] * 512 + (k + 1) * P], hid[:, k * P:(k + 1) * P], ident)
                return last

            def down_product(r0):
                for c in range(2):
                    for k in range(2):
                        w = [w2[r0 + x][:, k, c * 512:(c + 1) * 512] for x in range(2)]
                        last = two_experts(bank(A[c]), hT[:, k, :], w, k == 0, k == 1)
                return last

            def pair_rows(i, y):
                pe.wait_ge(xg_in[y].h, xg_in[y].at(lay, 16) + i * 16)
                transpose_rows(xg[y]).then_inc(x_t.h, 1)

            def combine(parts, added, value):
                for x in range(8):
                    t, c = x // 2, slice(x % 2 * 512, (x % 2 + 1) * 512)
                    pe.wait_ge(added[0], value + x)
                    for m, (tokens, rows) in enumerate(parts):
                        last = mm(bank((1, A[5])[x % 2]), tokens[:, tmc(t)], rows[:, c], start=m == 0, stop=m == len(parts) - 1)
                    last.then_inc(added[1], 1)

            def combine_two(i):
                hold(pe, y_l.h, y_l.at(lay, 2) + i * 2)
                hold(pe, t_of.h, t_of.at(lay, 2) + i * 2)
                combine([(tok_of[y], w[y]) for y in range(2) for w in (yH, yL)], (ca.h, cm.h), ca.at(lay, -1) + i * 8)

            def pair(i, y, more, behind=True):
                pe.wait_ge(x_ca.h, x_ca.at(lay, y + 1) + i * 2)
                pe.wait_ge(x_cd.h, x_cd.at(lay, y + 1) + i * 2)
                for x in range(2):
                    pe.wait_ge(w13_in[2 * y + x].h, w13_in[2 * y + x].at(lay, 32) + i * 32)
                up_product(0, xT[y], 2 * y).then_inc(up.h, 1)
                if more:
                    pair_rows(i + y, 1 - y)
                if behind:
                    combine_two(i - 1)
                pe.wait_ge(hd.h, hd.at(lay, y + 1) + i * 2)
                transpose_hidden().then_inc(h_t.h, 1)
                pe.wait_ge(h_c.h, h_c.at(lay, y + 1) + i * 2)
                for x in range(2):
                    pe.wait_ge(w2_in[2 * y + x].h, w2_in[2 * y + x].at(lay, 16) + i * 16)
                down_product(2 * y).then_inc(yd.h, 1)

            pair_rows(0, 0)
            pair(0, 0, True, behind=False)
            pair(0, 1, True, False)
            with pe.Fori(1, NP // 2 - 1) as i:
                pair(i, 0, True)
                pair(i, 1, True, behind=False)
            pair(NP // 2 - 1, 0, True)
            pair(NP // 2 - 1, 1, False, behind=False)

            def window_lists(n):
                hold(pe, ov_la, n + 1)
                list_tokens()
                list_weights().then_inc(ov_lp, 1)

            def window_item(n, p):
                hold(pe, ca.h, ca.at(lay, SUMS - 8))
                hold(pe, ov_x, n * 16 + 16)
                hold(pe, ov_c, n + 1)
                transpose_rows(xg[0]).then_inc(ov_t, 1)
                hold(pe, ov_w, n * 96 + 96)
                hold(pe, ov_c, n + 2)
                up_product(0, xT[0], 0).then_inc(ov_u, 1)
                hold(pe, ov_h, n + 1)
                transpose_hidden().then_inc(ov_ht, 1)
                hold(pe, y_l.h, y_l.at(lay, NP))
                hold(pe, ov_hc, n + 1)
                down_product(0).then_inc(ov_y, 1)
                hold(pe, ov_yl, n + 1)
                hold(pe, ov_of, n + 1)
                combine([(tok_w, yHw), (tok_w, yLw)], (ov_ca, ov_cm), n * 8 + 1)

            before, own = window_range(pe, lay)
            later_windows(pe, before, own, window_lists, window_item)
            hold(pe, ov_ca, (before + own) * (NP * 8) + 2)
            combine_two(NP // 2 - 1)

    @block.scalar
    def _(act):
        fn = nc.scalar.activation
        act.wait_ge(s_cst.h, 16 * N_CST)

        with act.Fori(0, L) as lay:
            links = [0]

            def act_link(ins):
                links[0] += 1
                ins.then_inc(act_c.h, 1)
                act.wait_ge(act_c.h, act_c.at(lay, links[0]))

            def split_h(u):
                act.wait_ge(w_in_slot[u % RING].h, w_in_slot[u % RING].at(lay, 16 * (u // RING + 1)))
                n = 1024 if u == 1 else 2048
                fn(ringH[:, u % RING, 0:n], raw[:, u % RING, 0:n], ACT.Copy).then_inc(w_h.h, 1)

            def bank_full(q):
                act.wait_ge(pj.h, pj.at(lay, q + 1))

            def copy_out(q, dst, func=ACT.Copy):
                bank_full(q)
                n = bank(q % 2) if dst.shape[0] == P else ps[0:16, (q % 2) * 512:(q % 2) * 512 + 512]
                fn(dst, n, func).then_inc(pj_free[q % 2].h, 1)

            def squares(n, t, ready, value):
                act.wait_ge(ready.h, value)
                act.wait_ge(n_ss.h, n_ss.at(lay, n))
                fn(junk[:], hs[:, t, :], ACT.Square, accum_out=ss[:, n:n + 1]).then_inc(n_ss.h, 1)

            def norm_h(t):
                act.wait_ge(n_t.h, n_t.at(lay, t + 1))
                b = A[0] if t % 2 == 0 else A[2]
                fn(uH[:, :, tmc(t)], ps[:, b * 512:b * 512 + 1024].rearrange("p (k n) -> p k n", k=KD), ACT.Copy)\
                    .then_inc(n_h.h, 1)

            for t in range(NT):
                squares(t, t, ca, ca.at(lay, 2 * t - 6))
                if t % 2:
                    split_h(t // 2)
            for t in range(NT):
                norm_h(t)

            def k2_rows(br):
                act.wait_ge(ktr.h, ktr.at(lay, br + 1))
                fn(k2[:].rearrange("p t n -> p (t n)"), bank(A[4]), ACT.Copy).then_inc(kk2.h, 1)

            def head_squares(br):
                for h in range(HEADS):
                    act.wait_ge(o_m.h, o_m.at(lay, 4 * br + h + 1))
                    fn(on[:, :, h, :], bank(A[h], 256).rearrange("p (t e) -> p t e", t=NT), ACT.Square).then_inc(o_sq.h, 1)

            def out_h(br):
                for hh in range(2):
                    act.wait_ge(o_t.h, o_t.at(lay, 2 * br + hh + 1))
                    fn(oH[:, (0, 6)[br] + hh, :], bank(A[4 + hh]), ACT.Copy).then_inc(o_h.h, 1)

            def step(s):
                if 1 <= s <= NITEMS // 2:
                    n = 2 * s - 2
                    act.wait_ge(sc_t.h, sc_t.at(lay, n + 1))
                    nk = item(n)[4]
                    fn(prT[:, 0, 0:nk * P], bank(A[2], nk * P), ACT.Copy).then_inc(sc_ea.h, 1)
                if s - 2 in (3, 7, 11, 15):
                    m = (s - 2) // 4
                    act.wait_ge(a_o.h, a_o.at(lay, m + 1))
                    fn(oH[:, 2 + m, :], bank(A[4]), ACT.Copy).then_inc(a_h.h, 1)
                if s < NITEMS // 2:
                    for n in (2 * s, 2 * s + 1):
                        win, h, t, k0, nk = item(n)
                        x = n % 2
                        hold(act, sc_b.h, sc_b.at(lay, n + 1))
                        if win:
                            fn(es[:, x:x + 1], sink[:, ds(lay, 1), h:h + 1].rearrange("p a b -> p (a b)"), ACT.Exp,
                               bias=nb[:, x:x + 1])
                        fn(pr[:, x, 0:nk * P], bank(A[x], nk * P), ACT.Exp, bias=nb[:, x:x + 1], scale=HD ** -0.5,
                           accum_out=den[:, x:x + 1]).then_inc(sc_p.h, 1)

            for q in range(NH):
                kind, u, off, name = HALVES[q]
                if q == 0 or HALVES[q - 1][1] != u:
                    split_h(u + 2)
                if name == "ga":
                    fn(wa2s[:], wa2[:, ds(lay, 1), :].rearrange("p a n -> p (a n)"), ACT.Copy).then_inc(wa.h, 1)
                    copy_out(q, zaT[:])
                elif name in ("gv", "rv"):
                    copy_out(q, vv[:, 2 * off:2 * off + 2, :].rearrange("p t n -> p (t n)"))
                elif name in ("gr", "rg"):
                    copy_out(q, sr[:, 2 * off:2 * off + 2, :].rearrange("p t n -> p (t n)"), ACT.Silu)
                elif q == 7:
                    bank_full(q)
                    fn(swq[0:HD, 0, :], bank(1)[0:HD], ACT.Copy)
                    fn(swq[0:HD, 1, :], bank(1)[HD:P], ACT.Copy).then_inc(pj_free[1].h, 1)
                elif q == 9:
                    copy_out(q, swk[:])
                elif q == 11:
                    copy_out(q, qT[:])
                elif q == 12:
                    copy_out(q, kT[:])
                elif q == 17:
                    act.wait_ge(h_out.h, h_out.at(lay, 16))
                    copy_out(q, mq[:, 0, :])
                elif q == 19:
                    copy_out(q, mk[:, 0, :])
                elif q == 21:
                    copy_out(q, mv[:, 0:2, :].rearrange("p t n -> p (t n)"))
                if q == 3:
                    hold(act, lgm.h, lgm.at(lay, 1))
                    act_link(fn(lga[:, 0, :], bank(A[0]), ACT.Abs, bias=ba[:, ds(lay, 1)]))
                    act_link(fn(lga[:, 0, :], lga[:, 0, :], ACT.Exp, scale=-1.0))
                    fn(lga[:, 0, :], lga[:, 0, :], ACT.Ln, bias=1.0).then_inc(lg_a.h, 1)
                if q == 4:
                    act.wait_ge(lg_b.h, lg_b.at(lay, 1))
                    fn(qT[:], bT[:], ACT.Exp, scale=1.0 / 16).then_inc(lg_e.h, 1)
                    fn(kT[:], bT[:], ACT.Exp, scale=-1.0 / 16).then_inc(lg_e.h, 1)
                    fn(dec[:], bT[:].rearrange("p (n c) -> p n c", c=CG)[:, :, CG - 1], ACT.Exp, scale=1.0 / 16).then_inc(lg_e.h, 1)
                    act.wait_ge(lg_d.h, lg_d.at(lay, 1))
                    fn(k2T[:], k2T[:], ACT.Exp, scale=1.0 / 16).then_inc(lg_e.h, 1)
                if q in (7, 15):
                    k2_rows(q // 15)
                if q in (10, 18):
                    head_squares(q // 18)
                if q in (12, 20):
                    out_h(q // 20)
                if q >= STEP0:
                    step(q - STEP0)

            def branch(i, steps):
                for j in range(KD):
                    c, b = j // 2, (NH + j) % 2
                    if j % 2 == 0:
                        x = c % 2
                        act.wait_ge(b_in[x].h, b_in[x].at(lay, 16 * (c // 2 + 1)) + i * 32)
                        fn(bH[x][:], braw[x][:], ACT.Copy).then_inc(b_h.h, 1)
                        s = (c + 2) % RING
                        act.wait_ge(w_in_slot[s].h, w_in_slot[s].at(lay, 16 * ((U_GATE + c + 2) // RING + 1)) + i * 16)
                        fn(ringH[:, s, :], raw[:, s, :], ACT.Copy).then_inc(w_h.h, 1)
                    act.wait_ge(pj.h, pj.at(lay, NH + j + 1) + i * 8)
                    if not (isinstance(i, int) and i == 0 and j < 2):
                        act.wait_ge(tm.h, tm.at(lay, j - 1) + i * 8)
                    fn(sig[:, j % 2, :], bank(b), ACT.Sigmoid).then_inc(pj_free[b].h, 1)
                    if steps is not None and j + steps < NITEMS // 2 + 2:
                        step(j + steps)

            branch(0, NH - STEP0)
            branch(1, NH - STEP0 + KD)
            with act.Fori(2, 4) as i:
                branch(i, None)
            act.wait_ge(pj.h, pj.at(lay, NH + 32))
            for k in range(KD):
                act.wait_ge(mg.h, mg.at(lay, 16 + k + 1))
                fn(uH[:, k, :], merged[:, k, :], ACT.Copy).then_inc(m_h.h, 1)
            split_h(U_OUT + 2)
            split_h(U_OUT + 3)

            def norm_2(t):
                act.wait_ge(n_t.h, n_t.at(lay, NT + t + 1))
                b = A[0] if t % 2 == 0 else A[2]
                fn(u2T[:, :, tmc(t)], ps[:, b * 512:b * 512 + 1024].rearrange("p (k n) -> p k n", k=KD), ACT.Copy)\
                    .then_inc(n_h.h, 1)

            for t in range(NT):
                q = NH + 36 + t
                squares(NT + t, t, pj_free[q % 2], pj_free[q % 2].at(lay, q // 2 + 1))
                if t:
                    norm_2(t - 1)
            norm_2(NT - 1)
            act.wait_ge(r_x.h, r_x.at(lay, 1))
            fn(ge[:].rearrange("p t g -> p (t g)"), gd[:].rearrange("p t g -> p (t g)"), ACT.Exp).then_inc(r_e.h, 1)
            act.wait_ge(r_x.h, r_x.at(lay, 2))
            fn(ex[:], dx[:], ACT.Exp).then_inc(r_e.h, 1)

            def rows_copy(i, y):
                act.wait_ge(x_t.h, x_t.at(lay, y + 1) + i * 2)
                fn(xT[y][:, 0:512], bank(A[2]), ACT.Copy).then_inc(x_ca.h, 1)

            def hidden_copy():
                return fn(hT[:].rearrange("p k n -> p (k n)"), bank(A[4], 256), ACT.Copy)

            def pair(i, y, more):
                act.wait_ge(up.h, up.at(lay, y + 1) + i * 2)
                fn(silu[:], bank(0, FH), ACT.Silu).then_inc(sl.h, 1)
                if more:
                    rows_copy(i + y, 1 - y)
                act.wait_ge(h_t.h, h_t.at(lay, y + 1) + i * 2)
                hidden_copy().then_inc(h_c.h, 1)
                act.wait_ge(yd.h, yd.at(lay, y + 1) + i * 2)
                fn(yH[y][:], ps[:, A[0] * 512:A[0] * 512 + 1024], ACT.Copy).then_inc(y_h.h, 1)

            rows_copy(0, 0)
            with act.Fori(0, NP // 2 - 1) as i:
                pair(i, 0, True)
                pair(i, 1, True)
            pair(NP // 2 - 1, 0, True)
            pair(NP // 2 - 1, 1, False)

            def window_item(n, p):
                hold(act, ov_t, n + 1)
                fn(xT[0][:], ps[:, A[2] * 512:A[2] * 512 + 1024], ACT.Copy).then_inc(ov_c, 1)
                hold(act, ov_u, n + 1)
                fn(silu[:], bank(0, FH), ACT.Silu).then_inc(ov_s, 1)
                hold(act, ov_ht, n + 1)
                hidden_copy().then_inc(ov_hc, 1)
                hold(act, ov_y, n + 2)
                fn(yHw[:], ps[:, A[0] * 512:A[0] * 512 + 1024], ACT.Copy).then_inc(ov_yh, 1)

            before, own = window_range(act, lay)
            later_windows(act, before, own, None, window_item)
        for t in range(NT):
            act.wait_ge(ca.h, ca.at(L, 2 * t - 6))
            act.wait_ge(n_ss.h, n_ss.at(L, t))
            fn(junk[:], hs[:, t, :], ACT.Square, accum_out=ss[:, t:t + 1]).then_inc(n_ss.h, 1)

    @block.gpsimd
    def _(pool):
        gp_ = nc.gpsimd
        for s in (up, yb, ca, n_ss):
            pool.sem_inc(s.h, s.credit)
        for s, n in ((ov_c, 1), (ov_y, 1), (ov_ca, 2)):
            pool.sem_inc(s, n)
        hold(pool, s_cst.h, 16 * N_CST)

        with pool.Fori(0, L) as lay:

            def split_l(u):
                n = 1024 if u == 1 else 2048
                s = u % RING
                hold(pool, w_h.h, w_h.at(lay, u + 1))
                gp_.tensor_tensor(ringL[:, s, 0:n], raw[:, s, 0:n], ringH[:, s, 0:n].bitcast(f32), ALU.subtract).then_inc(w_l.h, 1)

            def norm_scale(n):
                hold(pool, n_ms.h, n_ms.at(lay, n + 1))
                gp_.tensor_tensor(rstd[:, n:n + 1], ms[:, n:n + 1], nhalf[:, 0:1], ALU.pow).then_inc(n_rs.h, 1)

            for t in range(NT):
                norm_scale(t)
                if t % 2:
                    split_l(t // 2)
            gp_.memset(attT[:].rearrange("p h t i -> p (h t i)"), 0.0).then_inc(att0.h, 1)

            def gain(br):
                q = (4, 16)[br]
                hold(pool, pj_free[0].h, pj_free[0].at(lay, q // 2 + 1))
                hold(pool, pj_free[1].h, pj_free[1].at(lay, q // 2))
                g = ng[:, ds(lay, 1), br, :].rearrange("p a e -> p (a e)").rearrange("p (o e) -> p o e", o=1)
                v = sr[:].rearrange("p t (h e) -> p (t h) e", e=DV)
                gp_.tensor_tensor(v, v, g.broadcast_to([P, 16, DV]), ALU.mult).then_inc(srg.h, 1)

            def head_scale(br):
                hold(pool, o_ms.h, o_ms.at(lay, br + 1))
                gp_.tensor_tensor(hrs[:].rearrange("p h t -> p (h t)"), hms[:], nhalf, ALU.pow).then_inc(o_rs.h, 1)

            for q in range(NH):
                u = HALVES[q][1]
                if q == 0 or HALVES[q - 1][1] != u:
                    split_l(u + 2)
                if q in (4, 16):
                    gain(q // 16)
                if q in (10, 18):
                    head_scale(q // 18)

            def branch(i):
                for j in range(KD):
                    c = j // 2
                    if j % 2 == 0:
                        x, s = c % 2, (c + 2) % RING
                        hold(pool, b_h.h, b_h.at(lay, c + 1) + i * 4)
                        gp_.tensor_tensor(bL[x][:], braw[x][:], bH[x][:].bitcast(f32), ALU.subtract).then_inc(b_l.h, 1)
                        hold(pool, w_h.h, w_h.at(lay, U_GATE + c + 3) + i * 4)
                        gp_.tensor_tensor(ringL[:, s, :], raw[:, s, :], ringH[:, s, :].bitcast(f32), ALU.subtract).then_inc(w_l.h, 1)
                    if not (isinstance(i, int) and i == 0):
                        hold(pool, tm.h, tm.at(lay, j + 1) + i * 8)
                        gp_.tensor_tensor(merged[:, j, :], merged[:, j, :], term[:, j % 2, :], ALU.add).then_inc(mg.h, 1)

            branch(0)
            with pool.Fori(1, 4) as i:
                branch(i)
            split_l(U_OUT + 2)
            split_l(U_OUT + 3)

            for t in range(NT):
                norm_scale(NT + t)
                hold(pool, n_u.h, n_u.at(lay, NT + t + 1))
                pool.dma_start(x_dram[t * P:(t + 1) * P, :], ut[:, t % 2, :]).then_inc(u2o[t % 2].h, 16)

            hold(pool, pj.h, pj.at(lay, NH + 40))
            for x in range(2):
                gp_.memset(xg[x][:], 0.0).then_inc(xz.h, 1)
            for x in range(2):
                hold(pool, u2o[x].h, u2o[x].at(lay, 32))

            def gather(i, y):
                if not isinstance(i, int) or i:
                    hold(pool, x_t.h, x_t.at(lay, y - 1) + i * 2)
                    hold(pool, xg_in[y].h, xg_in[y].at(lay, 0) + i * 16)
                p = i * 2 + y
                gp_.tensor_copy(gi[y][:], toks[:, p:p + 1] if isinstance(p, int) else toks[:, ds(p, 1)]).then_inc(pc.h, 1)
                hold(pool, pc.h, pc.at(lay, y + 1) + i * 2)
                gp_.indirect_dma_start(xg[y][:], None, x_dram, bass.IndirectOffsetOnAxis(gi[y][:, 0:1], axis=0),
                                       bounds_check=S - 1, oob_is_err=False).then_inc(xg_in[y].h, 16)

            hold(pool, xz.h, xz.at(lay, 2))
            hold(pool, l_g.h, l_g.at(lay, 1))
            gather(0, 0)
            gather(0, 1)
            with pool.Fori(1, NP // 2) as i:
                for y in range(2):
                    gather(i, y)

            def window_lists(n):
                hold(pool, ov_lg, n + 1)

            def window_rows(n, p):
                hold(pool, x_t.h, x_t.at(lay, NP))
                hold(pool, ov_c, n + 1)
                gp_.tensor_copy(gi[0][:], toks[:, ds(p, 1)]).then_inc(ov_p, 1)
                hold(pool, ov_p, n + 1)
                gp_.indirect_dma_start(xg[0][:], None, x_dram, bass.IndirectOffsetOnAxis(gi[0][:, 0:1], axis=0),
                                       bounds_check=S - 1, oob_is_err=False).then_inc(ov_x, 16)

            before, own = window_range(pool, lay)
            later_windows(pool, before, own, window_lists, window_rows)
        for t in range(NT):
            hold(pool, n_ms.h, n_ms.at(L, t + 1))
            gp_.tensor_tensor(rstd[:, t:t + 1], ms[:, t:t + 1], nhalf[:, 0:1], ALU.pow).then_inc(n_rs.h, 1)

    @block.vector
    def _(dve):
        v = nc.vector
        dve.wait_ge(s_cst.h, 16 * N_CST)
        v.memset(extra[:], 0.0)
        v.memset(windows[:].rearrange("p a b -> p (a b)"), 0)
        v.tensor_scalar(nsink[:], sink[:], -1.0, None, ALU.mult).then_inc(s_init.h, 1)
        dve.wait_ge(s_init.h, 1)

        def norm_rows(lay, n, gain, permute, slot_free=None):
            t = n % NT
            dve.wait_ge(n_rs.h, n_rs.at(lay, n + 1))
            if slot_free is not None:
                slot_free(t)
            o = ut[:, t % 2, :]
            i = hs[:, t, :]
            g = gain[:]
            if permute:
                o = o.rearrange("p (k q) -> p q k", k=KD)
                i = i.rearrange("p (q k) -> p q k", k=KD)
                g = g.rearrange("p (q k) -> p q k", k=KD)
            v.scalar_tensor_tensor(o, i, rstd[:, n:n + 1], g, ALU.mult, ALU.mult).then_inc(n_u.h, 1)

        def mean_square(lay, n):
            dve.wait_ge(n_ss.h, n_ss.at(lay, n + 1))
            v.tensor_scalar(ms[:, n:n + 1], ss[:, n:n + 1], 1.0 / D, EPS, ALU.mult, ALU.add).then_inc(n_ms.h, 1)

        with dve.Fori(0, L) as lay:
            links = [0]

            def link(ins, alone=False):
                links[0] += 1
                ins.then_inc(dve_c.h, 1)
                (hold if alone else wait)(dve, dve_c.h, dve_c.at(lay, links[0]))

            def norm_low(t):
                dve.wait_ge(n_h.h, n_h.at(lay, t + 1))
                b = A[0] if t % 2 == 0 else A[2]
                v.tensor_tensor(uL[:, :, tmc(t)], ps[:, b * 512:b * 512 + 1024].rearrange("p (k n) -> p k n", k=KD),
                                uH[:, :, tmc(t)].bitcast(f32), ALU.subtract).then_inc(n_l.h, 1)

            def ut_transposed(t):
                if t >= 2:
                    dve.wait_ge(n_t.h, n_t.at(lay, t - 1))

            dve.wait_ge(g1_in.h, g1_in.at(lay, 16))
            mean_square(lay, 0)
            mean_square(lay, 1)
            for t in range(NT):
                if t >= 2:
                    norm_low(t - 2)
                norm_rows(lay, t, g1, False, ut_transposed)
                if t < 2:
                    mean_square(lay, t + 2)
            norm_low(2)
            norm_low(3)

            def bank_full(q):
                dve.wait_ge(pj.h, pj.at(lay, q + 1))

            def copy_out(q, dst):
                bank_full(q)
                v.tensor_copy(dst, bank(q % 2)).then_inc(pj_free[q % 2].h, 1)

            def log_decay():
                dve.wait_ge(lg_a.h, lg_a.at(lay, 1))
                link(v.tensor_scalar(lga[:, 1, :], bank(A[0]), ba[:, ds(lay, 1)], 0.0, ALU.add, ALU.min))
                link(v.tensor_tensor(lga[:, 1, :], lga[:, 1, :], lga[:, 0, :], ALU.subtract))
                for n in range(S // CG):
                    c = slice(n * CG, (n + 1) * CG)
                    last = v.tensor_tensor_scan(bT[:, c], lga[:, 1, c], lga[:, 1, c], 0.0, ALU.add, ALU.bypass)
                last.then_inc(lg_b.h, 1)
                dve.wait_ge(lg_b.h, lg_b.at(lay, 1))
                b = bT[:].rearrange("p (n c) -> p n c", c=CG)
                v.tensor_tensor(k2T[:].rearrange("p (n c) -> p n c", c=CG), b[:, :, CG - 1:CG].broadcast_to([P, S // CG, CG]), b,
                                ALU.subtract).then_inc(lg_d.h, 1)

            def mask_scores(br):
                if br == 0:
                    dve.wait_ge(att0.h, att0.at(lay, 1))
                for h in range(HEADS):
                    hold(dve, att.h, att.at(lay, 4 * br + h + 1))
                    src = bank(A[h]).rearrange("p (t i) -> p t i", t=NT)
                    if br == 0:
                        m = gmask.bitcast(u32).rearrange("p (o i) -> p o i", o=1).broadcast_to([P, NT, P])
                        v.copy_predicated(attT[:, h, :, :], m, src).then_inc(att_e.h, 1)
                    else:
                        v.tensor_tensor(attT[:, h, :, :], src, decay[:, h:h + 1, :].broadcast_to([P, NT, P]), ALU.mult)\
                            .then_inc(att_e.h, 1)

            def states(br):
                if br == 0:
                    link(v.memset(prev[:, 0, :], 0.0))
                    dve.wait_ge(lg_e.h, lg_e.at(lay, 4))
                dve.wait_ge(kv.h, kv.at(lay, br + 1))
                count = 8 if br == 0 else NT
                for n in range(count - 1):
                    b = A[4] if br == 0 and n % 2 else A[5]
                    ins = v.scalar_tensor_tensor(prev[:, n + 1, :], prev[:, n, :], dec[:, n:n + 1] if br == 0 else cdec,
                                                 ps[:, b * 512 + n * DV:b * 512 + (n + 1) * DV], ALU.mult, ALU.add)
                    if n < count - 2:
                        link(ins)
                    else:
                        ins.then_inc(st.h, 1)

            def head_norm(br):
                for h in range(HEADS):
                    dve.wait_ge(o_sq.h, o_sq.at(lay, 4 * br + h + 1))
                    ins = v.tensor_reduce(hss[:, h, :], on[:, :, h, :], AX.X, ALU.add)
                link(ins)
                v.tensor_scalar(hms[:], hss[:].rearrange("p h t -> p (h t)"), 1.0 / DV, EPS, ALU.mult, ALU.add).then_inc(o_ms.h, 1)
                dve.wait_ge(o_rs.h, o_rs.at(lay, br + 1))
                for h in range(HEADS):
                    r = hrs[:, h, :].rearrange("p (t o) -> p t o", o=1).broadcast_to([P, NT, DV])
                    v.tensor_tensor(on[:, :, h, :], bank(A[h], 256).rearrange("p (t e) -> p t e", t=NT), r, ALU.mult)\
                        .then_inc(o_e.h, 1)
                dve.wait_ge(o_e.h, o_e.at(lay, 4 * br + 4))
                dve.wait_ge(srg.h, srg.at(lay, br + 1))
                o = on[:].rearrange("p t h e -> p (t h e)")
                v.tensor_tensor(o, o, sr[:].rearrange("p t n -> p (t n)"), ALU.mult).then_inc(o_n.h, 1)

            def out_low(br):
                for hh in range(2):
                    dve.wait_ge(o_h.h, o_h.at(lay, 2 * br + hh + 1))
                    k = (0, 6)[br] + hh
                    v.tensor_tensor(oL[:, k, :], bank(A[4 + hh]), oH[:, k, :].bitcast(f32), ALU.subtract).then_inc(o_l.h, 1)

            def rotate():
                dve.wait_ge(tabs_in.h, tabs_in.at(lay, 16))
                dve.wait_ge(rotd.h, rotd.at(lay, 2))
                v.tensor_tensor(bT[:], bank(A[0]), sin, ALU.mult)
                v.tensor_tensor(k2T[:], bank(A[1]), sin, ALU.mult)
                v.tensor_tensor(qT[:], qT[:], cos, ALU.mult)
                link(v.tensor_tensor(kT[:], kT[:], cos, ALU.mult))
                v.tensor_tensor(qT[:], qT[:], bT[:], ALU.add)
                link(v.tensor_tensor(kT[:], kT[:], k2T[:], ALU.add))
                for dst, src, d in ((bT, qT, qdec), (k2T, kT, kdec)):
                    last = v.tensor_tensor(dst[:].rearrange("p (t i) -> p t i", t=NT), src[:].rearrange("p (t i) -> p t i", t=NT),
                                           d.rearrange("p (o i) -> p o i", o=1).broadcast_to([P, NT, P]), ALU.mult)
                last.then_inc(rqk.h, 1)

            def step(s):
                if 1 <= s <= NITEMS // 2:
                    n = 2 * s - 1
                    dve.wait_ge(sc_t.h, sc_t.at(lay, n + 1))
                    nk = item(n)[4]
                    v.tensor_copy(prT[:, 1, 0:nk * P], bank(A[3], nk * P)).then_inc(sc_ed.h, 1)
                if s - 2 in (3, 7, 11, 15):
                    m = (s - 2) // 4
                    dve.wait_ge(a_h.h, a_h.at(lay, m + 1))
                    v.tensor_tensor(oL[:, 2 + m, :], bank(A[4]), oH[:, 2 + m, :].bitcast(f32), ALU.subtract).then_inc(a_l.h, 1)
                if s < NITEMS // 2:
                    pair = (2 * s, 2 * s + 1)
                    for n in pair:
                        win, h, t, k0, nk = item(n)
                        x = n % 2
                        dve.wait_ge(sc.h, sc.at(lay, n + 1))
                        m0 = 0 if win and nk == 2 else nk - 1
                        o = ps[:, A[x] * 512 + m0 * P:A[x] * 512 + nk * P]
                        link(v.tensor_tensor(o, o, wmask[:, 0:256] if m0 < nk - 1 else wmask[:, 128:256], ALU.add))
                        link(v.tensor_reduce(nm[:, x:x + 1], bank(A[x], nk * P), AX.X, ALU.max, negate=True))
                        if win:
                            lim = nsink[:, ds(lay, 1), h:h + 1].rearrange("p a b -> p (a b)")
                            v.tensor_scalar(nb[:, x:x + 1], nm[:, x:x + 1], HD ** -0.5, lim, ALU.mult, ALU.min).then_inc(sc_b.h, 1)
                        else:
                            v.tensor_scalar(nb[:, x:x + 1], nm[:, x:x + 1], HD ** -0.5, None, ALU.mult).then_inc(sc_b.h, 1)
                    for n in pair:
                        win, h, t, k0, nk = item(n)
                        x = n % 2
                        dve.wait_ge(sc_p.h, sc_p.at(lay, n + 1))
                        d = den
                        if win:
                            link(v.tensor_tensor(den2[:, x:x + 1], den[:, x:x + 1], es[:, x:x + 1], ALU.add))
                            d = den2
                        link(v.reciprocal(rden[:, x:x + 1], d[:, x:x + 1]))
                        v.tensor_scalar(pr[:, x, 0:nk * P], pr[:, x, 0:nk * P], rden[:, x:x + 1], None, ALU.mult).then_inc(sc_n.h, 1)

            for q in range(NH):
                name = HALVES[q][3]
                if name == "gq":
                    dve.wait_ge(lg_e.h, lg_e.at(lay, 4))
                    bank_full(q)
                    v.scalar_tensor_tensor(qT[:], bank(q % 2), DK ** -0.5, qT[:], ALU.mult, ALU.mult).then_inc(pj_free[q % 2].h, 1)
                elif name == "gk":
                    bank_full(q)
                    v.tensor_tensor(kT[:], bank(q % 2), kT[:], ALU.mult)
                    v.tensor_tensor(k2T[:], bank(q % 2), k2T[:], ALU.mult).then_inc(pj_free[q % 2].h, 1)
                elif q == 8:
                    bank_full(q)
                    v.tensor_copy(swq[HD:P, 0, :], bank(0)[0:HD])
                    v.tensor_copy(swq[HD:P, 1, :], bank(0)[HD:P]).then_inc(pj_free[0].h, 1)
                elif q == 10:
                    copy_out(q, svT)
                elif q == 18:
                    dve.wait_ge(h_out.h, h_out.at(lay, 16))
                    copy_out(q, mq[:, 1, :])
                elif q == 20:
                    copy_out(q, mk[:, 1, :])
                elif q == 22:
                    copy_out(q, mv[:, 2:4, :].rearrange("p t n -> p (t n)"))
                if q == 3:
                    log_decay()
                if q in (7, 15):
                    mask_scores(q // 15)
                if q in (8, 16):
                    states(q // 16)
                if q in (10, 18):
                    head_norm(q // 18)
                if q in (12, 20):
                    out_low(q // 20)
                if q == 11:
                    dve.wait_ge(sv_t.h, sv_t.at(lay, 1))
                    v.tensor_copy(swv[:].rearrange("p t n -> p (t n)"), bank(A[5])).then_inc(sv_c.h, 1)
                if q == 13:
                    rotate()
                if q >= STEP0:
                    step(q - STEP0)

            def branch(i, steps):
                for j in range(KD):
                    b = (NH + j) % 2
                    if steps is not None and j + steps < NITEMS // 2 + 2:
                        step(j + steps)
                    dve.wait_ge(pj_free[b].h, pj_free[b].at(lay, (NH + j) // 2 + 1) + i * 4)
                    dve.wait_ge(yb.h, yb.at(lay, j + 1) + i * 8)
                    if not (isinstance(i, int) and i == 0):
                        if not (isinstance(i, int) and i == 1 and j < 2):
                            dve.wait_ge(mg.h, mg.at(lay, j - 1 - 8) + i * 8)
                        v.tensor_tensor(term[:, j % 2, :], sig[:, j % 2, :], bank(A[5]), ALU.mult).then_inc(tm.h, 1)
                    else:
                        v.tensor_tensor(merged[:, j, :], sig[:, j % 2, :], bank(A[5]), ALU.mult).then_inc(tm.h, 1)

            branch(0, NH - STEP0)
            branch(1, NH - STEP0 + KD)
            with dve.Fori(2, 4) as i:
                branch(i, None)
            for k in range(KD):
                dve.wait_ge(m_h.h, m_h.at(lay, k + 1))
                v.tensor_tensor(uL[:, k, :], merged[:, k, :], uH[:, k, :].bitcast(f32), ALU.subtract).then_inc(m_l.h, 1)

            dve.wait_ge(h_in.h, h_in.at(lay, 16))
            def residual(c, t):
                q = NH + 32 + 4 * c + t
                bank_full(q)
                o = hs[:, t, c * 512:(c + 1) * 512]
                v.tensor_tensor(o, o, bank(q % 2), ALU.add).then_inc(pj_free[q % 2].h, 1)

            def ut_stored(t):
                if t >= 2:
                    dve.wait_ge(n_t.h, n_t.at(lay, NT + t - 1))
                    dve.wait_ge(u2o[t % 2].h, u2o[t % 2].at(lay, 16))

            for t in range(NT):
                residual(0, t)
            dve.wait_ge(g2_in.h, g2_in.at(lay, 16))
            for t in range(NT):
                residual(1, t)
                mean_square(lay, NT + t)
                norm_rows(lay, NT + t, g2, True, ut_stored)

            dve.wait_ge(rc_in.h, rc_in.at(lay, 48))
            dve.wait_ge(rl.h, rl.at(lay, NT))
            b2 = rb[:, ds(lay, 1), :].broadcast_to([P, NT, NG + NE])
            link(v.tensor_tensor(lg[:], bank(A[5], NT * 36).rearrange("p (t n) -> p t n", t=NT), b2, ALU.add))

            def over(x, n):
                return x.rearrange("p (t o) -> p t o", o=1).broadcast_to([P, NT, n])

            link(v.tensor_reduce(gm[:], lg[:, :, 0:NG], AX.X, ALU.max))
            v.tensor_tensor(gd[:], lg[:, :, 0:NG], over(gm[:], NG), ALU.subtract).then_inc(r_x.h, 1)
            dve.wait_ge(r_x.h, r_x.at(lay, 1))
            link(v.tensor_scalar(geq[:], gd[:], 0.0, None, ALU.is_equal))
            link(v.tensor_tensor(gp[:], geq[:], prio.rearrange("p (o g) -> p o g", o=1).broadcast_to([P, NT, NG]), ALU.mult))
            link(v.tensor_reduce(pm[:], gp[:], AX.X, ALU.max))
            link(v.tensor_tensor(oh[:], gp[:], over(pm[:], NG), ALU.is_equal))
            link(v.tensor_scalar(gidx[:], pm[:], -1.0, float(NG), ALU.mult, ALU.add))
            link(v.tensor_tensor(esel[:], lg[:, :, NG:].rearrange("p t (g e) -> p t g e", g=NG),
                                 oh[:].rearrange("p t (g o) -> p t g o", o=1).broadcast_to([P, NT, NG, EG]), ALU.mult))
            link(v.tensor_reduce(el[:], esel[:].rearrange("p t g e -> p t e g"), AX.X, ALU.add), alone=True)
            for t in range(NT):
                last = v.max(v8[:, t, :], el[:, t, :])
            link(last)
            v.tensor_tensor(dx[:], v8[:, :, 1], v8[:, :, 0], ALU.subtract).then_inc(r_x.h, 1)
            for t in range(NT):
                last = v.max_index(i8[:, t, :], v8[:, t, :], el[:, t, :])
            link(last)
            link(v.tensor_copy(idf[:], i8[:, :, 0:2]))
            link(v.scalar_tensor_tensor(eid[:], over(gidx[:], 2), float(EG), idf[:], ALU.mult, ALU.add))
            sel8 = sel[:].rearrange("p t c e -> p (t c) e")
            link(v.tensor_tensor(sel8, iota[:, 0:NE].rearrange("p (o e) -> p o e", o=1).broadcast_to([P, 2 * NT, NE]),
                                 eid[:].rearrange("p t (c o) -> p (t c) o", o=1).broadcast_to([P, 2 * NT, NE]), ALU.is_equal))
            v.memset(count[:, 0, :], 0.0)
            link(v.tensor_tensor(selM[:], sel[:, :, 0, :], sel[:, :, 1, :], ALU.add))
            link(v.tensor_copy(count[:, 1, :], selM[:, 0, :]))
            for t in range(1, NT):
                ins = v.tensor_tensor(count[:, t + 1, :], count[:, t, :], selM[:, t, :], ALU.add)
                if t < NT - 1:
                    link(ins)
                else:
                    ins.then_inc(r_m.h, 1)

            def over8(x, n):
                return x.rearrange("p (c o) -> p c o", o=1).broadcast_to([P, 8, n])

            e8 = eid[:].rearrange("p t c -> p (t c)")
            link(v.tensor_tensor(pair_of[:], sel8[:, :, 0:NP], sel8[:, :, NP:], ALU.add))
            v.tensor_copy(tok_rhs[:, :, 1, :], pair_of[:])
            v.tensor_tensor(tok_rhs[:, :, 0, :], pair_of[:], over8(val, NP), ALU.mult)
            v.tensor_scalar(x64[:], e8, float(NP), float(CAP), ALU.is_ge, ALU.mult)
            dve.wait_ge(r_r.h, r_r.at(lay, 1))
            link(v.tensor_tensor(rk[:], sel[:], bank(A[4], P).rearrange("p (t o e) -> p t o e", t=NT, o=1).broadcast_to([P, NT, 2, NE]),
                                 ALU.mult))
            v.tensor_reduce(most[:], bank(A[4], P + NE)[:, P:P + NE], AX.X, ALU.max)
            link(v.tensor_reduce(rank[:].rearrange("p (t c) -> p t c", t=NT), rk[:], AX.X, ALU.add))

            def choice_slots(chain):
                v.tensor_scalar(out_of[:], rank[:], float(CAP), 1024.0, ALU.is_ge, ALU.mult)
                v.tensor_scalar(below[:], rank[:], 0.0, 1024.0, ALU.is_lt, ALU.mult)
                chain(v.tensor_tensor(slot[:], rank[:], x64[:], ALU.add))
                chain(v.tensor_tensor(slot[:], slot[:], out_of[:], ALU.add))
                chain(v.scalar_tensor_tensor(slot[:], below[:], 2.0, slot[:], ALU.mult, ALU.add))
                return v.tensor_tensor(slot_of[:], iota[:, 0:P].rearrange("p (o i) -> p o i", o=1).broadcast_to([P, 8, P]),
                                       over8(slot[:], P), ALU.is_equal)

            def list_entries(chain):
                chain(v.tensor_scalar(empty[:], bank(A[4])[:, 256 + NP:256 + 2 * NP], -float(SENT), float(SENT), ALU.mult, ALU.add))
                chain(v.tensor_tensor(lists[:], bank(A[4])[:, 256:256 + NP], empty[:], ALU.add))
                chain(v.tensor_copy(toks[:], lists[:]))
                chain(v.tensor_scalar(toks[:], toks[:], 1, None, ALU.arith_shift_right))
                return v.tensor_copy(tokf[:], toks[:])

            choice_slots(link).then_inc(l_a.h, 1)
            dve.wait_ge(l_p.h, l_p.at(lay, 1))
            list_entries(link).then_inc(l_g.h, 1)
            dve.wait_ge(r_e.h, r_e.at(lay, 1))
            link(v.tensor_reduce(gs[:], ge[:], AX.X, ALU.add))
            link(v.reciprocal(gw[:], gs[:]))
            dve.wait_ge(r_e.h, r_e.at(lay, 2))
            link(v.tensor_scalar(ex1[:], ex[:], 1.0, None, ALU.add))
            link(v.reciprocal(rex[:], ex1[:]))
            link(v.tensor_tensor(wts[:, :, 0], rex[:], gw[:], ALU.mult))
            link(v.tensor_tensor(wts[:, :, 1], wts[:, :, 0], ex[:], ALU.mult))
            v.tensor_tensor(w_rhs[:], pair_of[:], over8(wts[:].rearrange("p t c -> p (t c)"), NP), ALU.mult).then_inc(l_b.h, 1)
            for x in range(1, NW):
                last = v.tensor_scalar(over_n[:, x - 1:x], most[:], float(x * CAP), None, ALU.is_gt)
            link(last)
            link(v.tensor_reduce(over_n[:, NW - 1:NW], over_n[:, 0:NW - 1], AX.X, ALU.add))
            link(v.tensor_tensor(extra[:, ds(lay + 1, 1)], over_n[:, NW - 1:NW], extra[:, ds(lay, 1)], ALU.add))
            v.tensor_copy(windows[:, 0, ds(lay + 1, 1)], extra[:, ds(lay + 1, 1)])
            v.tensor_copy(windows[:, 1, ds(lay, 1)], over_n[:, NW - 1:NW]).then_inc(win_n.h, 1)

            def slot_weights():
                return v.tensor_copy(slot_w[:], bank(A[4])[:, 384:384 + NP])

            dve.wait_ge(l_q.h, l_q.at(lay, 1))
            link(slot_weights())

            def rows_copy(i, y):
                dve.wait_ge(x_t.h, x_t.at(lay, y + 1) + i * 2)
                v.tensor_copy(xT[y][:, 512:1024], bank(A[3])).then_inc(x_cd.h, 1)

            def gated(col):
                return v.scalar_tensor_tensor(hid[:], silu[:], slot_w[:, col], bank(0)[:, FH:2 * FH], ALU.mult, ALU.mult)

            def out_low_rows(high, low):
                return v.tensor_tensor(low[:], ps[:, A[0] * 512:A[0] * 512 + 1024], high[:].bitcast(f32), ALU.subtract)

            def slot_tokens(to, col):
                return v.tensor_scalar(to[:], iota, tokf[:, col], None, ALU.is_equal)

            def add_rows(products, value, added):
                for x in range(8):
                    t, c = x // 2, x % 2
                    dve.wait_ge(products, value + x)
                    o = hs[:, t, c * 512:(c + 1) * 512]
                    v.tensor_tensor(o, o, bank((1, A[5])[x % 2]), ALU.add).then_inc(added, 1)

            def add_two(i):
                if not isinstance(i, int) or i:
                    dve.wait_ge(ca.h, ca.at(lay, 0) + i * 8)
                add_rows(cm.h, cm.at(lay, 1) + i * 8, ca.h)

            def pair(i, y, more, behind=True):
                p = i * 2 + y
                col = slice(p, p + 1) if isinstance(p, int) else ds(p, 1)
                dve.wait_ge(sl.h, sl.at(lay, y + 1) + i * 2)
                gated(col).then_inc(hd.h, 1)
                if more:
                    rows_copy(i + y, 1 - y)
                if behind:
                    add_two(i - 1)
                slot_tokens(tok_of[y], col).then_inc(t_of.h, 1)
                dve.wait_ge(y_h.h, y_h.at(lay, y + 1) + i * 2)
                out_low_rows(yH[y], yL[y]).then_inc(y_l.h, 1)

            dve.wait_ge(l_g.h, l_g.at(lay, 1))
            rows_copy(0, 0)
            pair(0, 0, True, behind=False)
            pair(0, 1, True, False)
            with dve.Fori(1, NP // 2 - 1) as i:
                pair(i, 0, True)
                pair(i, 1, True, behind=False)
            pair(NP // 2 - 1, 0, True)
            pair(NP // 2 - 1, 1, False, behind=False)

            def window_lists(n):
                count_ = [0]

                def chain(ins):
                    count_[0] += 1
                    ins.then_inc(ov_link, 1)
                    hold(dve, ov_link, n * WIN_LINKS + count_[0])

                chain(v.tensor_scalar(rank[:], rank[:], -float(CAP), None, ALU.add))
                choice_slots(chain).then_inc(ov_la, 1)
                hold(dve, ov_lp, n + 1)
                chain(slot_weights())
                list_entries(chain).then_inc(ov_lg, 1)
                hold(dve, ov_lg, n + 1)
                assert count_[0] == WIN_LINKS, count_

            def window_item(n, p):
                hold(dve, ov_s, n + 1)
                gated(ds(p, 1)).then_inc(ov_h, 1)
                slot_tokens(tok_w, ds(p, 1)).then_inc(ov_of, 1)
                hold(dve, ov_yh, n + 1)
                out_low_rows(yHw, yLw).then_inc(ov_yl, 1)
                hold(dve, ca.h, ca.at(lay, SUMS - 8))
                hold(dve, ov_ca, n * 8 + 2)
                add_rows(ov_cm, n * 8 + 1, ov_ca)

            before, own = window_range(dve, lay)
            later_windows(dve, before, own, window_lists, window_item)

            hold(dve, ov_ca, (before + own) * (NP * 8) + 2)
            add_two(NP // 2 - 1)
            assert links[0] == DVE_LINKS, links

        dve.wait_ge(g1_in.h, g1_in.at(L, 16))
        for t in range(NT):
            mean_square(L, t)
            dve.wait_ge(n_rs.h, n_rs.at(L, t + 1))
            if t >= 2:
                dve.wait_ge(s_out[t % 2].h, 16)
            v.scalar_tensor_tensor(ut[:, t % 2, :], hs[:, t, :], rstd[:, t:t + 1], g1[:], ALU.mult, ALU.mult).then_inc(fin.h, 1)

    return ctx


def tables():
    f = np.float32
    p = np.arange(P)
    ident = np.eye(P, dtype=f)
    wmask = np.where(np.concatenate([p[None, :] > p[:, None], p[None, :] <= p[:, None]], 1), 0.0, NEG).astype(f)
    gmask = ((p[:, None] <= p[None, :]) & (p[:, None] // CG == p[None, :] // CG)).astype(f)
    log_gamma = np.log1p(-np.exp2(-5.0 - np.arange(HEADS, dtype=np.float64)))
    head = p // DK
    cdec = np.exp(P * log_gamma)[head][:, None]
    small = np.zeros((P, 544), f)
    small[:, 0:128], small[:, 128:384], small[:, 384:512] = ident, wmask, gmask
    small[:, 512:513] = cdec
    small[:, 516:520] = np.arange(NG, 0, -1)
    small[:, 520:536] = -0.5
    half = DK // 2
    d = p % DK
    inv = (f(10000.0) ** (-np.arange(half, dtype=f) * f(2.0) / f(DK))).astype(f)
    ang = (np.arange(S, dtype=f)[None, :] * inv[d % half][:, None]).astype(f)
    rot = np.zeros((P, P), f)
    for m in range(P):
        if d[m] < half:
            rot[m + half, m] = -1.0
        else:
            rot[m - half, m] = 1.0
    idx = np.arange(P, dtype=np.float64)
    rel = idx[None, :] - idx[:, None]
    sc = DK ** -0.5
    dm = np.where(rel[:, None, :] >= 0, np.exp(np.maximum(rel, 0)[:, None, :] * log_gamma[None, :, None]), 0.0) * sc
    qd = np.exp((idx + 1)[None, :] * log_gamma[head][:, None])
    kd = np.exp((P - 1 - idx)[None, :] * log_gamma[head][:, None]) * sc
    tabs = np.concatenate([np.cos(ang.astype(np.float64)), np.sin(ang.astype(np.float64)), dm.reshape(P, -1), qd, kd, rot], 1).astype(f)
    router = np.concatenate([(p[:, None] < p[None, :]), np.ones((P, P)), np.tile(np.arange(S), (P, 1)),
                             2 * (p[:, None] + np.arange(8)[None, :] // 2 * P) + np.arange(8)[None, :] % 2], 1).astype(f)
    return {"c_small": small, "c_tabs": tabs, "c_router": router}


def kernel(**inputs):
    import concourse.bacc as bacc
    from concourse.bass_utils import run_bass_kernel_spmd

    nc = bacc.Bacc("TRN2", target_bir_lowering=False, num_devices=1)
    host = {k: np.ascontiguousarray(x) for k, x in inputs.items()}
    host["c_next_gain"] = np.concatenate([host["ln1_g"][1:], host.pop("final_g")[None]], 0)
    host.update(tables())
    arrays, a = {}, {}
    for k, x in host.items():
        arrays[f"in_{k}"] = x
        a[k] = nc.dram_tensor(f"in_{k}", x.shape, mybir.dt.from_np(x.dtype), kind="ExternalInput").ap()
    out = nc.dram_tensor("out", (1, S, D), mybir.dt.float32, kind="ExternalOutput").ap()
    trunk(nc, a, out).close()
    r = run_bass_kernel_spmd(nc, [arrays], core_ids=[0])
    return r.results[0]["out"]
```

```python
import concourse.bass as bass
from concourse import mybir
from contextlib import ExitStack
import numpy as np

L, D, S, P = 2, 1024, 512, 128
NT, KD = S // P, D // P
HEADS, DK, DV, HD, CG = 4, 32, 64, 64, 64
NE, NG, EG, FH = 32, 4, 8, 256
NP = NE // 2
CAP, NW = 64, 8
SUMS = 8 * (NP // 2)
EPS = 1e-6
NEG = -1.0e30
COL = {"gq": 0, "gk": 128, "gv": 256, "gr": 512, "ga": 768, "sq": 784, "sk": 1040, "sv": 1168,
       "mq": 1296, "mk": 1552, "mv": 1808, "rq": 2064, "rk": 2192, "rv": 2320, "rg": 2576, "gate": 2832}
UNITS = [("gv", 256), ("ga", 128), ("gr", 256), ("gq", 256), ("sq", 256), ("sk", 256), ("rq", 256),
         ("rv", 256), ("rg", 256), ("mq", 256), ("mk", 256), ("mv", 256)]
U_GATE, U_OUT, U_ALL = 12, 28, 32
RING = 4
PLACE = (0, 2, 1, 3)
HALVES = [("R", 0, 0, "gv"), ("R", 0, 1, "gv"), ("T", 1, 0, "ga"), ("R", 2, 0, "gr"), ("R", 2, 1, "gr"),
          ("T", 3, 0, "gq"), ("T", 3, 128, "gk"), ("T", 4, 0, "sq"), ("T", 4, 128, "sq"), ("T", 5, 0, "sk"),
          ("T", 5, 128, "sv"), ("T", 6, 0, "rq"), ("T", 6, 128, "rk"), ("R", 7, 0, "rv"), ("R", 7, 1, "rv"),
          ("R", 8, 0, "rg"), ("R", 8, 1, "rg"), ("T", 9, 0, "mq"), ("T", 9, 128, "mq"), ("T", 10, 0, "mk"),
          ("T", 10, 128, "mk"), ("R", 11, 0, "mv"), ("R", 11, 1, "mv")]
NH = len(HALVES)
N_CST = NT + 8
NITEMS = 2 * HEADS * NT
STEP0 = 20
SENT = 1 << 20


class Sig:

    def __init__(self, handle, per_layer, credit=0):
        self.h, self.k, self.credit = handle, per_layer, credit

    def at(self, lay, n):
        return lay * self.k + (n + self.credit)


def used_at(u):
    if u < U_GATE:
        return max(2 * u + 1, 2)
    return NH + 2 * (u - U_GATE + 1) if u < U_OUT else NH + 32 + (4 if u < U_OUT + 2 else 8)


def item(n):
    win, h, t = n < NITEMS // 2, n % 16 // 8 * 2 + n % 2, n % 8 // 2
    k0 = max(t - 1, 0) if win else 0
    return win, h, t, k0, t + 1 - k0


def trunk(nc, a, out):
    f32, f32r, i32, u32 = mybir.dt.float32, mybir.dt.float32r, mybir.dt.int32, mybir.dt.uint32
    ALU, ACT, AX = mybir.AluOpType, mybir.ActivationFunctionType, mybir.AxisListType
    ds = bass.ds
    ctx = ExitStack()
    KB = 1024
    BASE = -(-nc.sbuf_base // 64) * 64

    def sb(name, shape, dt, off):
        return nc.alloc_sbuf_tensor_at(name, shape, dt, offset=BASE + int(off))

    h_dram = nc.dram_tensor("h_dram", (S, D), f32, kind="Internal").ap()
    x_dram = nc.dram_tensor("x_dram", (S, D), f32, kind="Internal").ap()

    R_U, R_RAW, R_RH, R_B, R_O, R_T1, R_T2, R_C = (x * KB for x in (0, 32, 64, 96, 112, 144, 176, 198))
    uH = sb("uH", [P, KD, S], f32r, R_U)
    uL = sb("uL", [P, KD, S], f32r, R_U + 16 * KB)
    raw = sb("raw", [P, RING, 2048], f32, R_RAW)
    ringL = sb("ringL", [P, RING, 2048], f32r, R_RAW)
    ringH = sb("ringH", [P, RING, 2048], f32r, R_RH)
    swq = sb("swq", [P, 2, S], f32, R_B)
    swk = sb("swk", [P, S], f32, R_B + 4 * KB)
    swv = sb("swv", [P, NT, P], f32, R_B + 6 * KB)
    tabs = sb("tabs", [P, 1920], f32, R_B + 8 * KB)
    cos, sin = tabs[:, 0:512], tabs[:, 512:1024]
    decay = tabs[:, 1024:1536].rearrange("p (h i) -> p h i", h=HEADS)
    qdec, kdec, rot = tabs[:, 1536:1664], tabs[:, 1664:1792], tabs[:, 1792:1920]
    w13 = sb("w13", [P, 4, 2, 2048], f32, R_RAW)
    w2 = [sb(f"w2_{x}", [P, 2, D], f32, off) for x, off in
          enumerate((R_B, R_B + 8 * KB, R_T1, R_T1 + 8 * KB))]
    oH = sb("oH", [P, 8, S], f32r, R_O)
    oL = sb("oL", [P, 8, S], f32r, R_O + 16 * KB)
    u2T = sb("u2T", [P, KD, S], f32, R_O)
    ut = sb("ut", [P, 2, D], f32, R_O + 16 * KB)
    junk = sb("junk", [P, D], f32, R_O + 24 * KB)
    qT = sb("qT", [P, S], f32, R_T1)
    kT = sb("kT", [P, S], f32, R_T1 + 2 * KB)
    k2T = sb("k2T", [P, S], f32, R_T1 + 4 * KB)
    bT = sb("bT", [P, S], f32, R_T1 + 6 * KB)
    k2 = sb("k2", [P, NT, P], f32, R_T1 + 8 * KB)
    vv = sb("vv", [P, NT, 256], f32, R_T1 + 10 * KB)
    zaT = sb("zaT", [16, S], f32, R_T1 + 6 * KB)
    sr = sb("sr", [P, NT, 256], f32, R_T1 + 14 * KB)
    attT = sb("attT", [P, HEADS, NT, P], f32, R_T1 + 18 * KB)
    prev = sb("prev", [P, 8, DV], f32, R_T1 + 26 * KB)
    on = sb("on", [P, NT, HEADS, DV], f32, R_T1 + 28 * KB)
    lga = sb("lga", [P, 2, S], f32, R_T1 + 28 * KB)
    g1 = sb("g1", [P, D], f32, R_T1 + 28 * KB)
    g2 = sb("g2", [P, D], f32, R_T1 + 24 * KB)
    merged = sb("merged", [P, KD, S], f32, R_T1)
    sig = sb("sig", [P, 2, S], f32, R_T1 + 16 * KB)
    term = sb("term", [P, 2, S], f32, R_T1 + 20 * KB)
    braw = [sb(f"braw{x}", [P, 512], f32, R_T1 + (24 + 4 * x) * KB) for x in range(2)]
    bL = [sb(f"bL{x}", [P, 512], f32r, R_T1 + (24 + 4 * x) * KB) for x in range(2)]
    bH = [sb(f"bH{x}", [P, 512], f32r, R_T1 + (26 + 4 * x) * KB) for x in range(2)]
    mq = sb("mq", [P, 2, S], f32, R_T2)
    mk = sb("mk", [P, 2, S], f32, R_T2 + 4 * KB)
    mv = sb("mv", [P, NT, 256], f32, R_T2 + 8 * KB)
    pr = sb("pr", [P, 2, S], f32, R_T2 + 12 * KB)
    prT = sb("prT", [P, 2, S], f32, R_T2 + 16 * KB)
    svT = prT[:, 0, :]
    hs = sb("hs", [P, NT, D], f32, R_T2)
    rc = sb("rc", [P, 776], f32, R_T2 + 16 * KB)
    upper, ones, iota, val = rc[:, 0:128], rc[:, 128:256], rc[:, 256:768], rc[:, 768:776]
    wr = sb("wr", [P, KD, NG + NE], f32, R_T2 + 19.5 * KB)
    xg = [sb(f"xg{x}", [P, D], f32, R_U + 4 * x * KB) for x in range(2)]
    xT = [sb(f"xT{x}", [P, D], f32, R_U + (8 + 4 * x) * KB) for x in range(2)]
    yH = [sb(f"yH{x}", [P, D], f32r, off) for x, off in enumerate((R_U + 16 * KB, R_O + 12 * KB))]
    yL = [sb(f"yL{x}", [P, D], f32r, off) for x, off in enumerate((R_U + 20 * KB, R_U + 28 * KB))]
    silu = sb("silu", [P, FH], f32, R_U + 24 * KB)
    hid = sb("hid", [P, FH], f32, R_U + 25 * KB)
    hT = sb("hT", [P, 2, P], f32, R_U + 26 * KB)
    tok_of = [sb(f"tok_of{x}", [P, S], f32r, R_O + 2 * x * KB) for x in range(2)]
    tok_w = sb("tok_w", [P, S], f32r, R_T2 + 19.5 * KB)
    yHw = sb("yHw", [P, D], f32r, R_O + 4 * KB)
    yLw = sb("yLw", [P, D], f32r, R_O + 8 * KB)
    slot_of = sb("slot_of", [P, 8, P], f32, R_O + 28 * KB)
    at = [R_C]

    def small(name, shape, dt=f32):
        n = int(np.prod(shape[1:])) * 4
        t = sb(name, shape, dt, at[0])
        at[0] += -(-n // 32) * 32
        return t

    cst = small("cst", [P, 544])
    ident, wmask, gmask = cst[:, 0:128], cst[:, 128:384], cst[:, 384:512]
    cdec, prio, nhalf = cst[:, 512:513], cst[:, 516:520], cst[:, 520:536]
    wa2 = small("wa2", [16, L, P])
    wa2s = small("wa2s", [16, P])
    ba = small("ba", [P, L])
    ng = small("ng", [P, L, 2, DV])
    sink = small("sink", [P, L, HEADS])
    nsink = small("nsink", [P, L, HEADS])
    rb = small("rb", [P, L, NG + NE])
    ss = small("ss", [P, 8]); ms = small("ms", [P, 8]); rstd = small("rstd", [P, 8])
    hss = small("hss", [P, HEADS, NT]); hms = small("hms", [P, 16]); hrs = small("hrs", [P, HEADS, NT])
    dec = small("dec", [P, 8])
    nm = small("nm", [P, 2]); nb = small("nb", [P, 2]); es = small("es", [P, 2]); den = small("den", [P, 2])
    den2 = small("den2", [P, 2]); rden = small("rden", [P, 2])
    lists = small("lists", [P, NP]); toks = small("toks", [P, NP], i32); tokf = small("tokf", [P, NP])
    slot_w = small("slot_w", [P, NP]); empty = small("empty", [P, NP])
    gi = [small(f"gi{x}", [P, 1], i32) for x in range(2)]
    wts = small("wts", [P, NT, 2])
    extra = small("extra", [P, L + 1])
    windows = small("windows", [P, 2, L + 1], i32)
    most = small("most", [P, 1]); over_n = small("over_n", [P, NW])
    rt = [R_T1 + 16 * KB]

    def rtmp(name, shape, dt=f32):
        n = int(np.prod(shape[1:])) * 4
        t = sb(name, shape, dt, rt[0])
        rt[0] += -(-n // 32) * 32
        return t

    lg = rtmp("lg", [P, NT, NG + NE])
    gm = rtmp("gm", [P, NT]); gd = rtmp("gd", [P, NT, NG]); ge = rtmp("ge", [P, NT, NG])
    gs = rtmp("gs", [P, NT]); gw = rtmp("gw", [P, NT]); geq = rtmp("geq", [P, NT, NG])
    gp = rtmp("gp", [P, NT, NG]); pm = rtmp("pm", [P, NT]); oh = rtmp("oh", [P, NT, NG])
    gidx = rtmp("gidx", [P, NT]); esel = rtmp("esel", [P, NT, NG, EG]); el = rtmp("el", [P, NT, EG])
    v8 = rtmp("v8", [P, NT, 8]); i8 = rtmp("i8", [P, NT, 8], u32); dx = rtmp("dx", [P, NT])
    ex = rtmp("ex", [P, NT]); ex1 = rtmp("ex1", [P, NT]); rex = rtmp("rex", [P, NT])
    idf = rtmp("idf", [P, NT, 2]); eid = rtmp("eid", [P, NT, 2])
    x64 = rtmp("x64", [P, 8]); out_of = rtmp("out_of", [P, 8]); below = rtmp("below", [P, 8]); slot = rtmp("slot", [P, 8])
    pair_of = rtmp("pair_of", [P, 8, NP]); tok_rhs = rtmp("tok_rhs", [P, 8, 2, NP]); w_rhs = rtmp("w_rhs", [P, 8, NP])
    count = rtmp("count", [P, NT + 1, NE])
    sel = rtmp("sel", [P, NT, 2, NE]); selM = rtmp("selM", [P, NT, NE])
    rk = rtmp("rk", [P, NT, 2, NE]); rank = rtmp("rank", [P, 8])
    assert rt[0] <= R_T1 + 28 * KB and BASE + at[0] <= nc.sbuf_usable_end, (at[0], rt[0])

    ps = ctx.enter_context(nc.psum_tensor("ps", [P, 8 * 512], f32))

    def bank(b, n=512):
        return ps[:, b * 512:b * 512 + n]

    A = [2, 3, 4, 5, 6, 7]

    def signal(name, per_layer, credit=0):
        return Sig(ctx.enter_context(nc.semaphore(name)), per_layer, credit)

    s_cst = signal("s_cst", 0)
    s_init = signal("s_init", 0)
    w_in_slot = [signal(f"w_in_slot{s}", 16 * 8) for s in range(RING)]
    unit_high = signal("unit_high", U_ALL)
    unit_low = signal("unit_low", U_ALL)
    branch_in = [signal(f"branch_in{x}", 16 * 8) for x in range(2)]
    branch_high = signal("branch_high", 16)
    branch_low = signal("branch_low", 16)
    w13_in = [signal(f"w13_in{x}", 32 * 8) for x in range(4)]
    w2_in = [signal(f"w2_in{x}", 16 * 8) for x in range(4)]
    tabs_in = signal("tabs_in", 16)
    g1_in = signal("g1_in", 16)
    g2_in = signal("g2_in", 16)
    rc_in = signal("rc_in", 16 * 3)
    h_out = signal("h_out", 16)
    h_in = signal("h_in", 16)
    squares_summed = signal("squares_summed", 8, 1); mean_ready = signal("mean_ready", 8); scale_ready = signal("scale_ready", 8); rows_normed = signal("rows_normed", 8)
    rows_turned = signal("rows_turned", 8); rows_high = signal("rows_high", 8); rows_low = signal("rows_low", 4)
    bank_filled = signal("bank_filled", NH + 40)
    NB0, NB1 = (NH + 1) // 2, NH // 2
    bank_freed = [signal("bank_freed0", NB0 + 20), signal("bank_freed1", NB1 + 20)]
    sv_t = signal("sv_t", 1); sv_c = signal("sv_c", 1)
    lowrank_ready = signal("lowrank_ready", 1)
    decay_arg = signal("decay_arg", 1)
    decay_log = signal("decay_log", 1); decay_sum = signal("decay_sum", 1); decay_rest = signal("decay_rest", 1); decay_exps = signal("decay_exps", 4)
    rotate_filled = signal("rotate_filled", 2); rotary_done = signal("rotary_done", 1)
    att_cleared = signal("att_cleared", 1)
    att_filled = signal("att_filled", 8); att_masked = signal("att_masked", 8)
    keys_turned = signal("keys_turned", 2); keys_copied = signal("keys_copied", 2); kv_filled = signal("kv_filled", 2); states_ready = signal("states_ready", 2)
    gains_ready = signal("gains_ready", 2)
    mix_filled = signal("mix_filled", 8); mix_squares = signal("mix_squares", 8); mix_means = signal("mix_means", 2); mix_scales = signal("mix_scales", 2)
    mix_scaled = signal("mix_scaled", 8); mix_normed = signal("mix_normed", 2); mix_turned = signal("mix_turned", 4); mix_high = signal("mix_high", 4)
    mix_low = signal("mix_low", 4)
    scores_filled = signal("scores_filled", NITEMS); scores_bias = signal("scores_bias", NITEMS); probs_raw = signal("probs_raw", NITEMS)
    probs_ready = signal("probs_ready", NITEMS); probs_turned = signal("probs_turned", NITEMS)
    probs_copied_a = signal("probs_copied_a", NITEMS // 2); probs_copied_d = signal("probs_copied_d", NITEMS // 2)
    attn_filled = signal("attn_filled", 4); attn_high = signal("attn_high", 4); attn_low = signal("attn_low", 4)
    branch_filled = signal("branch_filled", 32, 4); term_ready = signal("term_ready", 32)
    term_added = signal("term_added", 24)
    merged_high = signal("merged_high", 8); merged_low = signal("merged_low", 8)
    u2_stored = [signal(f"u2_stored{x}", 16 * 2) for x in range(2)]
    logits_filled = signal("logits_filled", NT)
    router_exps = signal("router_exps", 2); router_args = signal("router_args", 2); choices_ready = signal("choices_ready", 1); ranks_filled = signal("ranks_filled", 1)
    slots_ready = signal("slots_ready", 1); list_filled = signal("list_filled", 1); list_weights_ready = signal("list_weights_ready", 1); list_weights_filled = signal("list_weights_filled", 1)
    rows_zeroed = signal("rows_zeroed", 2); lists_ready = signal("lists_ready", 1)
    rows_in = [signal(f"rows_in{x}", 16 * 8) for x in range(2)]
    x_turned = signal("x_turned", NP); x_copied_a = signal("x_copied_a", NP); x_copied_d = signal("x_copied_d", NP)
    up_filled = signal("up_filled", NP, 2); silu_ready = signal("silu_ready", NP); hidden_ready = signal("hidden_ready", NP); hidden_turned = signal("hidden_turned", NP)
    hidden_copied = signal("hidden_copied", NP); down_filled = signal("down_filled", NP)
    out_high = signal("out_high", NP); out_low_ready = signal("out_low_ready", NP); tokens_ready = signal("tokens_ready", NP)
    sum_filled = signal("sum_filled", SUMS); sum_added = signal("sum_added", SUMS, 10)
    win_n = signal("win_n", 1)
    win_weights, win_rows, win_turned, win_columns, win_up, win_silu, win_hidden, win_hidden_t, win_hidden_c, win_down, win_index = (
        ctx.enter_context(nc.semaphore(f"win_{x}")) for x in
        ("weights", "rows", "transposed", "columns", "up_filled", "silu", "hidden", "hidden_t", "hidden_c", "down", "index"))
    win_out_h, win_out_l, win_tokens, win_sum, win_added = (ctx.enter_context(nc.semaphore(f"win_{x}")) for x in
                                         ("out_h", "out_l", "tokens", "product", "added"))
    win_slots, win_list_filled, win_lists, win_link = (ctx.enter_context(nc.semaphore(f"win_{x}")) for x in
                                    ("slots", "lists_product", "lists", "link"))
    s_out = [signal(f"s_out{x}", 0) for x in range(2)]
    fin = signal("fin", 0)
    tmc = lambda t: slice(t * P, (t + 1) * P)

    block = ctx.enter_context(nc.Block())
    DVE_LINKS, ACT_LINKS, WIN_LINKS = 165, 2, 9
    dve_c = signal("dve_c", DVE_LINKS)
    act_c = signal("act_c", ACT_LINKS)
    index_copied = signal("index_copied", NP)

    def w_in_cols(l, c0, n):
        return a["w_in"][ds(l, 1), :, c0:c0 + n].rearrange("o (k p) n -> p (o k) n", p=P)

    held = ctx.enter_context(nc.semaphore("held"))

    def wait(eng, s, value):
        eng.wait_ge(s, value)

    def hold(eng, s, value):
        eng.wait_ge(s, value).then_inc(held, 1)

    def window_range(eng, lay):
        hold(eng, win_n.h, win_n.at(lay, 1))
        return (eng.value_load(windows[0:1, 0, ds(lay, 1)], min_val=0, max_val=(NW - 1) * L),
                eng.value_load(windows[0:1, 1, ds(lay, 1)], min_val=0, max_val=NW - 1))

    def later_windows(eng, before, own, lists_, item_):
        with eng.If(own):
            with eng.Fori(0, own) as w:
                if lists_ is not None:
                    lists_(before + w)
                with eng.Fori(0, NP) as p:
                    item_((before + w) * NP + p, p)

    @block.sync
    def _(sp):
        for t in range(NT):
            sp.dma_start(hs[:, t, :], a["x"][0, t * P:(t + 1) * P, :]).then_inc(s_cst.h, 16)
        for dst, src in ((cst[:], a["c_small"]), (wa2[:], a["gla_w_a2"].rearrange("l r n -> r l n")),
                         (ba[:], a["gla_b_a"].rearrange("l n -> n l")),
                         (ng[:, :, 0, :], a["gla_norm_g"].partition_broadcast(P)),
                         (ng[:, :, 1, :], a["ret_norm_g"].partition_broadcast(P)),
                         (sink[:], a["swa_sinks"].partition_broadcast(P)),
                         (rb[:, :, 0:NG], a["b_group"].partition_broadcast(P)),
                         (rb[:, :, NG:], a["b_expert"].partition_broadcast(P))):
            sp.dma_start(dst, src, allow_slow_non_contiguous=True).then_inc(s_cst.h, 16)
        sp.dma_start(g1[:], a["ln1_g"][0:1, :].partition_broadcast(P)).then_inc(g1_in.h, 16)
        with sp.Fori(0, L) as lay:

            def fill(u, src, dst=None):
                if u < RING:
                    hold(sp, up_filled.h, up_filled.at(lay, u // 2 - 1))
                else:
                    hold(sp, bank_filled.h, bank_filled.at(lay, used_at(u - RING)))
                sp.dma_start(dst, src).then_inc(w_in_slot[u % RING].h, 16)

            for u, (name, n) in enumerate(UNITS):
                slot = raw[:, u % RING, 0:KD * n].rearrange("p (k n) -> p k n", k=KD)
                fill(u, w_in_cols(lay, COL[name], n), slot)
                if u == 3:
                    hold(sp, s_cst.h, 16 * N_CST)
                    hold(sp, sum_added.h, sum_added.at(lay, 0))
                    sp.dma_start(h_dram.rearrange("(t p) n -> p t n", p=P), hs[:]).then_inc(h_out.h, 16)
                if u == 4:
                    sp.dma_start(tabs[:], a["c_tabs"]).then_inc(tabs_in.h, 16)

            def gate_fill(g, u):
                slot = raw[:, u % RING, :].rearrange("p (k n) -> p k n", k=KD)
                hold(sp, bank_filled.h, bank_filled.at(lay, used_at(u - RING)) if isinstance(g, int) else bank_filled.at(lay, NH - 2 * (RING - 1)) + g * 2)
                src = a["w_in"][ds(lay, 1), :, ds(g * 256 + COL["gate"], 256)].rearrange("o (k p) n -> p (o k) n", p=P)
                sp.dma_start(slot, src).then_inc(w_in_slot[u % RING].h, 16)

            def bfill(i, c):
                hold(sp, branch_filled.h, branch_filled.at(lay, 2 * c - 2) + i * 8)
                src = a["w_branch"][ds(lay, 1), ds(i, 1), :, c * 256:(c + 1) * 256].rearrange("o q (k p) n -> p (o q k) n", p=P)
                sp.dma_start(braw[c % 2][:].rearrange("p (k n) -> p k n", k=2), src).then_inc(branch_in[c % 2].h, 16)

            def out_fill(u):
                slot = raw[:, u % RING, :].rearrange("p (k n) -> p k n", k=KD)
                c0 = (u - U_OUT) * 256
                fill(u, a["w_out"][ds(lay, 1), :, c0:c0 + 256].rearrange("o (k p) n -> p (o k) n", p=P), slot)

            gate_fill(0, U_GATE)
            gate_fill(1, U_GATE + 1)
            for c in range(4):
                gate_fill(c + 2, U_GATE + c + 2)
                bfill(0, c)
            with sp.Fori(1, 3) as i:
                for c in range(4):
                    gate_fill(i * 4 + (c + 2), U_GATE + c + 2)
                    bfill(i, c)
            hold(sp, attn_low.h, attn_low.at(lay, 2))

            def w2_fill(i, r):
                src = a["w2"][ds(lay, 1), ds(i * 2 + (r // 2 + NP * (r % 2)), 1)].rearrange("o q (k p) n -> p (o q k) n", p=P)
                sp.dma_start(w2[r][:], src).then_inc(w2_in[r].h, 16)

            def w13_fill(i, r):
                for m, name in enumerate(("w1", "w3")):
                    src = a[name][ds(lay, 1), ds(i * 2 + (r // 2 + NP * (r % 2)), 1)].rearrange("o q (p k) n -> p (o q k n)", k=KD)
                    sp.dma_start(w13[:, PLACE[r], m, :], src).then_inc(w13_in[r].h, 16)

            w2_fill(0, 0)
            w2_fill(0, 1)
            for c in range(4):
                if c < 2:
                    gate_fill(14 + c, U_GATE + 14 + c)
                else:
                    out_fill(U_OUT + c - 2)
                bfill(3, c)
            out_fill(U_OUT + 2)
            sp.dma_start(hs[:], h_dram.rearrange("(t p) n -> p t n", p=P)).then_inc(h_in.h, 16)
            sp.dma_start(rc[:], a["c_router"]).then_inc(rc_in.h, 16)
            sp.dma_start(wr[:, :, 0:NG], a["w_group"][ds(lay, 1)].rearrange("o (p k) n -> p (o k) n", k=KD)).then_inc(rc_in.h, 16)
            sp.dma_start(wr[:, :, NG:], a["w_expert"][ds(lay, 1)].rearrange("o (p k) n -> p (o k) n", k=KD)).then_inc(rc_in.h, 16)
            out_fill(U_OUT + 3)
            hold(sp, branch_filled.h, branch_filled.at(lay, 32))
            sp.dma_start(g2[:], a["ln2_g"][ds(lay, 1), :].partition_broadcast(P)).then_inc(g2_in.h, 16)

            hold(sp, bank_filled.h, bank_filled.at(lay, used_at(U_OUT + 1)))
            w13_fill(0, 0)
            w13_fill(0, 1)
            hold(sp, merged_low.h, merged_low.at(lay, KD))
            w2_fill(0, 2)
            w2_fill(0, 3)
            hold(sp, bank_filled.h, bank_filled.at(lay, used_at(U_OUT + 3)))
            w13_fill(0, 2)
            w13_fill(0, 3)
            with sp.Fori(1, NP // 2) as i:
                for y in range(2):
                    hold(sp, up_filled.h, up_filled.at(lay, y - 1) + i * 2)
                    w13_fill(i, 2 * y)
                    w13_fill(i, 2 * y + 1)
                    hold(sp, down_filled.h, down_filled.at(lay, y - 1) + i * 2)
                    w2_fill(i, 2 * y)
                    w2_fill(i, 2 * y + 1)

            def window_weights(n, p):
                hold(sp, down_filled.h, down_filled.at(lay, NP))
                hold(sp, win_down, n + 1)
                for x in range(2):
                    for m, name in enumerate(("w1", "w3")):
                        src = a[name][ds(lay, 1), ds(p + NP * x, 1)].rearrange("o q (p k) n -> p (o q k n)", k=KD)
                        sp.dma_start(w13[:, PLACE[x], m, :], src).then_inc(win_weights, 16)
                    src = a["w2"][ds(lay, 1), ds(p + NP * x, 1)].rearrange("o q (k p) n -> p (o q k) n", p=P)
                    sp.dma_start(w2[x][:], src).then_inc(win_weights, 16)

            before, own = window_range(sp, lay)
            later_windows(sp, before, own, None, window_weights)
            hold(sp, win_down, (before + own) * NP + 1)
            hold(sp, rows_normed.h, rows_normed.at(lay, 8))
            sp.dma_start(g1[:], a["c_next_gain"][ds(lay, 1), :].partition_broadcast(P)).then_inc(g1_in.h, 16)
        hold(sp, h_out.h, 16 * L)
        for t in range(NT):
            hold(sp, fin.h, t + 1)
            sp.dma_start(out[0, t * P:(t + 1) * P, :], ut[:, t % 2, :]).then_inc(s_out[t % 2].h, 16)
        for x in range(2):
            hold(sp, s_out[x].h, 16 * NT // 2)


    @block.tensor
    def _(pe):
        mm = nc.tensor.matmul

        def mm3(o, h, l, rh, rl_, first, last):
            mm(o, h, rh, start=first, stop=False)
            mm(o, h, rl_, start=False, stop=False)
            return mm(o, l, rh, start=False, stop=last)

        pe.wait_ge(s_cst.h, 16 * N_CST)
        with pe.Fori(0, L) as lay:

            def norm_transposes(n, dst_free):
                t = n % NT
                b = A[0] if t % 2 == 0 else A[2]
                pe.wait_ge(rows_normed.h, rows_normed.at(lay, n + 1))
                if t >= 2:
                    pe.wait_ge(dst_free.h, dst_free.at(lay, n - 1))
                for k in range(KD):
                    last = nc.tensor.transpose(ps[:, b * 512 + k * P:b * 512 + (k + 1) * P],
                                               ut[:, t % 2, k * P:(k + 1) * P], ident)
                last.then_inc(rows_turned.h, 1)

            norm_transposes(0, rows_low)
            norm_transposes(1, rows_low)

            def half(q):
                kind, u, off, name = HALVES[q]
                s, b = u % RING, q % 2
                n = UNITS[u][1]
                wH = ringH[:, s, 0:KD * n].rearrange("p (k n) -> p k n", k=KD)
                wL = ringL[:, s, 0:KD * n].rearrange("p (k n) -> p k n", k=KD)
                pe.wait_ge(unit_low.h, unit_low.at(lay, u + 1))
                if q >= 2:
                    pe.wait_ge(bank_freed[b].h, bank_freed[b].at(lay, q // 2))
                if kind == "T":
                    for k in range(KD):
                        last = mm3(bank(b), wH[:, k, off:off + P], wL[:, k, off:off + P], uH[:, k, :], uL[:, k, :],
                                   k == 0, k == KD - 1)
                else:
                    for i in range(2):
                        if q < 2:
                            if 1 <= 2 * q + i < NT - 1:
                                norm_transposes(2 * q + i + 1, rows_low)
                            hold(pe, rows_low.h, rows_low.at(lay, 2 * q + i + 1))
                        for k in range(KD):
                            last = mm3(ps[:, b * 512 + i * n:b * 512 + (i + 1) * n], uH[:, k, tmc(2 * off + i)],
                                       uL[:, k, tmc(2 * off + i)], wH[:, k, :], wL[:, k, :], k == 0, k == KD - 1)
                last.then_inc(bank_filled.h, 1)

            def log_decay():
                pe.wait_ge(bank_freed[0].h, bank_freed[0].at(lay, 2))
                pe.wait_ge(lowrank_ready.h, lowrank_ready.at(lay, 1))
                mm(bank(A[0]), wa2s[:], zaT[:], start=True, stop=True).then_inc(decay_arg.h, 1)

            def scores(br):
                if br == 0:
                    pe.wait_ge(bank_freed[0].h, bank_freed[0].at(lay, 4))
                else:
                    pe.wait_ge(rotary_done.h, rotary_done.at(lay, 1))
                for t in range(NT):
                    for h in range(HEADS):
                        r = slice(DK * h, DK * (h + 1))
                        last = mm(ps[:, A[h] * 512 + t * P:A[h] * 512 + (t + 1) * P], kT[r, tmc(t)], qT[r, tmc(t)],
                                  start=True, stop=True)
                        if t == NT - 1:
                            last.then_inc(att_filled.h, 1)
                if br:
                    pe.wait_ge(mix_low.h, mix_low.at(lay, 2))
                for t in range(NT):
                    last = nc.tensor.transpose(ps[:, A[4] * 512 + t * P:A[4] * 512 + (t + 1) * P], k2T[:, tmc(t)], ident)
                last.then_inc(keys_turned.h, 1)

            def chunk_kv(br):
                hold(pe, keys_copied.h, keys_copied.at(lay, br + 1))
                if br:
                    pe.wait_ge(bank_freed[0].h, bank_freed[0].at(lay, 8))
                for n in range(8 if br == 0 else NT):
                    b = A[4] if br == 0 and n % 2 else A[5]
                    r = slice(CG * (n % 2), CG * (n % 2 + 1)) if br == 0 else slice(0, P)
                    t = n // 2 if br == 0 else n
                    for h in range(HEADS):
                        last = mm(ps[DK * h:DK * (h + 1), b * 512 + n * DV:b * 512 + (n + 1) * DV],
                                  k2[r, t, DK * h:DK * (h + 1)], vv[r, t, DV * h:DV * (h + 1)], start=True, stop=True)
                last.then_inc(kv_filled.h, 1)

            def mix_out(br):
                pe.wait_ge(states_ready.h, states_ready.at(lay, br + 1))
                pe.wait_ge(att_masked.h, att_masked.at(lay, 4 * br + 4))
                r4 = [slice(DK * h, DK * (h + 1)) for h in range(HEADS)]
                qi = qT if br == 0 else bT
                for t in range(NT):
                    o = [ps[:, A[h] * 512 + t * DV:A[h] * 512 + (t + 1) * DV] for h in range(HEADS)]
                    for c in ((2 * t, 2 * t + 1) if br == 0 else (t,)):
                        for h in range(HEADS):
                            if br == 0:
                                half_rows = slice(CG * (c % 2), CG * (c % 2 + 1))
                                mm(o[h][half_rows], qi[r4[h], CG * c:CG * (c + 1)], prev[r4[h], c, :], start=True, stop=False,
                                   skip_group_check=True)
                            else:
                                mm(o[h], qi[r4[h], tmc(t)], prev[r4[h], t, :], start=True, stop=False, skip_group_check=True)
                    for h in range(HEADS):
                        last = mm(o[h], attT[:, h, t, :], vv[:, t, DV * h:DV * (h + 1)], start=False, stop=True,
                                  skip_group_check=True)
                        if t == NT - 1:
                            last.then_inc(mix_filled.h, 1)

            def window_values():
                pe.wait_ge(bank_freed[0].h, bank_freed[0].at(lay, 6))
                for t in range(NT):
                    last = nc.tensor.transpose(ps[:, A[5] * 512 + t * P:A[5] * 512 + (t + 1) * P], svT[:, tmc(t)], ident)
                last.then_inc(sv_t.h, 1)

            def out_transposes(br):
                if br == 0:
                    pe.wait_ge(sv_c.h, sv_c.at(lay, 1))
                pe.wait_ge(mix_normed.h, mix_normed.at(lay, br + 1))
                for hh in range(2):
                    for t in range(NT):
                        last = nc.tensor.transpose(ps[:, A[4 + hh] * 512 + t * P:A[4 + hh] * 512 + (t + 1) * P],
                                                   on[:, t, 2 * hh:2 * hh + 2, :].rearrange("p h e -> p (h e)"), ident)
                    last.then_inc(mix_turned.h, 1)

            def rotate():
                pe.wait_ge(bank_freed[0].h, bank_freed[0].at(lay, 7))
                pe.wait_ge(mix_scaled.h, mix_scaled.at(lay, 4))
                for x, src in enumerate((qT, kT)):
                    mm(bank(A[x]), rot, src[:], start=True, stop=True).then_inc(rotate_filled.h, 1)

            def step(s):
                if 2 <= s:
                    pair_ = (2 * s - 4, 2 * s - 3)
                    for n in pair_:
                        e = (probs_copied_a, probs_copied_d)[n % 2]
                        hold(pe, e.h, e.at(lay, n // 2 + 1))
                    if n % 8 == 1 and n > 1:
                        hold(pe, attn_low.h, attn_low.at(lay, n // 8))
                    if n == 1:
                        hold(pe, mix_low.h, mix_low.at(lay, 4))
                    for i in range(item(n)[4]):
                        for n in pair_:
                            win, h, t, k0, nk = item(n)
                            o = ps[HD * (h % 2):HD * (h % 2 + 1), A[4] * 512 + t * P:A[4] * 512 + (t + 1) * P]
                            v = swv[:, k0 + i, HD * (h // 2):HD * (h // 2 + 1)] if win else mv[:, k0 + i, HD * h:HD * (h + 1)]
                            last = mm(o, v, prT[:, n % 2, i * P:(i + 1) * P], start=i == 0, stop=i == nk - 1, skip_group_check=True)
                    if n % 8 == 7:
                        last.then_inc(attn_filled.h, 1)
                if 1 <= s <= NITEMS // 2:
                    for n in (2 * s - 2, 2 * s - 1):
                        nk = item(n)[4]
                        pe.wait_ge(probs_ready.h, probs_ready.at(lay, n + 1))
                        for i in range(nk):
                            last = nc.tensor.transpose(ps[:, A[2 + n % 2] * 512 + i * P:A[2 + n % 2] * 512 + (i + 1) * P],
                                                       pr[:, n % 2, i * P:(i + 1) * P], ident)
                        last.then_inc(probs_turned.h, 1)
                if s < NITEMS // 2:
                    if s == 0:
                        pe.wait_ge(mix_scaled.h, mix_scaled.at(lay, 8))
                    for n in (2 * s, 2 * s + 1):
                        win, h, t, k0, nk = item(n)
                        g = h // 2 if win else h % 2
                        r = slice(HD * g, HD * (g + 1))
                        keys = slice(k0 * P, (k0 + nk) * P)
                        q, k = (swq[r, h % 2, tmc(t)], swk[r, keys]) if win else (mq[r, h // 2, tmc(t)], mk[r, h // 2, keys])
                        mm(bank(A[n % 2], nk * P), q, k, start=True, stop=True).then_inc(scores_filled.h, 1)

            PIECES = {3: log_decay, 7: lambda: scores(0), 8: lambda: chunk_kv(0), 10: lambda: mix_out(0),
                      11: window_values, 12: lambda: out_transposes(0), 13: rotate, 15: lambda: scores(1), 16: lambda: chunk_kv(1),
                      18: lambda: mix_out(1), 20: lambda: out_transposes(1)}
            for q in range(NH):
                half(q)
                if q in PIECES:
                    PIECES[q]()
                if q >= STEP0:
                    step(q - STEP0)

            def branch(i, steps):
                for j in range(KD):
                    c, b = j // 2, (NH + j) % 2
                    wH, wL = (w[:, c, :].rearrange("p (k n) -> p k n", k=KD) for w in (ringH, ringL))
                    if j % 2 == 0:
                        pe.wait_ge(unit_low.h, unit_low.at(lay, U_GATE + c + 1) + i * 4)
                    pe.wait_ge(bank_freed[b].h, bank_freed[b].at(lay, (NH + j) // 2) + i * 4)
                    for k in range(KD):
                        last = mm3(bank(b), wH[:, k, ds((j % 2) * P, P)], wL[:, k, ds((j % 2) * P, P)],
                                   uH[:, k, :], uL[:, k, :], k == 0, k == KD - 1)
                    last.then_inc(bank_filled.h, 1)
                    if steps is not None and j + steps < NITEMS // 2 + 2:
                        step(j + steps)
                    if j == 0 and steps == NH - STEP0:
                        pe.wait_ge(mix_low.h, mix_low.at(lay, 4))
                    if j == 0 and steps == NH - STEP0 + KD:
                        pe.wait_ge(attn_low.h, attn_low.at(lay, 2))
                    if j == 0 and steps is None:
                        pe.wait_ge(attn_low.h, attn_low.at(lay, 4))
                    if j % 2 == 0:
                        pe.wait_ge(branch_low.h, branch_low.at(lay, c + 1) + i * 4)
                    if not (steps == NH - STEP0 and j == 0):
                        pe.wait_ge(term_ready.h, term_ready.at(lay, j) + i * 8)
                    cc = ds((j % 2) * P, P)
                    for k in range(2):
                        h, l = (w[c % 2][:].rearrange("p (k n) -> p k n", k=2)[:, k, cc] for w in (bH, bL))
                        rh, rl_ = ((w[:, ds(i * 2 + k, 1), :] if steps is None else w[:, i * 2 + k:i * 2 + k + 1, :]).rearrange("p a n -> p (a n)")
                                   for w in (oH, oL))
                        last = mm3(bank(A[5]), h, l, rh, rl_, k == 0, k == 1)
                    last.then_inc(branch_filled.h, 1)

            branch(0, NH - STEP0)
            branch(1, NH - STEP0 + KD)
            with pe.Fori(2, 4) as i:
                branch(i, None)

            def out_half(c, t):
                b = (NH + 32 + 4 * c + t) % 2
                pe.wait_ge(bank_freed[b].h, bank_freed[b].at(lay, (NH + 32 + 4 * c + t) // 2))
                if t == 0:
                    pe.wait_ge(unit_low.h, unit_low.at(lay, U_OUT + 2 * c + 2))
                for k in range(KD):
                    if c == 0 and t == 0:
                        pe.wait_ge(merged_low.h, merged_low.at(lay, k + 1))
                    rh, rl_ = (w[:, 2 * c:2 * c + 2, k * 256:(k + 1) * 256] for w in (ringH, ringL))
                    last = mm3(bank(b).rearrange("p (a n) -> p a n", a=2), uH[:, k, tmc(t)], uL[:, k, tmc(t)], rh, rl_,
                               k == 0, k == KD - 1)
                last.then_inc(bank_filled.h, 1)

            def transpose_2(t):
                norm_transposes(NT + t, rows_high)

            def route(t):
                if t == 0:
                    pe.wait_ge(rc_in.h, rc_in.at(lay, 48))
                pe.wait_ge(rows_high.h, rows_high.at(lay, NT + t + 1))
                for k in range(KD):
                    last = mm(ps[:, A[5] * 512 + t * 36:A[5] * 512 + (t + 1) * 36], u2T[:, k, tmc(t)], wr[:, k, :],
                              start=k == 0, stop=k == KD - 1, skip_group_check=True)
                last.then_inc(logits_filled.h, 1)

            for t in range(NT):
                out_half(0, t)
            for t in range(NT):
                out_half(1, t)
                if t >= 1:
                    transpose_2(t - 1)
                if t >= 2:
                    route(t - 2)
            route(NT - 2)
            transpose_2(NT - 1)
            route(NT - 1)

            pe.wait_ge(choices_ready.h, choices_ready.at(lay, 1))
            mm(bank(A[4], (NT + 1) * NE), ones, count[:].rearrange("p t e -> p (t e)"), start=True, stop=False,
               skip_group_check=True)
            mm(bank(A[4], P), upper, selM[:].rearrange("p t e -> p (t e)"), start=False, stop=True,
               skip_group_check=True).then_inc(ranks_filled.h, 1)

            def list_product(rhs, c0, n):
                for x in range(8):
                    last = mm(ps[:, A[4] * 512 + c0:A[4] * 512 + c0 + n], slot_of[:, x, :], rhs(x), start=x == 0, stop=x == 7,
                              skip_group_check=True)
                return last

            def list_tokens():
                return list_product(lambda x: tok_rhs[:, x].rearrange("p a e -> p (a e)"), 256, 2 * NP)

            def list_weights():
                return list_product(lambda x: w_rhs[:, x, :], 384, NP)

            pe.wait_ge(slots_ready.h, slots_ready.at(lay, 1))
            list_tokens().then_inc(list_filled.h, 1)

            def transpose_rows(src):
                for k in range(KD):
                    last = nc.tensor.transpose(ps[:, A[2] * 512 + k * P:A[2] * 512 + (k + 1) * P],
                                               src[:, k * P:(k + 1) * P], ident)
                return last

            def two_experts(o, lhs, rhs, first, last):
                for x in range(2):
                    r = slice(CAP * x, CAP * (x + 1))
                    ins = mm(o[r], lhs[:, r], rhs[x], start=first, stop=last, skip_group_check=True)
                return ins

            def up_product(b, x_t_, r0):
                for k in range(KD):
                    w = [w13[:, PLACE[r0 + x]].rearrange("p m (k n) -> p m k n", k=KD)[:, :, k, :] for x in range(2)]
                    last = two_experts(bank(b).rearrange("p (m n) -> p m n", m=2), x_t_[:, k * P:(k + 1) * P], w, k == 0, k == KD - 1)
                return last

            def transpose_hidden():
                for k in range(2):
                    last = nc.tensor.transpose(ps[:, A[4] * 512 + k * P:A[4] * 512 + (k + 1) * P], hid[:, k * P:(k + 1) * P], ident)
                return last

            def down_product(r0):
                for c in range(2):
                    for k in range(2):
                        w = [w2[r0 + x][:, k, c * 512:(c + 1) * 512] for x in range(2)]
                        last = two_experts(bank(A[c]), hT[:, k, :], w, k == 0, k == 1)
                return last

            def pair_rows(i, y):
                pe.wait_ge(rows_in[y].h, rows_in[y].at(lay, 16) + i * 16)
                transpose_rows(xg[y]).then_inc(x_turned.h, 1)

            def combine(parts, added, value):
                for x in range(8):
                    t, c = x // 2, slice(x % 2 * 512, (x % 2 + 1) * 512)
                    pe.wait_ge(added[0], value + x)
                    for m, (tokens, rows) in enumerate(parts):
                        last = mm(bank((1, A[5])[x % 2]), tokens[:, tmc(t)], rows[:, c], start=m == 0, stop=m == len(parts) - 1)
                    last.then_inc(added[1], 1)

            def combine_two(i):
                hold(pe, out_low_ready.h, out_low_ready.at(lay, 2) + i * 2)
                hold(pe, tokens_ready.h, tokens_ready.at(lay, 2) + i * 2)
                combine([(tok_of[y], w[y]) for y in range(2) for w in (yH, yL)], (sum_added.h, sum_filled.h), sum_added.at(lay, -1) + i * 8)

            def pair(i, y, more, behind=True):
                pe.wait_ge(x_copied_a.h, x_copied_a.at(lay, y + 1) + i * 2)
                pe.wait_ge(x_copied_d.h, x_copied_d.at(lay, y + 1) + i * 2)
                for x in range(2):
                    pe.wait_ge(w13_in[2 * y + x].h, w13_in[2 * y + x].at(lay, 32) + i * 32)
                up_product(0, xT[y], 2 * y).then_inc(up_filled.h, 1)
                if isinstance(i, int) and i == 0 and y == 0:
                    pe.wait_ge(list_weights_ready.h, list_weights_ready.at(lay, 1))
                    list_weights().then_inc(list_weights_filled.h, 1)
                if more:
                    pair_rows(i + y, 1 - y)
                if behind:
                    combine_two(i - 1)
                pe.wait_ge(hidden_ready.h, hidden_ready.at(lay, y + 1) + i * 2)
                transpose_hidden().then_inc(hidden_turned.h, 1)
                pe.wait_ge(hidden_copied.h, hidden_copied.at(lay, y + 1) + i * 2)
                for x in range(2):
                    pe.wait_ge(w2_in[2 * y + x].h, w2_in[2 * y + x].at(lay, 16) + i * 16)
                down_product(2 * y).then_inc(down_filled.h, 1)

            pair_rows(0, 0)
            pair(0, 0, True, behind=False)
            pair(0, 1, True, False)
            with pe.Fori(1, NP // 2 - 1) as i:
                pair(i, 0, True)
                pair(i, 1, True, behind=False)
            pair(NP // 2 - 1, 0, True)
            pair(NP // 2 - 1, 1, False, behind=False)

            def window_lists(n):
                hold(pe, win_slots, n + 1)
                list_tokens()
                list_weights().then_inc(win_list_filled, 1)

            def window_item(n, p):
                hold(pe, sum_added.h, sum_added.at(lay, SUMS - 8))
                hold(pe, win_rows, n * 16 + 16)
                hold(pe, win_columns, n + 1)
                transpose_rows(xg[0]).then_inc(win_turned, 1)
                hold(pe, win_weights, n * 96 + 96)
                hold(pe, win_columns, n + 2)
                up_product(0, xT[0], 0).then_inc(win_up, 1)
                hold(pe, win_hidden, n + 1)
                transpose_hidden().then_inc(win_hidden_t, 1)
                hold(pe, out_low_ready.h, out_low_ready.at(lay, NP))
                hold(pe, win_hidden_c, n + 1)
                down_product(0).then_inc(win_down, 1)
                hold(pe, win_out_l, n + 1)
                hold(pe, win_tokens, n + 1)
                combine([(tok_w, yHw), (tok_w, yLw)], (win_added, win_sum), n * 8 + 1)

            before, own = window_range(pe, lay)
            later_windows(pe, before, own, window_lists, window_item)
            hold(pe, win_added, (before + own) * (NP * 8) + 2)
            combine_two(NP // 2 - 1)

    @block.scalar
    def _(act):
        fn = nc.scalar.activation
        act.wait_ge(s_cst.h, 16 * N_CST)

        with act.Fori(0, L) as lay:
            links = [0]

            def act_link(ins):
                links[0] += 1
                ins.then_inc(act_c.h, 1)
                act.wait_ge(act_c.h, act_c.at(lay, links[0]))

            def split_h(u):
                act.wait_ge(w_in_slot[u % RING].h, w_in_slot[u % RING].at(lay, 16 * (u // RING + 1)))
                n = 1024 if u == 1 else 2048
                fn(ringH[:, u % RING, 0:n], raw[:, u % RING, 0:n], ACT.Copy).then_inc(unit_high.h, 1)

            def bank_full(q):
                act.wait_ge(bank_filled.h, bank_filled.at(lay, q + 1))

            def copy_out(q, dst, func=ACT.Copy):
                bank_full(q)
                n = bank(q % 2) if dst.shape[0] == P else ps[0:16, (q % 2) * 512:(q % 2) * 512 + 512]
                fn(dst, n, func).then_inc(bank_freed[q % 2].h, 1)

            def squares(n, t, ready, value):
                act.wait_ge(ready.h, value)
                act.wait_ge(squares_summed.h, squares_summed.at(lay, n))
                fn(junk[:], hs[:, t, :], ACT.Square, accum_out=ss[:, n:n + 1]).then_inc(squares_summed.h, 1)

            def norm_h(t):
                act.wait_ge(rows_turned.h, rows_turned.at(lay, t + 1))
                b = A[0] if t % 2 == 0 else A[2]
                fn(uH[:, :, tmc(t)], ps[:, b * 512:b * 512 + 1024].rearrange("p (k n) -> p k n", k=KD), ACT.Copy)\
                    .then_inc(rows_high.h, 1)

            for t in range(NT):
                squares(t, t, sum_added, sum_added.at(lay, 2 * t - 6))
                if t % 2:
                    split_h(t // 2)
            for t in range(NT):
                norm_h(t)

            def k2_rows(br):
                act.wait_ge(keys_turned.h, keys_turned.at(lay, br + 1))
                fn(k2[:].rearrange("p t n -> p (t n)"), bank(A[4]), ACT.Copy).then_inc(keys_copied.h, 1)

            def head_squares(br):
                for h in range(HEADS):
                    act.wait_ge(mix_filled.h, mix_filled.at(lay, 4 * br + h + 1))
                    fn(on[:, :, h, :], bank(A[h], 256).rearrange("p (t e) -> p t e", t=NT), ACT.Square).then_inc(mix_squares.h, 1)

            def out_h(br):
                for hh in range(2):
                    act.wait_ge(mix_turned.h, mix_turned.at(lay, 2 * br + hh + 1))
                    fn(oH[:, (0, 6)[br] + hh, :], bank(A[4 + hh]), ACT.Copy).then_inc(mix_high.h, 1)

            def step(s):
                if 1 <= s <= NITEMS // 2:
                    n = 2 * s - 2
                    act.wait_ge(probs_turned.h, probs_turned.at(lay, n + 1))
                    nk = item(n)[4]
                    fn(prT[:, 0, 0:nk * P], bank(A[2], nk * P), ACT.Copy).then_inc(probs_copied_a.h, 1)
                if s - 2 in (3, 7, 11, 15):
                    m = (s - 2) // 4
                    act.wait_ge(attn_filled.h, attn_filled.at(lay, m + 1))
                    fn(oH[:, 2 + m, :], bank(A[4]), ACT.Copy).then_inc(attn_high.h, 1)
                if s < NITEMS // 2:
                    for n in (2 * s, 2 * s + 1):
                        win, h, t, k0, nk = item(n)
                        x = n % 2
                        hold(act, scores_bias.h, scores_bias.at(lay, n + 1))
                        if win:
                            fn(es[:, x:x + 1], sink[:, ds(lay, 1), h:h + 1].rearrange("p a b -> p (a b)"), ACT.Exp,
                               bias=nb[:, x:x + 1])
                        fn(pr[:, x, 0:nk * P], bank(A[x], nk * P), ACT.Exp, bias=nb[:, x:x + 1], scale=HD ** -0.5,
                           accum_out=den[:, x:x + 1]).then_inc(probs_raw.h, 1)

            for q in range(NH):
                kind, u, off, name = HALVES[q]
                if q == 0 or HALVES[q - 1][1] != u:
                    split_h(u + 2)
                if name == "ga":
                    fn(wa2s[:], wa2[:, ds(lay, 1), :].rearrange("p a n -> p (a n)"), ACT.Copy).then_inc(lowrank_ready.h, 1)
                    copy_out(q, zaT[:])
                elif name in ("gv", "rv"):
                    copy_out(q, vv[:, 2 * off:2 * off + 2, :].rearrange("p t n -> p (t n)"))
                elif name in ("gr", "rg"):
                    copy_out(q, sr[:, 2 * off:2 * off + 2, :].rearrange("p t n -> p (t n)"), ACT.Silu)
                elif q == 7:
                    bank_full(q)
                    fn(swq[0:HD, 0, :], bank(1)[0:HD], ACT.Copy)
                    fn(swq[0:HD, 1, :], bank(1)[HD:P], ACT.Copy).then_inc(bank_freed[1].h, 1)
                elif q == 9:
                    copy_out(q, swk[:])
                elif q == 11:
                    copy_out(q, qT[:])
                elif q == 12:
                    copy_out(q, kT[:])
                elif q == 17:
                    act.wait_ge(h_out.h, h_out.at(lay, 16))
                    copy_out(q, mq[:, 0, :])
                elif q == 19:
                    copy_out(q, mk[:, 0, :])
                elif q == 21:
                    copy_out(q, mv[:, 0:2, :].rearrange("p t n -> p (t n)"))
                if q == 3:
                    hold(act, decay_arg.h, decay_arg.at(lay, 1))
                    act_link(fn(lga[:, 0, :], bank(A[0]), ACT.Abs, bias=ba[:, ds(lay, 1)]))
                    act_link(fn(lga[:, 0, :], lga[:, 0, :], ACT.Exp, scale=-1.0))
                    fn(lga[:, 0, :], lga[:, 0, :], ACT.Ln, bias=1.0).then_inc(decay_log.h, 1)
                if q == 4:
                    act.wait_ge(decay_sum.h, decay_sum.at(lay, 1))
                    fn(qT[:], bT[:], ACT.Exp, scale=1.0 / 16).then_inc(decay_exps.h, 1)
                    fn(kT[:], bT[:], ACT.Exp, scale=-1.0 / 16).then_inc(decay_exps.h, 1)
                    fn(dec[:], bT[:].rearrange("p (n c) -> p n c", c=CG)[:, :, CG - 1], ACT.Exp, scale=1.0 / 16).then_inc(decay_exps.h, 1)
                    act.wait_ge(decay_rest.h, decay_rest.at(lay, 1))
                    fn(k2T[:], k2T[:], ACT.Exp, scale=1.0 / 16).then_inc(decay_exps.h, 1)
                if q in (7, 15):
                    k2_rows(q // 15)
                if q in (10, 18):
                    head_squares(q // 18)
                if q in (12, 20):
                    out_h(q // 20)
                if q >= STEP0:
                    step(q - STEP0)

            def branch(i, steps):
                for j in range(KD):
                    c, b = j // 2, (NH + j) % 2
                    if j % 2 == 0:
                        x = c % 2
                        act.wait_ge(branch_in[x].h, branch_in[x].at(lay, 16 * (c // 2 + 1)) + i * 32)
                        fn(bH[x][:], braw[x][:], ACT.Copy).then_inc(branch_high.h, 1)
                        s = (c + 2) % RING
                        act.wait_ge(w_in_slot[s].h, w_in_slot[s].at(lay, 16 * ((U_GATE + c + 2) // RING + 1)) + i * 16)
                        fn(ringH[:, s, :], raw[:, s, :], ACT.Copy).then_inc(unit_high.h, 1)
                    act.wait_ge(bank_filled.h, bank_filled.at(lay, NH + j + 1) + i * 8)
                    if not (isinstance(i, int) and i == 0 and j < 2):
                        act.wait_ge(term_ready.h, term_ready.at(lay, j - 1) + i * 8)
                    fn(sig[:, j % 2, :], bank(b), ACT.Sigmoid).then_inc(bank_freed[b].h, 1)
                    if steps is not None and j + steps < NITEMS // 2 + 2:
                        step(j + steps)

            branch(0, NH - STEP0)
            branch(1, NH - STEP0 + KD)
            with act.Fori(2, 4) as i:
                branch(i, None)
            act.wait_ge(bank_filled.h, bank_filled.at(lay, NH + 32))
            for k in range(KD):
                act.wait_ge(term_added.h, term_added.at(lay, 16 + k + 1))
                fn(uH[:, k, :], merged[:, k, :], ACT.Copy).then_inc(merged_high.h, 1)
            split_h(U_OUT + 2)
            split_h(U_OUT + 3)

            def norm_2(t):
                act.wait_ge(rows_turned.h, rows_turned.at(lay, NT + t + 1))
                b = A[0] if t % 2 == 0 else A[2]
                fn(u2T[:, :, tmc(t)], ps[:, b * 512:b * 512 + 1024].rearrange("p (k n) -> p k n", k=KD), ACT.Copy)\
                    .then_inc(rows_high.h, 1)

            for t in range(NT):
                q = NH + 36 + t
                squares(NT + t, t, bank_freed[q % 2], bank_freed[q % 2].at(lay, q // 2 + 1))
                if t:
                    norm_2(t - 1)
            norm_2(NT - 1)
            act.wait_ge(router_args.h, router_args.at(lay, 1))
            fn(ge[:].rearrange("p t g -> p (t g)"), gd[:].rearrange("p t g -> p (t g)"), ACT.Exp).then_inc(router_exps.h, 1)
            act.wait_ge(router_args.h, router_args.at(lay, 2))
            fn(ex[:], dx[:], ACT.Exp).then_inc(router_exps.h, 1)

            def rows_copy(i, y):
                act.wait_ge(x_turned.h, x_turned.at(lay, y + 1) + i * 2)
                fn(xT[y][:, 0:512], bank(A[2]), ACT.Copy).then_inc(x_copied_a.h, 1)

            def hidden_copy():
                return fn(hT[:].rearrange("p k n -> p (k n)"), bank(A[4], 256), ACT.Copy)

            def pair(i, y, more):
                act.wait_ge(up_filled.h, up_filled.at(lay, y + 1) + i * 2)
                fn(silu[:], bank(0, FH), ACT.Silu).then_inc(silu_ready.h, 1)
                if more:
                    rows_copy(i + y, 1 - y)
                act.wait_ge(hidden_turned.h, hidden_turned.at(lay, y + 1) + i * 2)
                hidden_copy().then_inc(hidden_copied.h, 1)
                act.wait_ge(down_filled.h, down_filled.at(lay, y + 1) + i * 2)
                fn(yH[y][:], ps[:, A[0] * 512:A[0] * 512 + 1024], ACT.Copy).then_inc(out_high.h, 1)

            rows_copy(0, 0)
            with act.Fori(0, NP // 2 - 1) as i:
                pair(i, 0, True)
                pair(i, 1, True)
            pair(NP // 2 - 1, 0, True)
            pair(NP // 2 - 1, 1, False)

            def window_item(n, p):
                hold(act, win_turned, n + 1)
                fn(xT[0][:], ps[:, A[2] * 512:A[2] * 512 + 1024], ACT.Copy).then_inc(win_columns, 1)
                hold(act, win_up, n + 1)
                fn(silu[:], bank(0, FH), ACT.Silu).then_inc(win_silu, 1)
                hold(act, win_hidden_t, n + 1)
                hidden_copy().then_inc(win_hidden_c, 1)
                hold(act, win_down, n + 2)
                fn(yHw[:], ps[:, A[0] * 512:A[0] * 512 + 1024], ACT.Copy).then_inc(win_out_h, 1)

            before, own = window_range(act, lay)
            later_windows(act, before, own, None, window_item)
        for t in range(NT):
            act.wait_ge(sum_added.h, sum_added.at(L, 2 * t - 6))
            act.wait_ge(squares_summed.h, squares_summed.at(L, t))
            fn(junk[:], hs[:, t, :], ACT.Square, accum_out=ss[:, t:t + 1]).then_inc(squares_summed.h, 1)

    @block.gpsimd
    def _(pool):
        gp_ = nc.gpsimd
        for s in (up_filled, branch_filled, sum_added, squares_summed):
            pool.sem_inc(s.h, s.credit)
        for s, n in ((win_columns, 1), (win_down, 1), (win_added, 2)):
            pool.sem_inc(s, n)
        hold(pool, s_cst.h, 16 * N_CST)

        with pool.Fori(0, L) as lay:

            def split_l(u):
                n = 1024 if u == 1 else 2048
                s = u % RING
                hold(pool, unit_high.h, unit_high.at(lay, u + 1))
                gp_.tensor_tensor(ringL[:, s, 0:n], raw[:, s, 0:n], ringH[:, s, 0:n].bitcast(f32), ALU.subtract).then_inc(unit_low.h, 1)

            def norm_scale(n):
                hold(pool, mean_ready.h, mean_ready.at(lay, n + 1))
                gp_.tensor_tensor(rstd[:, n:n + 1], ms[:, n:n + 1], nhalf[:, 0:1], ALU.pow).then_inc(scale_ready.h, 1)

            for t in range(NT):
                norm_scale(t)
                if t % 2:
                    split_l(t // 2)
            gp_.memset(attT[:].rearrange("p h t i -> p (h t i)"), 0.0).then_inc(att_cleared.h, 1)

            def gain(br):
                q = (4, 16)[br]
                hold(pool, bank_freed[0].h, bank_freed[0].at(lay, q // 2 + 1))
                hold(pool, bank_freed[1].h, bank_freed[1].at(lay, q // 2))
                g = ng[:, ds(lay, 1), br, :].rearrange("p a e -> p (a e)").rearrange("p (o e) -> p o e", o=1)
                v = sr[:].rearrange("p t (h e) -> p (t h) e", e=DV)
                gp_.tensor_tensor(v, v, g.broadcast_to([P, 16, DV]), ALU.mult).then_inc(gains_ready.h, 1)

            def head_scale(br):
                hold(pool, mix_means.h, mix_means.at(lay, br + 1))
                gp_.tensor_tensor(hrs[:].rearrange("p h t -> p (h t)"), hms[:], nhalf, ALU.pow).then_inc(mix_scales.h, 1)

            for q in range(NH):
                u = HALVES[q][1]
                if q == 0 or HALVES[q - 1][1] != u:
                    split_l(u + 2)
                if q in (4, 16):
                    gain(q // 16)
                if q in (10, 18):
                    head_scale(q // 18)

            def branch(i):
                for j in range(KD):
                    c = j // 2
                    if j % 2 == 0:
                        x, s = c % 2, (c + 2) % RING
                        hold(pool, branch_high.h, branch_high.at(lay, c + 1) + i * 4)
                        gp_.tensor_tensor(bL[x][:], braw[x][:], bH[x][:].bitcast(f32), ALU.subtract).then_inc(branch_low.h, 1)
                        hold(pool, unit_high.h, unit_high.at(lay, U_GATE + c + 3) + i * 4)
                        gp_.tensor_tensor(ringL[:, s, :], raw[:, s, :], ringH[:, s, :].bitcast(f32), ALU.subtract).then_inc(unit_low.h, 1)
                    if not (isinstance(i, int) and i == 0):
                        hold(pool, term_ready.h, term_ready.at(lay, j + 1) + i * 8)
                        gp_.tensor_tensor(merged[:, j, :], merged[:, j, :], term[:, j % 2, :], ALU.add).then_inc(term_added.h, 1)

            branch(0)
            with pool.Fori(1, 4) as i:
                branch(i)
            split_l(U_OUT + 2)
            split_l(U_OUT + 3)

            for t in range(NT):
                norm_scale(NT + t)
                hold(pool, rows_normed.h, rows_normed.at(lay, NT + t + 1))
                pool.dma_start(x_dram[t * P:(t + 1) * P, :], ut[:, t % 2, :]).then_inc(u2_stored[t % 2].h, 16)

            hold(pool, bank_filled.h, bank_filled.at(lay, NH + 40))
            for x in range(2):
                gp_.memset(xg[x][:], 0.0).then_inc(rows_zeroed.h, 1)
            for x in range(2):
                hold(pool, u2_stored[x].h, u2_stored[x].at(lay, 32))

            def gather(i, y):
                if not isinstance(i, int) or i:
                    hold(pool, x_turned.h, x_turned.at(lay, y - 1) + i * 2)
                    hold(pool, rows_in[y].h, rows_in[y].at(lay, 0) + i * 16)
                p = i * 2 + y
                gp_.tensor_copy(gi[y][:], toks[:, p:p + 1] if isinstance(p, int) else toks[:, ds(p, 1)]).then_inc(index_copied.h, 1)
                hold(pool, index_copied.h, index_copied.at(lay, y + 1) + i * 2)
                gp_.indirect_dma_start(xg[y][:], None, x_dram, bass.IndirectOffsetOnAxis(gi[y][:, 0:1], axis=0),
                                       bounds_check=S - 1, oob_is_err=False).then_inc(rows_in[y].h, 16)

            hold(pool, rows_zeroed.h, rows_zeroed.at(lay, 2))
            hold(pool, lists_ready.h, lists_ready.at(lay, 1))
            gather(0, 0)
            gather(0, 1)
            with pool.Fori(1, NP // 2) as i:
                for y in range(2):
                    gather(i, y)

            def window_lists(n):
                hold(pool, win_lists, n + 1)

            def window_rows(n, p):
                hold(pool, x_turned.h, x_turned.at(lay, NP))
                hold(pool, win_columns, n + 1)
                gp_.tensor_copy(gi[0][:], toks[:, ds(p, 1)]).then_inc(win_index, 1)
                hold(pool, win_index, n + 1)
                gp_.indirect_dma_start(xg[0][:], None, x_dram, bass.IndirectOffsetOnAxis(gi[0][:, 0:1], axis=0),
                                       bounds_check=S - 1, oob_is_err=False).then_inc(win_rows, 16)

            before, own = window_range(pool, lay)
            later_windows(pool, before, own, window_lists, window_rows)
        for t in range(NT):
            hold(pool, mean_ready.h, mean_ready.at(L, t + 1))
            gp_.tensor_tensor(rstd[:, t:t + 1], ms[:, t:t + 1], nhalf[:, 0:1], ALU.pow).then_inc(scale_ready.h, 1)

    @block.vector
    def _(dve):
        v = nc.vector
        dve.wait_ge(s_cst.h, 16 * N_CST)
        v.memset(extra[:], 0.0)
        v.memset(windows[:].rearrange("p a b -> p (a b)"), 0)
        v.tensor_scalar(nsink[:], sink[:], -1.0, None, ALU.mult).then_inc(s_init.h, 1)
        dve.wait_ge(s_init.h, 1)

        def norm_rows(lay, n, gain, permute, slot_free=None):
            t = n % NT
            dve.wait_ge(scale_ready.h, scale_ready.at(lay, n + 1))
            if slot_free is not None:
                slot_free(t)
            o = ut[:, t % 2, :]
            i = hs[:, t, :]
            g = gain[:]
            if permute:
                o = o.rearrange("p (k q) -> p q k", k=KD)
                i = i.rearrange("p (q k) -> p q k", k=KD)
                g = g.rearrange("p (q k) -> p q k", k=KD)
            v.scalar_tensor_tensor(o, i, rstd[:, n:n + 1], g, ALU.mult, ALU.mult).then_inc(rows_normed.h, 1)

        def mean_square(lay, n):
            dve.wait_ge(squares_summed.h, squares_summed.at(lay, n + 1))
            v.tensor_scalar(ms[:, n:n + 1], ss[:, n:n + 1], 1.0 / D, EPS, ALU.mult, ALU.add).then_inc(mean_ready.h, 1)

        with dve.Fori(0, L) as lay:
            links = [0]

            def link(ins, alone=False):
                links[0] += 1
                ins.then_inc(dve_c.h, 1)
                (hold if alone else wait)(dve, dve_c.h, dve_c.at(lay, links[0]))

            def norm_low(t):
                dve.wait_ge(rows_high.h, rows_high.at(lay, t + 1))
                b = A[0] if t % 2 == 0 else A[2]
                v.tensor_tensor(uL[:, :, tmc(t)], ps[:, b * 512:b * 512 + 1024].rearrange("p (k n) -> p k n", k=KD),
                                uH[:, :, tmc(t)].bitcast(f32), ALU.subtract).then_inc(rows_low.h, 1)

            def ut_transposed(t):
                if t >= 2:
                    dve.wait_ge(rows_turned.h, rows_turned.at(lay, t - 1))

            dve.wait_ge(g1_in.h, g1_in.at(lay, 16))
            mean_square(lay, 0)
            mean_square(lay, 1)
            for t in range(NT):
                if t >= 2:
                    norm_low(t - 2)
                norm_rows(lay, t, g1, False, ut_transposed)
                if t < 2:
                    mean_square(lay, t + 2)
            norm_low(2)
            norm_low(3)

            def bank_full(q):
                dve.wait_ge(bank_filled.h, bank_filled.at(lay, q + 1))

            def copy_out(q, dst):
                bank_full(q)
                v.tensor_copy(dst, bank(q % 2)).then_inc(bank_freed[q % 2].h, 1)

            def log_decay():
                dve.wait_ge(decay_log.h, decay_log.at(lay, 1))
                link(v.tensor_scalar(lga[:, 1, :], bank(A[0]), ba[:, ds(lay, 1)], 0.0, ALU.add, ALU.min))
                link(v.tensor_tensor(lga[:, 1, :], lga[:, 1, :], lga[:, 0, :], ALU.subtract))
                for n in range(S // CG):
                    c = slice(n * CG, (n + 1) * CG)
                    last = v.tensor_tensor_scan(bT[:, c], lga[:, 1, c], lga[:, 1, c], 0.0, ALU.add, ALU.bypass)
                last.then_inc(decay_sum.h, 1)
                dve.wait_ge(decay_sum.h, decay_sum.at(lay, 1))
                b = bT[:].rearrange("p (n c) -> p n c", c=CG)
                v.tensor_tensor(k2T[:].rearrange("p (n c) -> p n c", c=CG), b[:, :, CG - 1:CG].broadcast_to([P, S // CG, CG]), b,
                                ALU.subtract).then_inc(decay_rest.h, 1)

            def mask_scores(br):
                if br == 0:
                    dve.wait_ge(att_cleared.h, att_cleared.at(lay, 1))
                for h in range(HEADS):
                    hold(dve, att_filled.h, att_filled.at(lay, 4 * br + h + 1))
                    src = bank(A[h]).rearrange("p (t i) -> p t i", t=NT)
                    if br == 0:
                        m = gmask.bitcast(u32).rearrange("p (o i) -> p o i", o=1).broadcast_to([P, NT, P])
                        v.copy_predicated(attT[:, h, :, :], m, src).then_inc(att_masked.h, 1)
                    else:
                        v.tensor_tensor(attT[:, h, :, :], src, decay[:, h:h + 1, :].broadcast_to([P, NT, P]), ALU.mult)\
                            .then_inc(att_masked.h, 1)

            def states(br):
                if br == 0:
                    link(v.memset(prev[:, 0, :], 0.0))
                    dve.wait_ge(decay_exps.h, decay_exps.at(lay, 4))
                dve.wait_ge(kv_filled.h, kv_filled.at(lay, br + 1))
                count = 8 if br == 0 else NT
                for n in range(count - 1):
                    b = A[4] if br == 0 and n % 2 else A[5]
                    ins = v.scalar_tensor_tensor(prev[:, n + 1, :], prev[:, n, :], dec[:, n:n + 1] if br == 0 else cdec,
                                                 ps[:, b * 512 + n * DV:b * 512 + (n + 1) * DV], ALU.mult, ALU.add)
                    if n < count - 2:
                        link(ins)
                    else:
                        ins.then_inc(states_ready.h, 1)

            def head_norm(br):
                for h in range(HEADS):
                    dve.wait_ge(mix_squares.h, mix_squares.at(lay, 4 * br + h + 1))
                    ins = v.tensor_reduce(hss[:, h, :], on[:, :, h, :], AX.X, ALU.add)
                link(ins)
                v.tensor_scalar(hms[:], hss[:].rearrange("p h t -> p (h t)"), 1.0 / DV, EPS, ALU.mult, ALU.add).then_inc(mix_means.h, 1)
                dve.wait_ge(mix_scales.h, mix_scales.at(lay, br + 1))
                for h in range(HEADS):
                    r = hrs[:, h, :].rearrange("p (t o) -> p t o", o=1).broadcast_to([P, NT, DV])
                    v.tensor_tensor(on[:, :, h, :], bank(A[h], 256).rearrange("p (t e) -> p t e", t=NT), r, ALU.mult)\
                        .then_inc(mix_scaled.h, 1)
                dve.wait_ge(mix_scaled.h, mix_scaled.at(lay, 4 * br + 4))
                dve.wait_ge(gains_ready.h, gains_ready.at(lay, br + 1))
                o = on[:].rearrange("p t h e -> p (t h e)")
                v.tensor_tensor(o, o, sr[:].rearrange("p t n -> p (t n)"), ALU.mult).then_inc(mix_normed.h, 1)

            def out_low(br):
                for hh in range(2):
                    dve.wait_ge(mix_high.h, mix_high.at(lay, 2 * br + hh + 1))
                    k = (0, 6)[br] + hh
                    v.tensor_tensor(oL[:, k, :], bank(A[4 + hh]), oH[:, k, :].bitcast(f32), ALU.subtract).then_inc(mix_low.h, 1)

            def rotate():
                dve.wait_ge(tabs_in.h, tabs_in.at(lay, 16))
                dve.wait_ge(rotate_filled.h, rotate_filled.at(lay, 2))
                v.tensor_tensor(bT[:], bank(A[0]), sin, ALU.mult)
                v.tensor_tensor(k2T[:], bank(A[1]), sin, ALU.mult)
                v.tensor_tensor(qT[:], qT[:], cos, ALU.mult)
                link(v.tensor_tensor(kT[:], kT[:], cos, ALU.mult))
                v.tensor_tensor(qT[:], qT[:], bT[:], ALU.add)
                link(v.tensor_tensor(kT[:], kT[:], k2T[:], ALU.add))
                for dst, src, d in ((bT, qT, qdec), (k2T, kT, kdec)):
                    last = v.tensor_tensor(dst[:].rearrange("p (t i) -> p t i", t=NT), src[:].rearrange("p (t i) -> p t i", t=NT),
                                           d.rearrange("p (o i) -> p o i", o=1).broadcast_to([P, NT, P]), ALU.mult)
                last.then_inc(rotary_done.h, 1)

            def step(s):
                if 1 <= s <= NITEMS // 2:
                    n = 2 * s - 1
                    dve.wait_ge(probs_turned.h, probs_turned.at(lay, n + 1))
                    nk = item(n)[4]
                    v.tensor_copy(prT[:, 1, 0:nk * P], bank(A[3], nk * P)).then_inc(probs_copied_d.h, 1)
                if s - 2 in (3, 7, 11, 15):
                    m = (s - 2) // 4
                    dve.wait_ge(attn_high.h, attn_high.at(lay, m + 1))
                    v.tensor_tensor(oL[:, 2 + m, :], bank(A[4]), oH[:, 2 + m, :].bitcast(f32), ALU.subtract).then_inc(attn_low.h, 1)
                if s < NITEMS // 2:
                    pair = (2 * s, 2 * s + 1)
                    for n in pair:
                        win, h, t, k0, nk = item(n)
                        x = n % 2
                        dve.wait_ge(scores_filled.h, scores_filled.at(lay, n + 1))
                        m0 = 0 if win and nk == 2 else nk - 1
                        o = ps[:, A[x] * 512 + m0 * P:A[x] * 512 + nk * P]
                        link(v.tensor_tensor(o, o, wmask[:, 0:256] if m0 < nk - 1 else wmask[:, 128:256], ALU.add))
                        link(v.tensor_reduce(nm[:, x:x + 1], bank(A[x], nk * P), AX.X, ALU.max, negate=True))
                        if win:
                            lim = nsink[:, ds(lay, 1), h:h + 1].rearrange("p a b -> p (a b)")
                            v.tensor_scalar(nb[:, x:x + 1], nm[:, x:x + 1], HD ** -0.5, lim, ALU.mult, ALU.min).then_inc(scores_bias.h, 1)
                        else:
                            v.tensor_scalar(nb[:, x:x + 1], nm[:, x:x + 1], HD ** -0.5, None, ALU.mult).then_inc(scores_bias.h, 1)
                    for n in pair:
                        win, h, t, k0, nk = item(n)
                        x = n % 2
                        dve.wait_ge(probs_raw.h, probs_raw.at(lay, n + 1))
                        d = den
                        if win:
                            link(v.tensor_tensor(den2[:, x:x + 1], den[:, x:x + 1], es[:, x:x + 1], ALU.add))
                            d = den2
                        link(v.reciprocal(rden[:, x:x + 1], d[:, x:x + 1]))
                        v.tensor_scalar(pr[:, x, 0:nk * P], pr[:, x, 0:nk * P], rden[:, x:x + 1], None, ALU.mult).then_inc(probs_ready.h, 1)

            for q in range(NH):
                name = HALVES[q][3]
                if name == "gq":
                    dve.wait_ge(decay_exps.h, decay_exps.at(lay, 4))
                    bank_full(q)
                    v.scalar_tensor_tensor(qT[:], bank(q % 2), DK ** -0.5, qT[:], ALU.mult, ALU.mult).then_inc(bank_freed[q % 2].h, 1)
                elif name == "gk":
                    bank_full(q)
                    v.tensor_tensor(kT[:], bank(q % 2), kT[:], ALU.mult)
                    v.tensor_tensor(k2T[:], bank(q % 2), k2T[:], ALU.mult).then_inc(bank_freed[q % 2].h, 1)
                elif q == 8:
                    bank_full(q)
                    v.tensor_copy(swq[HD:P, 0, :], bank(0)[0:HD])
                    v.tensor_copy(swq[HD:P, 1, :], bank(0)[HD:P]).then_inc(bank_freed[0].h, 1)
                elif q == 10:
                    copy_out(q, svT)
                elif q == 18:
                    dve.wait_ge(h_out.h, h_out.at(lay, 16))
                    copy_out(q, mq[:, 1, :])
                elif q == 20:
                    copy_out(q, mk[:, 1, :])
                elif q == 22:
                    copy_out(q, mv[:, 2:4, :].rearrange("p t n -> p (t n)"))
                if q == 3:
                    log_decay()
                if q in (7, 15):
                    mask_scores(q // 15)
                if q in (8, 16):
                    states(q // 16)
                if q in (10, 18):
                    head_norm(q // 18)
                if q in (12, 20):
                    out_low(q // 20)
                if q == 11:
                    dve.wait_ge(sv_t.h, sv_t.at(lay, 1))
                    v.tensor_copy(swv[:].rearrange("p t n -> p (t n)"), bank(A[5])).then_inc(sv_c.h, 1)
                if q == 13:
                    rotate()
                if q >= STEP0:
                    step(q - STEP0)

            def branch(i, steps):
                for j in range(KD):
                    b = (NH + j) % 2
                    if steps is not None and j + steps < NITEMS // 2 + 2:
                        step(j + steps)
                    dve.wait_ge(bank_freed[b].h, bank_freed[b].at(lay, (NH + j) // 2 + 1) + i * 4)
                    dve.wait_ge(branch_filled.h, branch_filled.at(lay, j + 1) + i * 8)
                    if not (isinstance(i, int) and i == 0):
                        if not (isinstance(i, int) and i == 1 and j < 2):
                            dve.wait_ge(term_added.h, term_added.at(lay, j - 1 - 8) + i * 8)
                        v.tensor_tensor(term[:, j % 2, :], sig[:, j % 2, :], bank(A[5]), ALU.mult).then_inc(term_ready.h, 1)
                    else:
                        v.tensor_tensor(merged[:, j, :], sig[:, j % 2, :], bank(A[5]), ALU.mult).then_inc(term_ready.h, 1)

            branch(0, NH - STEP0)
            branch(1, NH - STEP0 + KD)
            with dve.Fori(2, 4) as i:
                branch(i, None)
            for k in range(KD):
                dve.wait_ge(merged_high.h, merged_high.at(lay, k + 1))
                v.tensor_tensor(uL[:, k, :], merged[:, k, :], uH[:, k, :].bitcast(f32), ALU.subtract).then_inc(merged_low.h, 1)

            dve.wait_ge(h_in.h, h_in.at(lay, 16))
            def residual(c, t):
                q = NH + 32 + 4 * c + t
                bank_full(q)
                o = hs[:, t, c * 512:(c + 1) * 512]
                v.tensor_tensor(o, o, bank(q % 2), ALU.add).then_inc(bank_freed[q % 2].h, 1)

            def ut_stored(t):
                if t >= 2:
                    dve.wait_ge(rows_turned.h, rows_turned.at(lay, NT + t - 1))
                    dve.wait_ge(u2_stored[t % 2].h, u2_stored[t % 2].at(lay, 16))

            for t in range(NT):
                residual(0, t)
            dve.wait_ge(g2_in.h, g2_in.at(lay, 16))
            for t in range(NT):
                residual(1, t)
                mean_square(lay, NT + t)
                norm_rows(lay, NT + t, g2, True, ut_stored)

            dve.wait_ge(rc_in.h, rc_in.at(lay, 48))
            dve.wait_ge(logits_filled.h, logits_filled.at(lay, NT))
            b2 = rb[:, ds(lay, 1), :].broadcast_to([P, NT, NG + NE])
            link(v.tensor_tensor(lg[:], bank(A[5], NT * 36).rearrange("p (t n) -> p t n", t=NT), b2, ALU.add))

            def over(x, n):
                return x.rearrange("p (t o) -> p t o", o=1).broadcast_to([P, NT, n])

            link(v.tensor_reduce(gm[:], lg[:, :, 0:NG], AX.X, ALU.max))
            v.tensor_tensor(gd[:], lg[:, :, 0:NG], over(gm[:], NG), ALU.subtract).then_inc(router_args.h, 1)
            dve.wait_ge(router_args.h, router_args.at(lay, 1))
            link(v.tensor_scalar(geq[:], gd[:], 0.0, None, ALU.is_equal))
            link(v.tensor_tensor(gp[:], geq[:], prio.rearrange("p (o g) -> p o g", o=1).broadcast_to([P, NT, NG]), ALU.mult))
            link(v.tensor_reduce(pm[:], gp[:], AX.X, ALU.max))
            link(v.tensor_tensor(oh[:], gp[:], over(pm[:], NG), ALU.is_equal))
            link(v.tensor_scalar(gidx[:], pm[:], -1.0, float(NG), ALU.mult, ALU.add))
            link(v.tensor_tensor(esel[:], lg[:, :, NG:].rearrange("p t (g e) -> p t g e", g=NG),
                                 oh[:].rearrange("p t (g o) -> p t g o", o=1).broadcast_to([P, NT, NG, EG]), ALU.mult))
            link(v.tensor_reduce(el[:], esel[:].rearrange("p t g e -> p t e g"), AX.X, ALU.add), alone=True)
            for t in range(NT):
                last = v.max(v8[:, t, :], el[:, t, :])
            link(last)
            v.tensor_tensor(dx[:], v8[:, :, 1], v8[:, :, 0], ALU.subtract).then_inc(router_args.h, 1)
            for t in range(NT):
                last = v.max_index(i8[:, t, :], v8[:, t, :], el[:, t, :])
            link(last)
            link(v.tensor_copy(idf[:], i8[:, :, 0:2]))
            link(v.scalar_tensor_tensor(eid[:], over(gidx[:], 2), float(EG), idf[:], ALU.mult, ALU.add))
            sel8 = sel[:].rearrange("p t c e -> p (t c) e")
            link(v.tensor_tensor(sel8, iota[:, 0:NE].rearrange("p (o e) -> p o e", o=1).broadcast_to([P, 2 * NT, NE]),
                                 eid[:].rearrange("p t (c o) -> p (t c) o", o=1).broadcast_to([P, 2 * NT, NE]), ALU.is_equal))
            v.memset(count[:, 0, :], 0.0)
            link(v.tensor_tensor(selM[:], sel[:, :, 0, :], sel[:, :, 1, :], ALU.add))
            link(v.tensor_copy(count[:, 1, :], selM[:, 0, :]))
            for t in range(1, NT):
                ins = v.tensor_tensor(count[:, t + 1, :], count[:, t, :], selM[:, t, :], ALU.add)
                if t < NT - 1:
                    link(ins)
                else:
                    ins.then_inc(choices_ready.h, 1)

            def over8(x, n):
                return x.rearrange("p (c o) -> p c o", o=1).broadcast_to([P, 8, n])

            e8 = eid[:].rearrange("p t c -> p (t c)")
            link(v.tensor_tensor(pair_of[:], sel8[:, :, 0:NP], sel8[:, :, NP:], ALU.add))
            v.tensor_copy(tok_rhs[:, :, 1, :], pair_of[:])
            v.tensor_tensor(tok_rhs[:, :, 0, :], pair_of[:], over8(val, NP), ALU.mult)
            v.tensor_scalar(x64[:], e8, float(NP), float(CAP), ALU.is_ge, ALU.mult)
            dve.wait_ge(ranks_filled.h, ranks_filled.at(lay, 1))
            link(v.tensor_tensor(rk[:], sel[:], bank(A[4], P).rearrange("p (t o e) -> p t o e", t=NT, o=1).broadcast_to([P, NT, 2, NE]),
                                 ALU.mult))
            v.tensor_reduce(most[:], bank(A[4], P + NE)[:, P:P + NE], AX.X, ALU.max)
            link(v.tensor_reduce(rank[:].rearrange("p (t c) -> p t c", t=NT), rk[:], AX.X, ALU.add))

            def choice_slots(chain):
                v.tensor_scalar(out_of[:], rank[:], float(CAP), 1024.0, ALU.is_ge, ALU.mult)
                v.tensor_scalar(below[:], rank[:], 0.0, 1024.0, ALU.is_lt, ALU.mult)
                chain(v.tensor_tensor(slot[:], rank[:], x64[:], ALU.add))
                chain(v.tensor_tensor(slot[:], slot[:], out_of[:], ALU.add))
                chain(v.scalar_tensor_tensor(slot[:], below[:], 2.0, slot[:], ALU.mult, ALU.add))
                return v.tensor_tensor(slot_of[:], iota[:, 0:P].rearrange("p (o i) -> p o i", o=1).broadcast_to([P, 8, P]),
                                       over8(slot[:], P), ALU.is_equal)

            def list_entries(chain):
                chain(v.tensor_scalar(empty[:], bank(A[4])[:, 256 + NP:256 + 2 * NP], -float(SENT), float(SENT), ALU.mult, ALU.add))
                chain(v.tensor_tensor(lists[:], bank(A[4])[:, 256:256 + NP], empty[:], ALU.add))
                chain(v.tensor_copy(toks[:], lists[:]))
                chain(v.tensor_scalar(toks[:], toks[:], 1, None, ALU.arith_shift_right))
                return v.tensor_copy(tokf[:], toks[:])

            choice_slots(link).then_inc(slots_ready.h, 1)
            dve.wait_ge(list_filled.h, list_filled.at(lay, 1))
            list_entries(link).then_inc(lists_ready.h, 1)
            dve.wait_ge(router_exps.h, router_exps.at(lay, 1))
            link(v.tensor_reduce(gs[:], ge[:], AX.X, ALU.add))
            link(v.reciprocal(gw[:], gs[:]))
            dve.wait_ge(router_exps.h, router_exps.at(lay, 2))
            link(v.tensor_scalar(ex1[:], ex[:], 1.0, None, ALU.add))
            link(v.reciprocal(rex[:], ex1[:]))
            link(v.tensor_tensor(wts[:, :, 0], rex[:], gw[:], ALU.mult))
            link(v.tensor_tensor(wts[:, :, 1], wts[:, :, 0], ex[:], ALU.mult))
            v.tensor_tensor(w_rhs[:], pair_of[:], over8(wts[:].rearrange("p t c -> p (t c)"), NP), ALU.mult).then_inc(list_weights_ready.h, 1)
            for x in range(1, NW):
                last = v.tensor_scalar(over_n[:, x - 1:x], most[:], float(x * CAP), None, ALU.is_gt)
            link(last)
            link(v.tensor_reduce(over_n[:, NW - 1:NW], over_n[:, 0:NW - 1], AX.X, ALU.add))
            link(v.tensor_tensor(extra[:, ds(lay + 1, 1)], over_n[:, NW - 1:NW], extra[:, ds(lay, 1)], ALU.add))
            v.tensor_copy(windows[:, 0, ds(lay + 1, 1)], extra[:, ds(lay + 1, 1)])
            v.tensor_copy(windows[:, 1, ds(lay, 1)], over_n[:, NW - 1:NW]).then_inc(win_n.h, 1)

            def slot_weights():
                return v.tensor_copy(slot_w[:], bank(A[4])[:, 384:384 + NP])

            def rows_copy(i, y):
                dve.wait_ge(x_turned.h, x_turned.at(lay, y + 1) + i * 2)
                v.tensor_copy(xT[y][:, 512:1024], bank(A[3])).then_inc(x_copied_d.h, 1)

            def gated(col):
                return v.scalar_tensor_tensor(hid[:], silu[:], slot_w[:, col], bank(0)[:, FH:2 * FH], ALU.mult, ALU.mult)

            def out_low_rows(high, low):
                return v.tensor_tensor(low[:], ps[:, A[0] * 512:A[0] * 512 + 1024], high[:].bitcast(f32), ALU.subtract)

            def slot_tokens(to, col):
                return v.tensor_scalar(to[:], iota, tokf[:, col], None, ALU.is_equal)

            def add_rows(products, value, added):
                for x in range(8):
                    t, c = x // 2, x % 2
                    dve.wait_ge(products, value + x)
                    o = hs[:, t, c * 512:(c + 1) * 512]
                    v.tensor_tensor(o, o, bank((1, A[5])[x % 2]), ALU.add).then_inc(added, 1)

            def add_two(i):
                if not isinstance(i, int) or i:
                    dve.wait_ge(sum_added.h, sum_added.at(lay, 0) + i * 8)
                add_rows(sum_filled.h, sum_filled.at(lay, 1) + i * 8, sum_added.h)

            def pair(i, y, more, behind=True):
                p = i * 2 + y
                col = slice(p, p + 1) if isinstance(p, int) else ds(p, 1)
                dve.wait_ge(silu_ready.h, silu_ready.at(lay, y + 1) + i * 2)
                gated(col).then_inc(hidden_ready.h, 1)
                if more:
                    rows_copy(i + y, 1 - y)
                if behind:
                    add_two(i - 1)
                slot_tokens(tok_of[y], col).then_inc(tokens_ready.h, 1)
                dve.wait_ge(out_high.h, out_high.at(lay, y + 1) + i * 2)
                out_low_rows(yH[y], yL[y]).then_inc(out_low_ready.h, 1)

            dve.wait_ge(lists_ready.h, lists_ready.at(lay, 1))
            rows_copy(0, 0)
            dve.wait_ge(list_weights_filled.h, list_weights_filled.at(lay, 1))
            link(slot_weights())
            pair(0, 0, True, behind=False)
            pair(0, 1, True, False)
            with dve.Fori(1, NP // 2 - 1) as i:
                pair(i, 0, True)
                pair(i, 1, True, behind=False)
            pair(NP // 2 - 1, 0, True)
            pair(NP // 2 - 1, 1, False, behind=False)

            def window_lists(n):
                count_ = [0]

                def chain(ins):
                    count_[0] += 1
                    ins.then_inc(win_link, 1)
                    hold(dve, win_link, n * WIN_LINKS + count_[0])

                chain(v.tensor_scalar(rank[:], rank[:], -float(CAP), None, ALU.add))
                choice_slots(chain).then_inc(win_slots, 1)
                hold(dve, win_list_filled, n + 1)
                chain(slot_weights())
                list_entries(chain).then_inc(win_lists, 1)
                hold(dve, win_lists, n + 1)
                assert count_[0] == WIN_LINKS, count_

            def window_item(n, p):
                hold(dve, win_silu, n + 1)
                gated(ds(p, 1)).then_inc(win_hidden, 1)
                slot_tokens(tok_w, ds(p, 1)).then_inc(win_tokens, 1)
                hold(dve, win_out_h, n + 1)
                out_low_rows(yHw, yLw).then_inc(win_out_l, 1)
                hold(dve, sum_added.h, sum_added.at(lay, SUMS - 8))
                hold(dve, win_added, n * 8 + 2)
                add_rows(win_sum, n * 8 + 1, win_added)

            before, own = window_range(dve, lay)
            later_windows(dve, before, own, window_lists, window_item)

            hold(dve, win_added, (before + own) * (NP * 8) + 2)
            add_two(NP // 2 - 1)
            assert links[0] == DVE_LINKS, links

        dve.wait_ge(g1_in.h, g1_in.at(L, 16))
        for t in range(NT):
            mean_square(L, t)
            dve.wait_ge(scale_ready.h, scale_ready.at(L, t + 1))
            if t >= 2:
                dve.wait_ge(s_out[t % 2].h, 16)
            v.scalar_tensor_tensor(ut[:, t % 2, :], hs[:, t, :], rstd[:, t:t + 1], g1[:], ALU.mult, ALU.mult).then_inc(fin.h, 1)

    return ctx


def tables():
    f = np.float32
    p = np.arange(P)
    ident = np.eye(P, dtype=f)
    wmask = np.where(np.concatenate([p[None, :] > p[:, None], p[None, :] <= p[:, None]], 1), 0.0, NEG).astype(f)
    gmask = ((p[:, None] <= p[None, :]) & (p[:, None] // CG == p[None, :] // CG)).astype(f)
    log_gamma = np.log1p(-np.exp2(-5.0 - np.arange(HEADS, dtype=np.float64)))
    head = p // DK
    cdec = np.exp(P * log_gamma)[head][:, None]
    small = np.zeros((P, 544), f)
    small[:, 0:128], small[:, 128:384], small[:, 384:512] = ident, wmask, gmask
    small[:, 512:513] = cdec
    small[:, 516:520] = np.arange(NG, 0, -1)
    small[:, 520:536] = -0.5
    half = DK // 2
    d = p % DK
    inv = (f(10000.0) ** (-np.arange(half, dtype=f) * f(2.0) / f(DK))).astype(f)
    ang = (np.arange(S, dtype=f)[None, :] * inv[d % half][:, None]).astype(f)
    rot = np.zeros((P, P), f)
    for m in range(P):
        if d[m] < half:
            rot[m + half, m] = -1.0
        else:
            rot[m - half, m] = 1.0
    idx = np.arange(P, dtype=np.float64)
    rel = idx[None, :] - idx[:, None]
    scores_filled = DK ** -0.5
    dm = np.where(rel[:, None, :] >= 0, np.exp(np.maximum(rel, 0)[:, None, :] * log_gamma[None, :, None]), 0.0) * scores_filled
    qd = np.exp((idx + 1)[None, :] * log_gamma[head][:, None])
    kd = np.exp((P - 1 - idx)[None, :] * log_gamma[head][:, None]) * scores_filled
    tabs = np.concatenate([np.cos(ang.astype(np.float64)), np.sin(ang.astype(np.float64)), dm.reshape(P, -1), qd, kd, rot], 1).astype(f)
    router = np.concatenate([(p[:, None] < p[None, :]), np.ones((P, P)), np.tile(np.arange(S), (P, 1)),
                             2 * (p[:, None] + np.arange(8)[None, :] // 2 * P) + np.arange(8)[None, :] % 2], 1).astype(f)
    return {"c_small": small, "c_tabs": tabs, "c_router": router}


def kernel(**inputs):
    import concourse.bacc as bacc
    from concourse.bass_utils import run_bass_kernel_spmd

    nc = bacc.Bacc("TRN2", target_bir_lowering=False, num_devices=1)
    host = {k: np.ascontiguousarray(x) for k, x in inputs.items()}
    host["c_next_gain"] = np.concatenate([host["ln1_g"][1:], host.pop("final_g")[None]], 0)
    host.update(tables())
    arrays, a = {}, {}
    for k, x in host.items():
        arrays[f"in_{k}"] = x
        a[k] = nc.dram_tensor(f"in_{k}", x.shape, mybir.dt.from_np(x.dtype), kind="ExternalInput").ap()
    out = nc.dram_tensor("out", (1, S, D), mybir.dt.float32, kind="ExternalOutput").ap()
    trunk(nc, a, out).close()
    r = run_bass_kernel_spmd(nc, [arrays], core_ids=[0])
    return r.results[0]["out"]
```
